# Optimizing a Trainium2 kernel written in Bass

```python
import jax
import jax.numpy as jnp
from jax import lax
import numpy as np
import math

D_MODEL = 1024
BATCH = 1
SEQ = 256
DEPTH = 1

D_MIX = D_MODEL
RWKV_WIDTH = D_MIX // 2
RWKV_HEAD_DIM = 64
RWKV_HEADS = RWKV_WIDTH // RWKV_HEAD_DIM
DECAY_LORA = 64
ICLR_LORA = 64
GATE_LORA = 128
GLA_V_WIDTH = D_MIX - RWKV_WIDTH
GLA_HEADS = 4
GLA_DV = GLA_V_WIDTH // GLA_HEADS
GLA_DK = GLA_DV // 2
GLA_K_WIDTH = GLA_HEADS * GLA_DK
GLA_GATE_LORA = 16
GLA_TAU = 16.0
GLA_CHUNK = 16
N_GROUPS = 4
EXPERTS_PER_GROUP = 8
N_EXPERTS = N_GROUPS * EXPERTS_PER_GROUP
TOP_K = 2
D_EXPERT = 512
MOE_BLOCK = 128
RMS_EPS = 1e-6
RWKV_GN_EPS = 64e-5

RWKV_SPLITS = (RWKV_WIDTH, RWKV_WIDTH, RWKV_WIDTH, DECAY_LORA, DECAY_LORA, ICLR_LORA, ICLR_LORA, GATE_LORA)
GLA_SPLITS = (GLA_K_WIDTH, GLA_K_WIDTH, GLA_V_WIDTH, GLA_GATE_LORA, GLA_GATE_LORA, GLA_V_WIDTH)
RWKV_COLS = sum(RWKV_SPLITS)
D_IN_PROJ = RWKV_COLS + sum(GLA_SPLITS)


def _split(p, sizes):
    return jnp.split(p, np.cumsum(sizes)[:-1].tolist(), axis=-1)

def rmsnorm(x, w):
    xf = x.astype(jnp.float32)
    y = xf * lax.rsqrt(jnp.mean(xf * xf, axis=-1, keepdims=True) + RMS_EPS)
    return (y * w.astype(jnp.float32)).astype(x.dtype)

def centred_shift(p):
    prev = jnp.pad(p[:, :-1], ((0, 0), (1, 0), (0, 0)))
    nxt = jnp.pad(p[:, 1:], ((0, 0), (0, 1), (0, 0)))
    return 0.5 * (prev + nxt)

def rwkv7_bidir_scan(r, w, k, v, kk, b):
    def to_dir(z):
        z = jnp.stack([z[0], jnp.flip(z[1], axis=1)])
        return jnp.moveaxis(z, 2, 0)

    def both(z):
        return to_dir(jnp.stack([z, z]))

    xs = (both(r), to_dir(w), to_dir(k), both(v), both(kk), to_dir(b))
    bsz, _, h, n = r.shape
    s0 = jnp.zeros((2, bsz, h, n, n), jnp.float32)

    def step(s, inp):
        r_t, w_t, k_t, v_t, kk_t, b_t = inp
        sa = jnp.einsum('dbhvk,dbhk->dbhv', s, -kk_t)
        s = s * w_t[..., None, :] + sa[..., None] * b_t[..., None, :] + v_t[..., None] * k_t[..., None, :]
        return s, jnp.einsum('dbhvk,dbhk->dbhv', s, r_t)

    _, ys = lax.scan(step, s0, xs)
    ys = jnp.moveaxis(ys, 0, 2)
    return ys[0] + jnp.flip(ys[1], axis=1)

def rwkv7_mixer(p, mu, w0_f, w2_f, w0_b, w2_b, a0_f, a2_f, a0_b, a2_b, g2, k_k, k_a, r_k, ln_w, ln_b):
    p = p.astype(jnp.float32)
    p = p + mu * (centred_shift(p) - p)
    r, k, v, wl_f, wl_b, al_f, al_b, gl = _split(p, RWKV_SPLITS)

    def decay(w0, wl, w2):
        logw = -jax.nn.softplus(-(w0 + jnp.tanh(wl) @ w2)) - 0.5
        return jnp.exp(-jnp.exp(logw))

    def heads(z):
        return z.reshape(z.shape[:-1] + (RWKV_HEADS, RWKV_HEAD_DIM))

    w = jnp.stack([decay(w0_f, wl_f, w2_f), decay(w0_b, wl_b, w2_b)])
    a = jax.nn.sigmoid(jnp.stack([a0_f + al_f @ a2_f, a0_b + al_b @ a2_b]))
    g = jax.nn.sigmoid(gl) @ g2
    kk = heads(k * k_k)
    kk = kk / jnp.maximum(jnp.sqrt(jnp.sum(kk * kk, axis=-1, keepdims=True)), 1e-12)
    k_dir = k * (1.0 + (a - 1.0) * k_a)
    b = kk * heads(a)
    rh, vh = heads(r), heads(v)
    y = rwkv7_bidir_scan(rh, heads(w), heads(k_dir), vh, kk, b)
    mean = jnp.mean(y, axis=-1, keepdims=True)
    var = jnp.var(y, axis=-1, keepdims=True)
    y = (y - mean) * lax.rsqrt(var + RWKV_GN_EPS)
    y = y.reshape(y.shape[:-2] + (RWKV_WIDTH,)) * ln_w + ln_b
    bonus = jnp.sum(rh * heads(k_dir[0] + k_dir[1]) * r_k, axis=-1, keepdims=True) * vh
    return (y + bonus.reshape(y.shape)) * g

def gla_chunked(q, k, v, g):
    bsz, h, t, dk = q.shape
    dv = v.shape[-1]
    c = GLA_CHUNK
    n = t // c
    q, k, g = (z.reshape(bsz, h, n, c, dk) for z in (q, k, g))
    v = v.reshape(bsz, h, n, c, dv)
    bc = jnp.cumsum(g, axis=3)
    causal = jnp.tril(jnp.ones((c, c), dtype=bool))
    diff = bc[..., :, None, :] - bc[..., None, :, :]
    dec = jnp.exp(jnp.where(causal[:, :, None], diff, -jnp.inf))
    att = jnp.einsum('bhnid,bhnjd,bhnijd->bhnij', q, k, dec)
    o = jnp.einsum('bhnij,bhnjv->bhniv', att, v)
    b_last = bc[..., -1, :]
    u = jnp.einsum('bhncd,bhncv->nbhdv', k * jnp.exp(b_last[..., None, :] - bc), v)

    def step(s, inp):
        u_n, d_n = inp
        return s * d_n[..., None] + u_n, s

    s0 = jnp.zeros((bsz, h, dk, dv), jnp.float32)
    _, s_in = lax.scan(step, s0, (u, jnp.moveaxis(jnp.exp(b_last), 2, 0)))
    o = o + jnp.einsum('bhncd,nbhdv->bhncv', q * jnp.exp(bc), s_in)
    return o.reshape(bsz, h, t, dv)

def gla_mixer(p, gw2_f, gb_f, gw2_b, gb_b, norm_w):
    p = p.astype(jnp.float32)
    bsz, t, _ = p.shape
    q, k, v, gl_f, gl_b, og = _split(p, GLA_SPLITS)

    def heads(z, d):
        return jnp.moveaxis(z.reshape(z.shape[:-1] + (GLA_HEADS, d)), 2, 1)

    q = heads(q, GLA_DK) * (GLA_DK ** -0.5)
    k = heads(k, GLA_DK)
    v = heads(v, GLA_DV)
    g_f = heads(jax.nn.log_sigmoid(gl_f @ gw2_f + gb_f) / GLA_TAU, GLA_DK)
    g_b = heads(jax.nn.log_sigmoid(gl_b @ gw2_b + gb_b) / GLA_TAU, GLA_DK)

    def flip(z):
        return jnp.flip(z, axis=2)

    o = gla_chunked(q, k, v, g_f) + flip(gla_chunked(flip(q), flip(k), flip(v), flip(g_b)))
    o = o * lax.rsqrt(jnp.mean(o * o, axis=-1, keepdims=True) + RMS_EPS)
    o = jnp.moveaxis(o, 1, 2).reshape(bsz, t, GLA_V_WIDTH)
    return o * norm_w * jax.nn.silu(og)

def hier_moe(h, w_coarse, b_coarse, w_fine, b_fine, w_gate, w_up, w_down):
    bsz, t, d = h.shape
    n_tok = bsz * t
    hf = h.reshape(n_tok, d)
    tok_idx = jnp.arange(n_tok)
    coarse = (hf @ w_coarse + b_coarse).astype(jnp.float32)
    pc = jax.nn.softmax(coarse, axis=-1)
    gsel = jnp.argmax(coarse, axis=-1)
    pg = pc[tok_idx, gsel]
    fine = (hf @ w_fine + b_fine).astype(jnp.float32).reshape(n_tok, N_GROUPS, EXPERTS_PER_GROUP)
    pf = jax.nn.softmax(fine[tok_idx, gsel], axis=-1)
    top_p, top_e = lax.top_k(pf, TOP_K)
    comb = pg[:, None] * top_p / jnp.sum(top_p, axis=-1, keepdims=True)
    eid = (gsel[:, None] * EXPERTS_PER_GROUP + top_e).reshape(-1).astype(jnp.int32)
    n_asg = n_tok * TOP_K
    tok = jnp.repeat(tok_idx, TOP_K).astype(jnp.int32)
    wts = comb.reshape(-1)
    order = jnp.argsort(eid, stable=True)
    se, st, sw = eid[order], tok[order], wts[order]
    counts = jnp.bincount(eid, length=N_EXPERTS).astype(jnp.int32)
    starts = jnp.cumsum(counts) - counts
    padded = ((counts + MOE_BLOCK - 1) // MOE_BLOCK) * MOE_BLOCK
    pends = jnp.cumsum(padded)
    pstarts = pends - padded
    dest = pstarts[se] + jnp.arange(n_asg, dtype=jnp.int32) - starts[se]
    n_blocks = -(-n_asg // MOE_BLOCK) + N_EXPERTS
    n_rows = n_blocks * MOE_BLOCK
    row_tok = jnp.zeros((n_rows,), jnp.int32).at[dest].set(st)
    row_w = jnp.zeros((n_rows,), jnp.float32).at[dest].set(sw)
    block_e = jnp.minimum(jnp.searchsorted(pends, jnp.arange(n_blocks, dtype=jnp.int32) * MOE_BLOCK, side='right'), N_EXPERTS - 1)
    xs = hf[row_tok].reshape(n_blocks, MOE_BLOCK, d)

    def expert_block(args):
        xb, e = args
        return (jax.nn.silu(xb @ w_gate[e]) * (xb @ w_up[e])) @ w_down[e]

    ys = lax.map(expert_block, (xs, block_e)).reshape(n_rows, d)
    out = jax.ops.segment_sum(ys * row_w[:, None].astype(ys.dtype), row_tok, num_segments=n_tok)
    return out.reshape(bsz, t, d)

def first_inputs(seed: int = 0) -> dict:
    key = jax.random.key(seed)
    ks = iter(jax.random.split(key, 40))

    def nrm(shape, scale):
        return jax.random.normal(next(ks), shape, jnp.float32) * scale

    def unif(shape, lo, hi):
        return jax.random.uniform(next(ks), shape, jnp.float32, lo, hi)

    L, D = DEPTH, D_MODEL
    return {
        'x': nrm((BATCH, SEQ, D), 1.0),
        'ln1_w': 1.0 + nrm((L, D), 0.05),
        'w_in': nrm((L, D, D_IN_PROJ), D ** -0.5),
        'rw_mu': unif((L, RWKV_COLS), 0.0, 1.0),
        'rw_w0_f': unif((L, RWKV_WIDTH), -6.0, -1.0),
        'rw_w2_f': nrm((L, DECAY_LORA, RWKV_WIDTH), 0.1),
        'rw_w0_b': unif((L, RWKV_WIDTH), -6.0, -1.0),
        'rw_w2_b': nrm((L, DECAY_LORA, RWKV_WIDTH), 0.1),
        'rw_a0_f': nrm((L, RWKV_WIDTH), 0.1),
        'rw_a2_f': nrm((L, ICLR_LORA, RWKV_WIDTH), 0.5 * ICLR_LORA ** -0.5),
        'rw_a0_b': nrm((L, RWKV_WIDTH), 0.1),
        'rw_a2_b': nrm((L, ICLR_LORA, RWKV_WIDTH), 0.5 * ICLR_LORA ** -0.5),
        'rw_g2': nrm((L, GATE_LORA, RWKV_WIDTH), GATE_LORA ** -0.5),
        'rw_k_k': 0.85 + nrm((L, RWKV_WIDTH), 0.05),
        'rw_k_a': 1.0 + nrm((L, RWKV_WIDTH), 0.05),
        'rw_r_k': nrm((L, RWKV_HEADS, RWKV_HEAD_DIM), 0.1),
        'rw_ln_w': 1.0 + nrm((L, RWKV_WIDTH), 0.05),
        'rw_ln_b': nrm((L, RWKV_WIDTH), 0.01),
        'gla_gw2_f': nrm((L, GLA_GATE_LORA, GLA_K_WIDTH), GLA_GATE_LORA ** -0.5),
        'gla_gb_f': 2.0 + nrm((L, GLA_K_WIDTH), 0.5),
        'gla_gw2_b': nrm((L, GLA_GATE_LORA, GLA_K_WIDTH), GLA_GATE_LORA ** -0.5),
        'gla_gb_b': 2.0 + nrm((L, GLA_K_WIDTH), 0.5),
        'gla_norm_w': 1.0 + nrm((L, GLA_V_WIDTH), 0.05),
        'w_out': nrm((L, D_MIX, D), D_MIX ** -0.5),
        'ln2_w': 1.0 + nrm((L, D), 0.05),
        'moe_w_coarse': nrm((L, D, N_GROUPS), D ** -0.5),
        'moe_b_coarse': nrm((L, N_GROUPS), 0.01),
        'moe_w_fine': nrm((L, D, N_EXPERTS), D ** -0.5),
        'moe_b_fine': nrm((L, N_EXPERTS), 0.01),
        'moe_w_gate': nrm((L, N_EXPERTS, D, D_EXPERT), D ** -0.5),
        'moe_w_up': nrm((L, N_EXPERTS, D, D_EXPERT), D ** -0.5),
        'moe_w_down': nrm((L, N_EXPERTS, D_EXPERT, D), D_EXPERT ** -0.5),
        'ln_f_w': 1.0 + nrm((D,), 0.05),
    }

def first_block(x, ln1_w, w_in, rw_mu, rw_w0_f, rw_w2_f, rw_w0_b, rw_w2_b, rw_a0_f, rw_a2_f, rw_a0_b, rw_a2_b, rw_g2, rw_k_k, rw_k_a, rw_r_k, rw_ln_w, rw_ln_b, gla_gw2_f, gla_gb_f, gla_gw2_b, gla_gb_b, gla_norm_w, w_out, ln2_w, moe_w_coarse, moe_b_coarse, moe_w_fine, moe_b_fine, moe_w_gate, moe_w_up, moe_w_down, ln_f_w):
    for l in range(DEPTH):
        h = rmsnorm(x, ln1_w[l])
        p = h @ w_in[l]
        y_rw = rwkv7_mixer(p[..., :RWKV_COLS], rw_mu[l], rw_w0_f[l], rw_w2_f[l], rw_w0_b[l], rw_w2_b[l],
                           rw_a0_f[l], rw_a2_f[l], rw_a0_b[l], rw_a2_b[l], rw_g2[l], rw_k_k[l], rw_k_a[l],
                           rw_r_k[l], rw_ln_w[l], rw_ln_b[l])
        y_gla = gla_mixer(p[..., RWKV_COLS:], gla_gw2_f[l], gla_gb_f[l], gla_gw2_b[l], gla_gb_b[l], gla_norm_w[l])
        mix = jnp.concatenate([y_rw, y_gla], axis=-1).astype(x.dtype)
        x = x + mix @ w_out[l]
        x = x + hier_moe(rmsnorm(x, ln2_w[l]), moe_w_coarse[l], moe_b_coarse[l], moe_w_fine[l], moe_b_fine[l],
                         moe_w_gate[l], moe_w_up[l], moe_w_down[l])
    return rmsnorm(x, ln_f_w)


DEPTH_2 = 2

N_EVEN = (DEPTH_2 + 1) // 2
N_ODD = DEPTH_2 // 2
Q_BLOCK = 128
EPS = 1e-6
SB_HEADS = 8
SB_HEAD_DIM = 64
SB_WIDTH = SB_HEADS * SB_HEAD_DIM
MLA_HEADS = 8
MLA_Q_RANK = 256
MLA_KV_RANK = 128
MLA_NOPE_DIM = 64
MLA_ROPE_DIM = 32
MLA_QK_DIM = MLA_NOPE_DIM + MLA_ROPE_DIM
MLA_V_DIM = 64
MLA_WIDTH = MLA_HEADS * MLA_V_DIM
ROPE_THETA = 10000.0
OFF_SB_K = SB_WIDTH
OFF_SB_V = 2 * SB_WIDTH
OFF_CQ = 3 * SB_WIDTH
OFF_CKV = OFF_CQ + MLA_Q_RANK
OFF_KR = OFF_CKV + MLA_KV_RANK
IN_COLS = OFF_KR + MLA_ROPE_DIM
MIX_WIDTH = SB_WIDTH + MLA_WIDTH
SSM_WIDTH = D_MODEL // 2
SSM_GROUP = 16
SSM_GROUPS = SSM_WIDTH // SSM_GROUP
SSM_STATE = 64
DT_MIN = 1e-3
DT_MAX = 1e-1
EIG_RE_MAX = -1e-4
D_FF = 7 * D_MODEL // 2
N_EXPERTS_2 = 8
EXPERT_BLOCK = 128


def _rms_norm(x, gain):
    xf = x.astype(jnp.float32)
    y = xf * lax.rsqrt(jnp.mean(xf * xf, axis=-1, keepdims=True) + EPS)
    return (y * gain.astype(jnp.float32)).astype(x.dtype)

def _to_heads(t, heads):
    b, s, _ = t.shape
    return t.reshape(b, s, heads, -1).transpose(0, 2, 1, 3).astype(jnp.float32)

def _from_heads(t):
    b, h, s, d = t.shape
    return t.transpose(0, 2, 1, 3).reshape(b, s, h * d)

def _sweep_query_blocks(block_fn, q, k, v):
    b, h, s, dq = q.shape
    nb = s // Q_BLOCK
    qb = q.reshape(b, h, nb, Q_BLOCK, dq).transpose(2, 0, 1, 3, 4)
    starts = jnp.arange(nb, dtype=jnp.int32) * Q_BLOCK
    out = lax.map(lambda args: block_fn(args[0], args[1], k, v), (qb, starts))
    return out.transpose(1, 2, 0, 3, 4).reshape(b, h, s, v.shape[-1])

def _stick_breaking_block(q_blk, t0, k, v):
    s_len = k.shape[2]
    t_idx = t0 + jnp.arange(Q_BLOCK, dtype=jnp.int32)
    s_idx = jnp.arange(s_len, dtype=jnp.int32)
    earlier = s_idx[None, :] < t_idx[:, None]
    z = jnp.einsum('bhqd,bhkd->bhqk', q_blk, k) * (q_blk.shape[-1] ** -0.5)
    log_fail = jnp.where(earlier, jax.nn.log_sigmoid(-z), 0.0)
    log_stick = lax.cumsum(log_fail, axis=3, reverse=True) - log_fail
    w = jnp.where(earlier, jnp.exp(jax.nn.log_sigmoid(z) + log_stick), 0.0)
    return jnp.einsum('bhqk,bhkd->bhqd', w, v)

def _causal_softmax_block(q_blk, t0, k, v):
    s_len = k.shape[2]
    t_idx = t0 + jnp.arange(Q_BLOCK, dtype=jnp.int32)
    s_idx = jnp.arange(s_len, dtype=jnp.int32)
    visible = s_idx[None, :] <= t_idx[:, None]
    z = jnp.einsum('bhqd,bhkd->bhqk', q_blk, k) * (q_blk.shape[-1] ** -0.5)
    p = jax.nn.softmax(jnp.where(visible, z, -jnp.inf), axis=-1)
    return jnp.einsum('bhqk,bhkd->bhqd', p, v)

def _rope_tables(s_len):
    inv_freq = ROPE_THETA ** (-jnp.arange(0, MLA_ROPE_DIM, 2, dtype=jnp.float32) / MLA_ROPE_DIM)
    ang = jnp.arange(s_len, dtype=jnp.float32)[:, None] * inv_freq[None, :]
    return jnp.cos(ang), jnp.sin(ang)

def _rope_tail(t, cos, sin):
    half = MLA_ROPE_DIM // 2
    nope = t[..., :MLA_NOPE_DIM]
    r1 = t[..., MLA_NOPE_DIM:MLA_NOPE_DIM + half]
    r2 = t[..., MLA_NOPE_DIM + half:]
    c = cos[None, :, None, :]
    s = sin[None, :, None, :]
    return jnp.concatenate([nope, r1 * c - r2 * s, r2 * c + r1 * s], axis=-1)

def _attention_layer(x, norm_g, w_in, q_lat_g, w_q_up, kv_lat_g, w_kv_up, q_g, k_g, w_out):
    b, s, _ = x.shape
    h = _rms_norm(x, norm_g) @ w_in
    o_sb = _sweep_query_blocks(
        _stick_breaking_block,
        _to_heads(h[..., :OFF_SB_K], SB_HEADS),
        _to_heads(h[..., OFF_SB_K:OFF_SB_V], SB_HEADS),
        _to_heads(h[..., OFF_SB_V:OFF_CQ], SB_HEADS))
    c_q = _rms_norm(h[..., OFF_CQ:OFF_CKV], q_lat_g)
    c_kv = _rms_norm(h[..., OFF_CKV:OFF_KR], kv_lat_g)
    k_rope = h[..., OFF_KR:]
    q = (c_q @ w_q_up).reshape(b, s, MLA_HEADS, MLA_QK_DIM)
    kv = (c_kv @ w_kv_up).reshape(b, s, MLA_HEADS, MLA_NOPE_DIM + MLA_V_DIM)
    k = jnp.concatenate(
        [kv[..., :MLA_NOPE_DIM],
         jnp.broadcast_to(k_rope[:, :, None, :], (b, s, MLA_HEADS, MLA_ROPE_DIM))], axis=-1)
    v = kv[..., MLA_NOPE_DIM:].astype(jnp.float32)
    q = _rms_norm(q, q_g).astype(jnp.float32)
    k = _rms_norm(k, k_g).astype(jnp.float32)
    cos, sin = _rope_tables(s)
    q = _rope_tail(q, cos, sin)
    k = _rope_tail(k, cos, sin)
    o_mla = _sweep_query_blocks(
        _causal_softmax_block,
        q.transpose(0, 2, 1, 3), k.transpose(0, 2, 1, 3), v.transpose(0, 2, 1, 3))
    merged = jnp.concatenate([_from_heads(o_sb), _from_heads(o_mla)], axis=-1)
    return x + merged.astype(x.dtype) @ w_out

def _dense_swiglu_layer(x, norm_g, w_gate, w_up, w_down):
    xn = _rms_norm(x, norm_g)
    return x + (jax.nn.silu(xn @ w_gate) * (xn @ w_up)) @ w_down

def _s5_discretize(a_re, a_im, log_dt, b_re, b_im):
    a_re = jnp.minimum(a_re.astype(jnp.float32), EIG_RE_MAX)
    a_im = a_im.astype(jnp.float32)
    dt = jnp.exp(log_dt.astype(jnp.float32))[:, None]
    mag = jnp.exp(a_re * dt)
    lam_re = mag * jnp.cos(a_im * dt)
    lam_im = mag * jnp.sin(a_im * dt)
    den = a_re * a_re + a_im * a_im
    num_re = lam_re - 1.0
    coef_re = ((num_re * a_re + lam_im * a_im) / den)[..., None]
    coef_im = ((lam_im * a_re - num_re * a_im) / den)[..., None]
    b_re = b_re.astype(jnp.float32)
    b_im = b_im.astype(jnp.float32)
    bb_re = coef_re * b_re - coef_im * b_im
    bb_im = coef_re * b_im + coef_im * b_re
    return lam_re, lam_im, bb_re, bb_im

def _complex_affine_combine(first, second):
    a1r, a1i, b1r, b1i = first
    a2r, a2i, b2r, b2i = second
    return (a2r * a1r - a2i * a1i,
            a2r * a1i + a2i * a1r,
            a2r * b1r - a2i * b1i + b2r,
            a2r * b1i + a2i * b1r + b2i)

def _s5_layer(x, norm_g, w_in, a_re, a_im, log_dt, b_re, b_im, c_re, c_im, d_skip, w_glu):
    b, s, _ = x.shape
    u = (_rms_norm(x, norm_g) @ w_in).astype(jnp.float32)
    lam_re, lam_im, bb_re, bb_im = _s5_discretize(a_re, a_im, log_dt, b_re, b_im)
    ug = u.reshape(b, s, SSM_GROUPS, SSM_GROUP)
    bu_re = jnp.einsum('bsgc,gnc->bsgn', ug, bb_re)
    bu_im = jnp.einsum('bsgc,gnc->bsgn', ug, bb_im)
    full = bu_re.shape
    _, _, h_re, h_im = lax.associative_scan(
        _complex_affine_combine,
        (jnp.broadcast_to(lam_re, full), jnp.broadcast_to(lam_im, full), bu_re, bu_im),
        axis=1)
    y = (jnp.einsum('bsgn,gcn->bsgc', h_re, c_re.astype(jnp.float32))
         - jnp.einsum('bsgn,gcn->bsgc', h_im, c_im.astype(jnp.float32))).reshape(b, s, SSM_WIDTH)
    y = jax.nn.gelu(y + d_skip.astype(jnp.float32) * u).astype(x.dtype)
    z = y @ w_glu
    return x + z[..., :D_MODEL] * jax.nn.sigmoid(z[..., D_MODEL:])

def _moe_swiglu_layer(x, norm_g, w_router, w_gate, w_up, w_down):
    b, s, d = x.shape
    xt = _rms_norm(x, norm_g).reshape(-1, d)
    n_tok = xt.shape[0]
    logits = xt.astype(jnp.float32) @ w_router.astype(jnp.float32)
    top_vals, top_idx = lax.top_k(logits, TOP_K)
    gates = jax.nn.softmax(top_vals, axis=-1)
    n_assign = n_tok * TOP_K
    flat_e = top_idx.reshape(-1).astype(jnp.int32)
    flat_tok = jnp.repeat(jnp.arange(n_tok, dtype=jnp.int32), TOP_K)
    flat_w = gates.reshape(-1)
    order = jnp.argsort(flat_e)
    e_sorted = flat_e[order]
    counts = jnp.bincount(flat_e, length=N_EXPERTS_2).astype(jnp.int32)
    padded = (counts + EXPERT_BLOCK - 1) // EXPERT_BLOCK * EXPERT_BLOCK
    pad_end = jnp.cumsum(padded)
    pad_start = pad_end - padded
    unpad_start = jnp.cumsum(counts) - counts
    dest = pad_start[e_sorted] + jnp.arange(n_assign, dtype=jnp.int32) - unpad_start[e_sorted]
    n_slots = (n_assign + EXPERT_BLOCK - 1) // EXPERT_BLOCK * EXPERT_BLOCK + N_EXPERTS_2 * EXPERT_BLOCK
    n_blocks = n_slots // EXPERT_BLOCK
    slot_tok = jnp.zeros((n_slots,), jnp.int32).at[dest].set(flat_tok[order])
    slot_w = jnp.zeros((n_slots,), jnp.float32).at[dest].set(flat_w[order])
    blk_start = jnp.arange(n_blocks, dtype=jnp.int32) * EXPERT_BLOCK
    blk_expert = jnp.clip(jnp.searchsorted(pad_end, blk_start, side='right'), 0, N_EXPERTS_2 - 1)
    xs = xt[slot_tok].reshape(n_blocks, EXPERT_BLOCK, d)

    def expert_block(args):
        xb, e = args
        return (jax.nn.silu(xb @ w_gate[e]) * (xb @ w_up[e])) @ w_down[e]

    ys = lax.map(expert_block, (xs, blk_expert)).reshape(n_slots, d)
    out = jax.ops.segment_sum(ys.astype(jnp.float32) * slot_w[:, None], slot_tok, num_segments=n_tok)
    return x + out.reshape(b, s, d).astype(x.dtype)

def second_inputs(seed: int = 0) -> dict:
    key = jax.random.key(seed)
    ks = jax.random.split(key, 30)
    f32 = jnp.float32

    def nrm(k, shape, scale):
        return jax.random.normal(k, shape, f32) * scale

    def gain(k, shape):
        return 1.0 + 0.02 * jax.random.normal(k, shape, f32)

    ne, no = N_EVEN, N_ODD
    return {
        'x': jax.random.normal(ks[0], (BATCH, SEQ, D_MODEL), f32),
        'att_norm': gain(ks[1], (ne, D_MODEL)),
        'att_w_in': nrm(ks[2], (ne, D_MODEL, IN_COLS), D_MODEL ** -0.5),
        'att_q_latent_norm': gain(ks[3], (ne, MLA_Q_RANK)),
        'att_w_q_up': nrm(ks[4], (ne, MLA_Q_RANK, MLA_HEADS * MLA_QK_DIM), MLA_Q_RANK ** -0.5),
        'att_kv_latent_norm': gain(ks[5], (ne, MLA_KV_RANK)),
        'att_w_kv_up': nrm(ks[6], (ne, MLA_KV_RANK, MLA_HEADS * (MLA_NOPE_DIM + MLA_V_DIM)), MLA_KV_RANK ** -0.5),
        'att_q_norm': gain(ks[7], (ne, MLA_QK_DIM)),
        'att_k_norm': gain(ks[8], (ne, MLA_QK_DIM)),
        'att_w_out': nrm(ks[9], (ne, MIX_WIDTH, D_MODEL), MIX_WIDTH ** -0.5),
        'dffn_norm': gain(ks[10], (ne, D_MODEL)),
        'dffn_w_gate': nrm(ks[11], (ne, D_MODEL, D_FF), D_MODEL ** -0.5),
        'dffn_w_up': nrm(ks[12], (ne, D_MODEL, D_FF), D_MODEL ** -0.5),
        'dffn_w_down': nrm(ks[13], (ne, D_FF, D_MODEL), D_FF ** -0.5),
        'ssm_norm': gain(ks[14], (no, D_MODEL)),
        'ssm_w_in': nrm(ks[15], (no, D_MODEL, SSM_WIDTH), D_MODEL ** -0.5),
        'ssm_a_re': -0.5 + nrm(ks[16], (no, SSM_GROUPS, SSM_STATE), 0.01),
        'ssm_a_im': math.pi * jnp.arange(SSM_STATE, dtype=f32)[None, None, :]
                    + nrm(ks[17], (no, SSM_GROUPS, SSM_STATE), 0.01),
        'ssm_log_dt': jax.random.uniform(ks[18], (no, SSM_GROUPS), f32,
                                         minval=math.log(DT_MIN), maxval=math.log(DT_MAX)),
        'ssm_b_re': nrm(ks[19], (no, SSM_GROUPS, SSM_STATE, SSM_GROUP), (2 * SSM_GROUP) ** -0.5),
        'ssm_b_im': nrm(ks[20], (no, SSM_GROUPS, SSM_STATE, SSM_GROUP), (2 * SSM_GROUP) ** -0.5),
        'ssm_c_re': nrm(ks[21], (no, SSM_GROUPS, SSM_GROUP, SSM_STATE), 0.5),
        'ssm_c_im': nrm(ks[22], (no, SSM_GROUPS, SSM_GROUP, SSM_STATE), 0.5),
        'ssm_d': nrm(ks[23], (no, SSM_WIDTH), 1.0),
        'ssm_w_glu': nrm(ks[24], (no, SSM_WIDTH, 2 * D_MODEL), SSM_WIDTH ** -0.5),
        'moe_norm': gain(ks[25], (no, D_MODEL)),
        'moe_router': nrm(ks[26], (no, D_MODEL, N_EXPERTS_2), D_MODEL ** -0.5),
        'moe_w_gate': nrm(ks[27], (no, N_EXPERTS_2, D_MODEL, D_FF), D_MODEL ** -0.5),
        'moe_w_up': nrm(ks[28], (no, N_EXPERTS_2, D_MODEL, D_FF), D_MODEL ** -0.5),
        'moe_w_down': nrm(ks[29], (no, N_EXPERTS_2, D_FF, D_MODEL), D_FF ** -0.5),
    }

def second_block(x, att_norm, att_w_in, att_q_latent_norm, att_w_q_up, att_kv_latent_norm, att_w_kv_up,
              att_q_norm, att_k_norm, att_w_out, dffn_norm, dffn_w_gate, dffn_w_up, dffn_w_down,
              ssm_norm, ssm_w_in, ssm_a_re, ssm_a_im, ssm_log_dt, ssm_b_re, ssm_b_im, ssm_c_re, ssm_c_im,
              ssm_d, ssm_w_glu, moe_norm, moe_router, moe_w_gate, moe_w_up, moe_w_down):
    h = x
    for layer in range(DEPTH_2):
        i = layer // 2
        if layer % 2 == 0:
            h = _attention_layer(h, att_norm[i], att_w_in[i], att_q_latent_norm[i], att_w_q_up[i],
                                 att_kv_latent_norm[i], att_w_kv_up[i], att_q_norm[i], att_k_norm[i],
                                 att_w_out[i])
            h = _dense_swiglu_layer(h, dffn_norm[i], dffn_w_gate[i], dffn_w_up[i], dffn_w_down[i])
        else:
            h = _s5_layer(h, ssm_norm[i], ssm_w_in[i], ssm_a_re[i], ssm_a_im[i], ssm_log_dt[i],
                          ssm_b_re[i], ssm_b_im[i], ssm_c_re[i], ssm_c_im[i], ssm_d[i], ssm_w_glu[i])
            h = _moe_swiglu_layer(h, moe_norm[i], moe_router[i], moe_w_gate[i], moe_w_up[i], moe_w_down[i])
    return h


def setup_inputs(seed=0):
    out = dict(first_inputs(seed))
    for name, value in second_inputs(seed + 1).items():
        if name != "x":
            out[name + "_2"] = value
    return out


def reference(
    x, ln1_w, w_in, rw_mu, rw_w0_f, rw_w2_f, rw_w0_b, rw_w2_b, rw_a0_f, rw_a2_f, rw_a0_b,
    rw_a2_b, rw_g2, rw_k_k, rw_k_a, rw_r_k, rw_ln_w, rw_ln_b, gla_gw2_f, gla_gb_f, gla_gw2_b,
    gla_gb_b, gla_norm_w, w_out, ln2_w, moe_w_coarse, moe_b_coarse, moe_w_fine, moe_b_fine,
    moe_w_gate, moe_w_up, moe_w_down, ln_f_w, att_norm_2, att_w_in_2, att_q_latent_norm_2,
    att_w_q_up_2, att_kv_latent_norm_2, att_w_kv_up_2, att_q_norm_2, att_k_norm_2, att_w_out_2,
    dffn_norm_2, dffn_w_gate_2, dffn_w_up_2, dffn_w_down_2, ssm_norm_2, ssm_w_in_2, ssm_a_re_2,
    ssm_a_im_2, ssm_log_dt_2, ssm_b_re_2, ssm_b_im_2, ssm_c_re_2, ssm_c_im_2, ssm_d_2,
    ssm_w_glu_2, moe_norm_2, moe_router_2, moe_w_gate_2, moe_w_up_2, moe_w_down_2,
):
    x = first_block(
        x, ln1_w, w_in, rw_mu, rw_w0_f, rw_w2_f, rw_w0_b, rw_w2_b, rw_a0_f, rw_a2_f, rw_a0_b,
        rw_a2_b, rw_g2, rw_k_k, rw_k_a, rw_r_k, rw_ln_w, rw_ln_b, gla_gw2_f, gla_gb_f,
        gla_gw2_b, gla_gb_b, gla_norm_w, w_out, ln2_w, moe_w_coarse, moe_b_coarse, moe_w_fine,
        moe_b_fine, moe_w_gate, moe_w_up, moe_w_down, ln_f_w,
    )
    return second_block(
        x, att_norm_2, att_w_in_2, att_q_latent_norm_2, att_w_q_up_2, att_kv_latent_norm_2,
        att_w_kv_up_2, att_q_norm_2, att_k_norm_2, att_w_out_2, dffn_norm_2, dffn_w_gate_2,
        dffn_w_up_2, dffn_w_down_2, ssm_norm_2, ssm_w_in_2, ssm_a_re_2, ssm_a_im_2,
        ssm_log_dt_2, ssm_b_re_2, ssm_b_im_2, ssm_c_re_2, ssm_c_im_2, ssm_d_2, ssm_w_glu_2,
        moe_norm_2, moe_router_2, moe_w_gate_2, moe_w_up_2, moe_w_down_2,
    )


_drawn_inputs = setup_inputs


def setup_inputs(seed=0):
    import zlib

    import numpy as np

    out = dict(_drawn_inputs(seed))
    spreads = {}
    factors = {'rw_ln_b': 4.122,
     'moe_b_coarse': 3.5,
     'moe_b_fine': 3.016,
     'att_q_latent_norm_2': 5.425,
     'att_kv_latent_norm_2': 3.754,
     'att_q_norm_2': 3.385,
     'att_k_norm_2': 4.162,
     'ssm_norm_2': 42.958,
     'ssm_a_re_2': 200.0,
     'dffn_norm_2': 5.68,
     'moe_norm_2': 4.348,
     'ssm_a_im_2': 2.9,
     'ssm_log_dt_2': 2.913,
     'ssm_b_re_2': 2.863,
     'ssm_b_im_2': 3.255,
     'ssm_c_re_2': 2.995,
     'ssm_c_im_2': 2.827}
    for name, (base, spread) in spreads.items():
        noise = np.random.default_rng([zlib.crc32(name.encode()), seed]).standard_normal(out[name].shape)
        drawn = base * np.exp(spread * noise) if base else spread * noise
        out[name] = jnp.asarray(drawn.astype(out[name].dtype))
    for name, factor in factors.items():
        out[name] = (out[name] * factor).astype(out[name].dtype)
    return out
```

```python
from contextlib import ExitStack

import numpy as np
import concourse.bass as bass
from concourse import mybir

F32 = mybir.dt.float32
ALU = mybir.AluOpType
ACT = mybir.ActivationFunctionType
AXX = mybir.AxisListType.X

P = 128
T = 256
TT = T // P
D = 1024
KT = D // P
CH = 64
NCH = T // CH
HD = 64
NH = 8
HP = NH // 2
NLEV = 6
DIRS = 2
W = NH * HD
EXPM = float(np.exp(np.float32(-0.5)))
EPS = 1e-6
GN_EPS = 64e-5

RW_COLS = 1920
GL_Q = RW_COLS
GL_V = GL_Q + 512
GL_GATE = GL_V + 512
GL_OG = GL_GATE + 32

AT_V = 1024
AT_CQ = 1536
AT_KR = AT_CQ + 256 + 128
MR, MN, MQK = 32, 64, 96

N_E1, F1 = 32, 512
N_E2, F2 = 8, 3584
FC = 512
NFC = F2 // FC

PAR = {}
_n = 0
for _name, _c in (("ln1", 8), ("mu", 15), ("w0", 8), ("a0", 8), ("k_k", 4), ("k_a", 4), ("r_k", 4), ("gb", 4),
                  ("ln2", 8), ("att", 8), ("qlat", 2), ("kvlat", 1), ("dffn", 8), ("ssm", 8), ("moe", 8),
                  ("sd", 4), ("lre", 16), ("lim", 16), ("ldt", 16)):
    PAR[_name] = (_n, _c)
    _n += _c
NPAR = _n
ROW = {}
_n = 0
for _name, _c in (("ln_w", 512), ("ln_b", 512), ("gnorm", 512), ("lnf", 1024), ("qn", 96), ("kn", 96),
                  ("rb", 36)):
    ROW[_name] = (_n, _c)
    _n += _c
NROW = _n


def constants():
    i = np.arange(P)
    r, c = i[:, None], i[None, :]
    same = (r // CH) == (c // CH)
    up = same & (r < c)
    dn = same & (r > c)
    eye = r == c
    k = {"ident": eye}
    k["mask2"] = np.concatenate([up, up | eye, dn, dn | eye], 1)
    lev = []
    for l in range(1, NLEV + 1):
        b = 2 ** l
        lev.append((r // b == c // b) & (r % b >= b // 2) & (c % b < b // 2))
    k["levf"] = np.concatenate(lev, 1)
    k["levb"] = np.concatenate([m.T for m in lev], 1)
    k["headones"] = (r // HD) == (c // HD)
    t = np.arange(T)
    k["reset"] = np.concatenate([np.tile(t % CH != 0, (P, 1)), np.tile(t % CH != CH - 1, (P, 1))], 1)
    k["before"] = r < c
    k["after"] = r > c
    k["ones"] = np.ones((P, P))
    k["eye2"] = (r % HD) == i[None, :HD]
    k["causal"] = np.where(c <= r, 0.0, -1e30)
    half = MR // 2
    inv = np.float32(10000.0) ** (-np.arange(0, MR, 2, dtype=np.float32) / np.float32(MR))
    ang = np.arange(T, dtype=np.float32)[:, None] * inv[None, :]
    rope = np.stack([np.cos(ang), np.sin(ang)], 1).reshape(TT, P, 2 * half).transpose(1, 0, 2)
    k["rope"] = rope.reshape(P, TT * 2 * half)
    return {n: np.ascontiguousarray(a, np.float32) for n, a in k.items()}


CONST_COLS = {n: a.shape[1] for n, a in constants().items()}
C0 = {}
_n = 0
for _name, _c in CONST_COLS.items():
    C0[_name] = (_n, _c)
    _n += _c
NCONST = _n


class Ring:

    def __init__(self, banks, filled, emptied, stages):
        self.banks, self.filled, self.emptied = banks, filled, emptied
        self.at, n = {}, 0
        for name, count in stages:
            self.at[name] = n
            n += count
        self.total = n

    def bank(self, n):
        return self.banks[n % 4]

    def claim(self, pe, n):
        if n >= 4:
            pe.wait_ge(self.emptied, n - 3)
        return self.banks[n % 4]

    def take(self, eng, n):
        eng.wait_ge(self.filled, n + 1)
        return self.banks[n % 4]

    def landed(self, eng, n):
        eng.wait_ge(self.emptied, n + 1)


class Own:

    def __init__(self, eng, sem):
        self.eng, self.sem, self.n = eng, sem, 0

    def __call__(self, ins):
        ins.then_inc(self.sem, 1)
        self.n += 1
        return self.n

    def settle(self):
        if self.n:
            self.eng.wait_ge(self.sem, self.n)


def block_kernel(nc, a, out):
    ctx = ExitStack()
    with ctx:
        def sb(name, shape, dt=F32, stack=None):
            return (stack or ctx).enter_context(nc.sbuf_tensor(name, shape, dt))

        def sem(name):
            return ctx.enter_context(nc.semaphore(name))

        par = sb("par", [P, NPAR])
        rows = sb("rows", [P, NROW])
        con = sb("con", [P, NCONST])
        x_sb = sb("x_sb", [P, TT, D])
        xn = sb("xn", [P, TT, D])
        hT = sb("hT", [P, KT, T])
        st = sb("st", [P, 96])
        slot = [sb(f"slot{i}", [P, KT, FC]) for i in range(3)]

        def pcol(name, i=0, n=1):
            o = PAR[name][0] + i
            return par[:, o:o + n]

        def row(name):
            o, n = ROW[name]
            return rows[:, o:o + n]

        def cst(name, i=0, n=None):
            o, m = C0[name]
            n = m if n is None else n
            return con[:, o + i * n:o + i * n + n]

        ident = cst("ident")
        psum = [ctx.enter_context(nc.psum_tensor(f"ps{i}", [P, 512], F32)) for i in range(8)]

        gla = ExitStack()
        qkT = sb("qkT", [P, 4, T], stack=gla)
        Vg = sb("Vg", [P, TT, W], stack=gla)
        glT = sb("glT", [32, T], stack=gla)
        gw2 = sb("gw2", [32, DIRS, T], stack=gla)
        ogs = sb("ogs", [P, TT, W], stack=gla)
        gz = sb("gz", [P, DIRS, 2 * T], stack=gla)
        ge = sb("ge", [P, DIRS, 2 * T], stack=gla)
        gc = sb("gc", [P, 2, T], stack=gla)
        gce = sb("gce", [P, 2, T], stack=gla)
        gP = sb("gP", [P, 3, 2 * T], stack=gla)
        gPc = sb("gPc", [P, 2 * NCH], stack=gla)
        gR = sb("gR", [P, 2, T], stack=gla)
        gK = sb("gK", [P, 2, T], stack=gla)
        gKh = sb("gKh", [P, 2, T], stack=gla)
        gKt = sb("gKt", [P, TT, 2 * P], stack=gla)
        gQ = sb("gQ", [P, TT, 4, P], stack=gla)
        gH = sb("gH", [P, NCH, 2, P], stack=gla)
        gS = sb("gS", [P, NCH, 2, P], stack=gla)
        Yg = sb("Yg", [P, TT, W], stack=gla)
        Yq = sb("Yq", [P, TT, W], stack=gla)
        gla.close()

        rw = ExitStack()
        pT = sb("pT", [P, 15, T], stack=rw)
        kk = sb("kk", [P, 4, T], stack=rw)
        w2 = sb("w2", [P, W], stack=rw)
        a2 = sb("a2", [P, W], stack=rw)
        g2 = sb("g2", [P, W], stack=rw)
        omka = sb("omka", [P, 4], stack=rw)
        mus = sb("mus", [P, 2, 15], stack=rw)
        Vt = hT[:, 0:4, :].rearrange("p a b -> p (a b)").rearrange("p (t w) -> p t w", t=TT)
        kds = hT[:, 4:8, :]
        Yr = xn[:, :, 0:W]
        bon = sb("bon", [P, TT, NH], stack=rw)
        sca = sb("sca", [P, 3, 4 * T], stack=rw)
        Pc = sb("Pc", [P, 4 * NCH], stack=rw)
        AR = sb("AR", [P, 4, TT, 2, P], stack=rw)
        BK = sb("BK", [P, 2, 4, T], stack=rw)
        BKh = sb("BKh", [P, 2, 4, T], stack=rw)
        BKt = sb("BKt", [P, 2, W], stack=rw)
        AM = sb("AM", [P, NH, P], stack=rw)
        LN = sb("LN", [P, NH, 2, P], stack=rw)
        MQ = sb("MQ", [P, NH, 2, P], stack=rw)
        L1 = sb("L1", [P, NH, P], stack=rw)
        X = sca[:, 0, :].rearrange("p (h c) -> p h c", h=NH)
        XT = sca[:, 1, :].rearrange("p (h c) -> p h c", h=NH)
        WM = sca[:, 2, :].rearrange("p (h c) -> p h c", h=NH)
        TAM = L1
        Rf = sb("Rf", [P, TT, 4, P], stack=rw)
        GT = sb("GT", [P, NCH, 4, HD], stack=rw)
        Hc = sb("Hc", [P, NCH, 4, HD], stack=rw)
        S = sb("S", [P, NCH, 4, HD], stack=rw)
        rw.close()

        slot += [sb(f"slot{i}", [P, KT, FC]) for i in range(3, 6)]
        att = ExitStack()
        sqkT = sb("sqkT", [P, 8, T], stack=att)
        sV = sb("sV", [P, TT, W], stack=att)
        lat = sb("lat", [P, TT, 416], stack=att)
        latT = sb("latT", [P, 3, T], stack=att)
        wq_up = sb("wq_up", [P, 2, NH * MQK], stack=att)
        wkv_up = sb("wkv_up", [P, NH * P], stack=att)
        qh = xn[:, :, 0:NH * MQK].rearrange("p t (h c) -> p t h c", h=NH)
        kh = sb("kh", [P, TT, NH, MQK], stack=att)
        mV = sb("mV", [P, TT, NH, HD], stack=att)
        qhT = sb("qhT", [MQK, NH, T], stack=att)
        khT = sb("khT", [MQK, NH, T], stack=att)
        rp = sb("rp", [P, 3, NH * MR // 2], stack=att)
        sqr = sb("sqr", [P, NH * MQK], stack=att)
        stt = sb("stt", [P, 8, NH], stack=att)
        za = wq_up[:, :, :].rearrange("p a b -> p (a b)").rearrange("p (a b) -> p a b", a=3)
        lf = wkv_up[:, 0:2 * T].rearrange("p (a b) -> p a b", a=2)
        wT = wkv_up[:, 2 * T:4 * T].rearrange("p (a b) -> p a b", a=2)
        pTt = wkv_up[:, 0:6 * P].rearrange("p (a b) -> p a b", a=2)
        att.close()

        ssm = ExitStack()
        uT = sb("uT", [P, 4, T], stack=ssm)
        bT = sb("bT", [P, 4, 2, P], stack=ssm)
        cT = sb("cT", [P, 16, 2, 32], stack=ssm)
        par16 = sb("par16", [P, 24, 16], stack=ssm)
        pi16 = sb("pi16", [P, 16], mybir.dt.int32, stack=ssm)
        rot = sb("rot", [P, 2, 16, T], stack=ssm)
        rtm = sb("rtm", [P, 2, 16, T // 2], stack=ssm)
        yT = hT[:, 0:4, :]
        vst = xn[:, 0, :].rearrange("p (a b) -> p a b", a=4)
        hst = xn[:, 1, 0:2 * T].rearrange("p (a b) -> p a b", a=2)
        gsig = xn[:, 1, 512:1024]
        gsig2 = hT[:, 4:6, :].rearrange("p a b -> p (a b)")
        ssm.close()

        ffn = ExitStack()
        sg = sb("sg", [P, 2, T], stack=ffn)
        hact = sb("hact", [P, 2, 4, T], stack=ffn)
        wr = sb("wr", [P, KT, 48], stack=ffn)
        lg = sb("lg", [P, TT, 36], stack=ffn)
        lm = sb("lm", [P, TT, 32], stack=ffn)
        top = sb("top", [P, TT, 8], stack=ffn)
        wexp = sb("wexp", [P, TT, N_E1], stack=ffn)
        ffn.close()

        misc_in = sem("misc_in")
        x_in = sem("x_in")
        lora_in = sem("lora_in")
        up_in = sem("up_in")
        ssm_in = sem("ssm_in")
        router_in = sem("router_in")
        slot_in = [sem(f"slot_in{i}") for i in range(6)]
        v_filled, v_emptied = sem("v_filled"), sem("v_emptied")
        s_filled, s_emptied = sem("s_filled"), sem("s_emptied")
        dve_own, act_own = sem("dve_own"), sem("act_own")
        meansq = sem("meansq")
        rooted = sem("rooted")
        normed = sem("normed")
        gl_arg = sem("gl_arg")
        gl_val = sem("gl_val")
        gl_ops = sem("gl_ops")
        shifted = sem("shifted")
        lora_act = sem("lora_act")
        kk_sq = sem("kk_sq")
        cum = sem("cum")
        cum_exp = sem("cum_exp")
        rw_ops = sem("rw_ops")
        inv_start = sem("inv_start")
        mixed = sem("mixed")
        w_read = sem("w_read")
        lat_ready = sem("lat_ready")
        heads_ready = sem("heads_ready")
        z_ready = sem("z_ready")
        z_soft = sem("z_soft")
        fails = sem("fails")
        w_arg = sem("w_arg")
        w_exp = sem("w_exp")
        w_ready = sem("w_ready")
        maxed = sem("maxed")
        p_exp = sem("p_exp")
        p_ready = sem("p_ready")
        logit_max = sem("logit_max")
        logit_exp = sem("logit_exp")
        silu_done = sem("silu_done")
        s5_arg = sem("s5_arg")
        s5_val = sem("s5_val")
        s5_mat = sem("s5_mat")
        s5_h = sem("s5_h")
        y_sum = sem("y_sum")
        y_gelu = sem("y_gelu")
        glu_sig = sem("glu_sig")
        out_ready = sem("out_ready")
        out_done = sem("out_done")

        inv_items = 4 + 4 + 2 + (NLEV - 1) * 2 + (NLEV - 2) * 2 + (NLEV - 1) * 2 + 4
        V = Ring(psum[0:4], v_filled, v_emptied, [
            ("ln1", 4), ("gl_z", 2)]
            + [(f"gl{d}_{n}", c) for d in range(DIRS) for n, c in (("q", 2), ("h", 2), ("y", 2))]
            + [("rw_p", 8), ("kk", 2)]
            + [(f"rw{d}_{n}", c) for d in range(DIRS) for n, c in (("t0", inv_items), ("t1", inv_items), ("s", 2), ("y", 2))]
            + [("bonus", 1), ("gate", 2), ("mixT", 4), ("wout", 4), ("ln2", 4), ("route1", 1), ("moe1", 4 * N_E1),
               ("att", 4), ("lat", 2), ("q_up", 4), ("kv_up", 4), ("stick", 16), ("mla", 8), ("wout2", 4),
               ("dffn", 4), ("ffn", 4 * NFC), ("ssm", 4), ("u", 2), ("s5", 32), ("glu", 4),
               ("moe", 4), ("route2", 1), ("moe2", 4 * N_E2 * NFC)])
        S_ = Ring(psum[4:8], s_filled, s_emptied, [
            ("gl_qk", 2), ("gl_v", 2), ("gl_g", 1), ("gl_og", 2), ("gl0_kt", 1), ("gl1_kt", 1),
            ("vt", 2)]
            + [(f"rw{d}_{n}", c) for d in range(DIRS) for n, c in (("lora", 4), ("t0", 8), ("t1", 8))]
            + [("moe1", 4 * N_E1), ("sqk", 4), ("sv", 2), ("lat", 2), ("headsT", 8)]
            + [(f"st{h}", 1) for h in range(HP)]
            + [(f"ml{h}", c) for h in range(HP) for c in (3,)]
            + [("ffn", 4 * NFC), ("glu", 4), ("moe2", 4 * N_E2 * NFC)])


        loads, uses = {}, [0] * 6

        def use(name, i):
            uses[i] += 1
            loads[name] = (i, uses[i])

        for n, i in (("g0", 0), ("g1", 1), ("g2", 2), ("g3", 0), ("r0", 1), ("r1", 2), ("r2", 0), ("r3", 1),
                     ("o0", 2), ("o1", 0)):
            use(n, i)
        moe1_use = list(uses)
        uses = [u + N_E1 // 2 for u in uses]
        for n, i in (("a0", 0), ("a1", 1), ("a2", 2), ("a3", 3), ("p0", 4), ("p1", 5)):
            use(n, i)
        ffn_use = list(uses)
        for u in range(NFC):
            for j in range(3):
                use(f"f{u}_{j}", 3 * (u % 2) + j)
        for n, i in (("s0", 3), ("s1", 4), ("s2", 5)):
            use(n, i)
        moe2_use = list(uses)

        def arrived(eng, name):
            i, n = loads[name]
            eng.wait_ge(slot_in[i], 16 * n)
            return slot[i]

        win = a["w_in"][0].rearrange("(t p) n -> p t n", p=P)
        ROOTS = ["ln1", "gla", "kk", "gn", "ln2", "lnf", "att", "lat", "heads", "dffn", "ssm", "moe"]
        NORMS = ["ln1", "ln2", "att", "dffn", "ssm", "moe"]
        block = ctx.enter_context(nc.Block())

        @block.sync
        def _(sp):
            def load(name, src, ring=None, item=None):
                if ring is not None:
                    sp.wait_ge(ring.filled, item + 1)
                i, n = loads[name]
                sp.dma_start(slot[i][:, 0:src.shape[1], 0:src.shape[2]], src).then_inc(slot_in[i], 16)

            sp.dma_start(x_sb[:], a["x"][0].rearrange("(t p) d -> p t d", p=P)).then_inc(x_in, 16)
            sp.dma_start(par[:], a["par"]).then_inc(misc_in, 16)
            sp.dma_start(con[:], a["con"]).then_inc(misc_in, 16)
            load("g0", win[:, :, GL_Q:GL_Q + 512])
            load("g1", win[:, :, GL_V:GL_V + 512])
            load("g2", win[:, :, GL_GATE:GL_GATE + 32])
            sp.dma_start(rows[:], a["rows"].partition_broadcast(P)).then_inc(misc_in, 16)
            sp.dma_start(gw2[:], a["gw2"]).then_inc(misc_in, 16)
            load("g3", win[:, :, GL_OG:GL_OG + 512], S_, S_.at["gl_qk"] + 1)
            load("r0", win[:, :, 0:512], S_, S_.at["gl_v"] + 1)
            load("r1", win[:, :, 512:1024], S_, S_.at["gl_g"])
            load("r2", win[:, :, 1024:1536], S_, S_.at["gl_og"] + 1)
            sp.wait_ge(mixed, 1)
            sp.dma_start(w2[:], a["w2"]).then_inc(lora_in, 16)
            sp.dma_start(a2[:], a["a2"]).then_inc(lora_in, 16)
            sp.dma_start(g2[:], a["rw_g2"][0]).then_inc(lora_in, 16)
            load("r3", win[:, :, 1536:RW_COLS], V, V.at["rw_p"] + 1)
            wo = a["w_out"][0].rearrange("(t p) n -> p t n", p=P)
            load("o0", wo[:, :, 0:512], V, V.at["rw_p"] + 3)
            load("o1", wo[:, :, 512:1024], V, V.at["rw_p"] + 5)

            def unit(parity, gate, up, down, vwait, swait):
                s = 3 * parity
                if vwait is not None:
                    sp.wait_ge(v_filled, vwait)
                sp.dma_start(slot[s][:], gate.rearrange("(t p) n -> p t n", p=P)).then_inc(slot_in[s], 16)
                sp.dma_start(slot[s + 1][:], up.rearrange("(t p) n -> p t n", p=P)).then_inc(slot_in[s + 1], 16)
                if swait is not None:
                    sp.wait_ge(s_filled, swait)
                sp.dma_start(slot[s + 2][:].rearrange("p a b -> p (a b)").rearrange("p (t n) -> p t n", t=4),
                             down.rearrange("(t p) n -> p t n", p=P)).then_inc(slot_in[s + 2], 16)

            g1, u1, d1 = a["moe_w_gate"][0], a["moe_w_up"][0], a["moe_w_down"][0]
            v1, s1 = V.at["moe1"], S_.at["moe1"]
            sp.wait_ge(mixed, 2)
            sp.wait_ge(v_filled, V.at["wout"] + 4)
            sp.dma_start(wr[:, :, 0:36], a["wr1"].rearrange("(t p) n -> p t n", p=P)).then_inc(router_in, 16)
            unit(0, g1[0], u1[0], d1[0], None, None)
            unit(1, g1[1], u1[1], d1[1], None, None)
            with sp.Fori(1, N_E1 // 2) as i:
                for s in range(2):
                    e = 2 * i + s
                    unit(s, g1[bass.ds(e, 1), :, :].rearrange("o k n -> (o k) n"),
                         u1[bass.ds(e, 1), :, :].rearrange("o k n -> (o k) n"),
                         d1[bass.ds(e, 1), :, :].rearrange("o k n -> (o k) n"),
                         v1 + 8 * i + 4 * s - 4, s1 + 8 * i + 4 * s - 4)
            aw = a["att_w_in_2"][0].rearrange("(t p) n -> p t n", p=P)
            load("a0", aw[:, :, 0:512], V, v1 + 4 * N_E1 - 5)
            load("a1", aw[:, :, 512:1024])
            load("a2", aw[:, :, 1024:1536], S_, s1 + 4 * N_E1 - 5)
            load("a3", aw[:, :, 1536:1952], V, v1 + 4 * N_E1 - 1)
            ow = a["att_w_out_2"][0].rearrange("(t p) n -> p t n", p=P)
            load("p0", ow[:, :, 0:512])
            load("p1", ow[:, :, 512:1024], S_, s1 + 4 * N_E1 - 1)
            sp.wait_ge(mixed, 3)
            sp.dma_start(wq_up[:], a["att_w_q_up_2"][0].rearrange("(t p) n -> p t n", p=P)).then_inc(up_in, 16)
            sp.dma_start(wkv_up[:], a["att_w_kv_up_2"][0]).then_inc(up_in, 16)
            fg, fu, fd = a["dffn_w_gate_2"][0], a["dffn_w_up_2"][0], a["dffn_w_down_2"][0]
            vf, sf = V.at["ffn"], S_.at["ffn"]
            for u in range(NFC):
                c = slice(u * FC, u * FC + FC)
                if u == 0:
                    vw, sw = None, None
                    sp.wait_ge(s_filled, S_.at["sv"] + 2)
                elif u == 1:
                    vw, sw = V.at["wout2"] + 4, None
                else:
                    vw, sw = vf + 4 * (u - 1), sf + 4 * (u - 1)
                unit(u % 2, fg[:, c], fu[:, c], fd[c, :], vw, sw)
            sp.wait_ge(mixed, 4)
            sp.dma_start(bT[:], a["bT"]).then_inc(ssm_in, 16)
            sp.dma_start(cT[:], a["cT"]).then_inc(ssm_in, 16)
            load("s0", a["ssm_w_in_2"][0].rearrange("(t p) n -> p t n", p=P), V, vf + 4 * (NFC - 1) - 1)
            glu = a["ssm_w_glu_2"][0].rearrange("(t p) n -> p t n", p=P)
            for n, k in (("s1", 0), ("s2", 1)):
                i, _ = loads[n]
                sp.wait_ge(s_filled, sf + 4 * (NFC - 1))
                sp.dma_start(slot[i][:].rearrange("p a b -> p (a b)").rearrange("p (t n) -> p t n", t=4),
                             glu[:, :, k * D:k * D + D]).then_inc(slot_in[i], 16)
            g2_, u2_, d2_ = a["moe_w_gate_2"][0], a["moe_w_up_2"][0], a["moe_w_down_2"][0]
            v2, s2 = V.at["moe2"], S_.at["moe2"]
            unit(0, g2_[0][:, 0:FC], u2_[0][:, 0:FC], d2_[0][0:FC, :], vf + 4 * NFC, sf + 4 * NFC)
            unit(1, g2_[0][:, FC:2 * FC], u2_[0][:, FC:2 * FC], d2_[0][FC:2 * FC, :], V.at["glu"] + 4, S_.at["glu"] + 4)
            sp.dma_start(wr[:, :, 0:8], a["moe_router_2"][0].rearrange("(t p) n -> p t n", p=P)).then_inc(router_in, 16)
            with sp.Fori(1, N_E2 * NFC // 2) as i:
                for s in range(2):
                    n = 2 * i + s
                    e, c = n // NFC, (n % NFC) * FC
                    unit(s, g2_[bass.ds(e, 1), :, bass.ds(c, FC)].rearrange("o k n -> (o k) n"),
                         u2_[bass.ds(e, 1), :, bass.ds(c, FC)].rearrange("o k n -> (o k) n"),
                         d2_[bass.ds(e, 1), bass.ds(c, FC), :].rearrange("o k n -> (o k) n"),
                         v2 + 8 * i + 4 * s - 4, s2 + 8 * i + 4 * s - 4)
            sp.wait_ge(out_ready, 1)
            sp.dma_start(out[0].rearrange("(t p) d -> p t d", p=P), x_sb[:]).then_inc(out_done, 16)
            sp.wait_ge(out_done, 16)

        @block.tensor
        def _(pe):
            def mm(o, l, r, start=True, stop=True):
                return nc.tensor.matmul(o, l, r, start=start, stop=stop)

            def turn(n):
                for j in range(4):
                    b = V.claim(pe, n + j)
                    for k in range(2):
                        for t in range(TT):
                            c = (2 * j + k) * P
                            last = nc.tensor.transpose(b[:, k * T + t * P:k * T + t * P + P],
                                                       xn[:, t, c:c + P], ident)
                    last.then_inc(V.filled, 1)

            def project_T(o, w, c, width=P):
                for k in range(KT):
                    last = mm(o, w[:, k, c:c + width], hT[:, k, :], k == 0, k == KT - 1)
                return last

            def project(o, w, t, c, n):
                for k in range(KT):
                    last = mm(o, hT[:, k, t * P:t * P + P], w[:, k, c:c + n], k == 0, k == KT - 1)
                return last

            pe.wait_ge(misc_in, 64)
            pe.wait_ge(normed, 1)
            turn(V.at["ln1"])
            V.landed(pe, V.at["ln1"] + 3)
            w = arrived(pe, "g0")
            for j in range(2):
                b = S_.claim(pe, S_.at["gl_qk"] + j)
                for k in range(2):
                    last = project_T(b[:, k * T:k * T + T], w, (2 * j + k) * P)
                last.then_inc(S_.filled, 1)
            w = arrived(pe, "g1")
            for t in range(TT):
                project(S_.claim(pe, S_.at["gl_v"] + t)[:, :], w, t, 0, 512).then_inc(S_.filled, 1)
            w = arrived(pe, "g2")
            project_T(S_.claim(pe, S_.at["gl_g"])[0:32, 0:T], w, 0, 32).then_inc(S_.filled, 1)
            w = arrived(pe, "g3")
            for t in range(TT):
                project(S_.claim(pe, S_.at["gl_og"] + t)[:, :], w, t, 0, 512).then_inc(S_.filled, 1)
            S_.landed(pe, S_.at["gl_g"])
            for d in range(DIRS):
                b = V.claim(pe, V.at["gl_z"] + d)
                for k in range(2):
                    last = mm(b[:, k * T:k * T + T], gw2[:, d, k * P:k * P + P], glT[:, :])
                last.then_inc(V.filled, 1)

            for d in range(DIRS):
                order = list(range(NCH))[::1 - 2 * d]
                pe.wait_ge(gl_ops, 2 * d + 1)
                b = S_.claim(pe, S_.at[f"gl{d}_kt"])
                for t in range(TT):
                    for k in range(2):
                        last = nc.tensor.transpose(b[:, t * T + k * P:t * T + k * P + P],
                                                   gKh[:, k, t * P:t * P + P], ident)
                last.then_inc(S_.filled, 1)
                for e in range(2):
                    b = V.claim(pe, V.at[f"gl{d}_q"] + e)
                    o = 64 * e
                    for t in range(TT):
                        for k in range(2):
                            q = (2 * t + k) * P
                            last = mm(b[:, q:q + P], gK[o:o + 64, k, t * P:t * P + P],
                                      gR[o:o + 64, k, t * P:t * P + P])
                    last.then_inc(V.filled, 1)
                S_.landed(pe, S_.at[f"gl{d}_kt"])
                for c in range(2):
                    b = V.claim(pe, V.at[f"gl{d}_h"] + c)
                    for t in range(TT):
                        for h in range(4):
                            o = 64 * (h % 2)
                            last = mm(b[o:o + 64, t * 256 + (h // 2) * P:t * 256 + (h // 2) * P + P],
                                      gKt[64 * c:64 * c + 64, t, h * 64:h * 64 + 64],
                                      Vg[64 * c:64 * c + 64, t, h * P:h * P + P])
                    last.then_inc(V.filled, 1)
                pe.wait_ge(gl_ops, 2 * d + 2)
                for e in range(2):
                    b = V.claim(pe, V.at[f"gl{d}_y"] + e)
                    o = 64 * e
                    for t in range(TT):
                        for k in range(2):
                            h, q = 2 * k + e, (2 * t + k) * P
                            for c in range(2):
                                g = 2 * t + c
                                first = g == order[0]
                                last = mm(b[64 * c:64 * c + 64, q:q + P], gQ[:, t, h, 64 * c:64 * c + 64],
                                          Vg[:, t, h * P:h * P + P], True, first)
                                if not first:
                                    last = mm(b[64 * c:64 * c + 64, q:q + P], gR[o:o + 64, k, g * 64:g * 64 + 64],
                                              gS[o:o + 64, g, k, :], False, True)
                    last.then_inc(V.filled, 1)

            for j in range(8):
                w = arrived(pe, f"r{j // 2}")
                b = V.claim(pe, V.at["rw_p"] + j)
                for k in range(2):
                    c = 2 * j + k
                    if c < 15:
                        last = project_T(b[:, k * T:k * T + T], w, (c % 4) * P)
                last.then_inc(V.filled, 1)
            pe.wait_ge(shifted, 8)
            for t in range(TT):
                b = S_.claim(pe, S_.at["vt"] + t)
                for k in range(4):
                    last = nc.tensor.transpose(b[:, k * P:k * P + P], pT[:, 8 + k, t * P:t * P + P], ident)
                last.then_inc(S_.filled, 1)
            pe.wait_ge(kk_sq, 1)
            for j in range(2):
                b = V.claim(pe, V.at["kk"] + j)
                for k in range(2):
                    last = mm(b[:, k * T:k * T + T], cst("headones"), kds[:, 2 * j + k, :])
                last.then_inc(V.filled, 1)
            pe.wait_ge(lora_in, 48)
            pe.wait_ge(lora_act, 2)

            for d in range(DIRS):
                order = list(range(NCH))[::1 - 2 * d]
                lo = 64 * d
                for i, (wt, src) in enumerate(((w2, 12), (a2, 13))):
                    for j in range(2):
                        b = S_.claim(pe, S_.at[f"rw{d}_lora"] + 2 * i + j)
                        for k in range(2):
                            c = (2 * j + k) * P
                            last = mm(b[:, k * T:k * T + T], wt[lo:lo + 64, c:c + P], pT[lo:lo + 64, src, :])
                        last.then_inc(S_.filled, 1)
                pe.wait_ge(rw_ops, d + 1)
                for t in range(TT):
                    v, s = V.at[f"rw{d}_t{t}"], S_.at[f"rw{d}_t{t}"]
                    tk = slice(t * P, t * P + P)
                    for j in range(3):
                        b = S_.claim(pe, s + j)
                        for k in range(4):
                            src = AR[:, k, t, 0, :] if j == 0 else BKh[:, j - 1, k, tk]
                            last = nc.tensor.transpose(b[:, k * P:k * P + P], src, ident)
                        last.then_inc(S_.filled, 1)
                    for i in range(2):
                        for j in range(4):
                            b = V.claim(pe, v + 4 * i + j)
                            o = 64 * (j // 2)
                            for k in range(2):
                                hp = 2 * (j % 2) + k
                                last = mm(b[:, k * 256:k * 256 + 256], BK[o:o + 64, i, hp, tk],
                                          AR[o:o + 64, hp, t, :, :].rearrange("p a b -> p (a b)"))
                            last.then_inc(V.filled, 1)
                    for e in range(2):
                        b = V.claim(pe, v + 8 + e)
                        o = 64 * e
                        for k in range(4):
                            last = mm(b[:, k * P:k * P + P], AR[o:o + 64, k, t, 0, :], BK[o:o + 64, 0, k, tk])
                        last.then_inc(V.filled, 1)
                    n = v + 10
                    pe.wait_ge(inv_start, 2 * d + t + 1)
                    prev = [None, None]
                    for l in range(2, NLEV + 1):
                        wm_at = n
                        for g in range(2):
                            if prev[g] is not None:
                                V.landed(pe, prev[g])
                            b = V.claim(pe, n)
                            n += 1
                            for q in range(4):
                                h = 4 * g + q
                                last = mm(b[:, q * P:q * P + P], LN[:, h, 0, :], X[:, h, :])
                            last.then_inc(V.filled, 1)
                        for g in range(2):
                            V.landed(pe, wm_at + g)
                            if l < NLEV:
                                b = V.claim(pe, n)
                                n += 1
                                for q in range(4):
                                    h = 4 * g + q
                                    last = mm(b[:, q * P:q * P + P], XT[:, h, :], WM[:, h, :])
                                last.then_inc(V.filled, 1)
                            b = V.claim(pe, n)
                            for q in range(4):
                                h = 4 * g + q
                                last = mm(b[:, q * P:q * P + P], WM[:, h, :], XT[:, h, :])
                            last.then_inc(V.filled, 1)
                            prev[g] = n
                            n += 1
                    if d == 0 and t == 0:
                        S_.landed(pe, S_.at["vt"] + 1)
                    V.landed(pe, v + 9)
                    b = S_.claim(pe, s + 3)
                    for h in range(NH):
                        last = mm(b[:, h * 64:h * 64 + 64], MQ[:, h, 0, :], Vt[:, t, h * 64:h * 64 + 64])
                    last.then_inc(S_.filled, 1)
                    S_.landed(pe, s + 3)
                    for g in range(2):
                        V.landed(pe, prev[g])
                        b = S_.claim(pe, s + 4 + g)
                        for q in range(4):
                            h = 4 * g + q
                            last = mm(b[:, q * P:q * P + P], XT[:, h, :], AM[:, h, :])
                        last.then_inc(S_.filled, 1)
                    S_.landed(pe, s + 5)
                    b = V.claim(pe, n)
                    for h in range(NH):
                        o = 64 * (h % 2)
                        last = mm(b[o:o + 64, (h // 2) * P:(h // 2) * P + P], TAM[:, h, 0:64], LN[:, h, 1, :])
                    last.then_inc(V.filled, 1)
                    for c in range(2):
                        b = V.claim(pe, n + 1 + c)
                        r = slice(64 * c, 64 * c + 64)
                        for h in range(NH):
                            o = 64 * (h % 2)
                            q = (h // 2) * 64
                            last = mm(b[o:o + 64, q:q + 64], TAM[r, h, 0:64], BKt[r, 0, h * 64:h * 64 + 64])
                        last.then_inc(V.filled, 1)
                    for c in range(2):
                        b = S_.claim(pe, s + 6 + c)
                        r = slice(64 * c, 64 * c + 64)
                        for h in range(NH):
                            o = 64 * (h % 2)
                            q = (h // 2) * 64
                            mm(b[o:o + 64, q:q + 64], BKt[r, 1, h * 64:h * 64 + 64],
                               Vt[r, t, h * 64:h * 64 + 64], True, False)
                            last = mm(b[o:o + 64, q:q + 64], BKt[r, 0, h * 64:h * 64 + 64],
                                      TAM[r, h, 64:128], False, True)
                        last.then_inc(S_.filled, 1)
                    n += 1
                    b = V.claim(pe, n + 2)
                    for h in range(NH):
                        c = slice(h * 64, h * 64 + 64)
                        mm(b[:, c], MQ[:, h, 1, :], Vt[:, t, c], True, False)
                        last = mm(b[:, c], LN[:, h, 1, :], TAM[:, h, 64:128], False, True)
                    last.then_inc(V.filled, 1)
                    V.landed(pe, n + 2)
                S_.landed(pe, S_.at[f"rw{d}_t1"] + 7)
                for i in range(2):
                    c0 = order[i + 1]
                    src = Hc[:, order[0]] if i == 0 else S[:, c0]
                    if i:
                        V.landed(pe, V.at[f"rw{d}_s"] + i - 1)
                    b = V.claim(pe, V.at[f"rw{d}_s"] + i)
                    for h in range(NH):
                        o = 64 * (h % 2)
                        last = mm(b[o:o + 64, (h // 2) * 64:(h // 2) * 64 + 64], GT[o:o + 64, c0, h // 2, :],
                                  src[o:o + 64, h // 2, :])
                    last.then_inc(V.filled, 1)
                V.landed(pe, V.at[f"rw{d}_s"] + 1)
                for e in range(2):
                    b = V.claim(pe, V.at[f"rw{d}_y"] + e)
                    o = 64 * e
                    for g in order[1:]:
                        t, c = g // 2, g % 2
                        src = Hc[:, order[0]] if g == order[1] else S[:, g]
                        for k in range(4):
                            last = mm(b[64 * c:64 * c + 64, t * 256 + k * 64:t * 256 + k * 64 + 64],
                                      Rf[o:o + 64, t, k, 64 * c:64 * c + 64], src[o:o + 64, k, :])
                    last.then_inc(V.filled, 1)
            pe.wait_ge(kk_sq, 2)
            b = V.claim(pe, V.at["bonus"])
            for t in range(TT):
                for k in range(4):
                    last = mm(b[:, t * NH + 2 * k:t * NH + 2 * k + 2], kds[:, k, t * P:t * P + P],
                              cst("headones")[:, 0:128:64])
            last.then_inc(V.filled, 1)
            for t in range(TT):
                b = V.claim(pe, V.at["gate"] + t)
                mm(b[:, :], pT[:, 14, t * P:t * P + P], g2[:, :]).then_inc(V.filled, 1)

            pe.wait_ge(mixed, 2)
            turn(V.at["mixT"])
            V.landed(pe, V.at["mixT"] + 3)

            def out_proj(names, n):
                for c, name in enumerate(names):
                    w = arrived(pe, name)
                    for t in range(TT):
                        project(V.claim(pe, n + 2 * c + t)[:, :], w, t, 0, 512).then_inc(V.filled, 1)

            out_proj(("o0", "o1"), V.at["wout"])

            def expert(parity, loaded, name, vn, sn):
                gate, up, down = slot[3 * parity:3 * parity + 3]
                down = down[:].rearrange("p a b -> p (a b)").rearrange("p (t n) -> p t n", t=4)
                pe.wait_ge(slot_in[3 * parity], 16 * loaded[0])
                pe.wait_ge(slot_in[3 * parity + 1], 16 * loaded[1])
                for f in range(4):
                    pe.wait_ge(V.emptied, vn + f - 3)
                    b = V.bank(V.at[name] + f)
                    project_T(b[:, 0:T], gate, f * P)
                    project_T(b[:, T:2 * T], up, f * P).then_inc(V.filled, 1)
                pe.wait_ge(slot_in[3 * parity + 2], 16 * loaded[2])
                pe.wait_ge(V.emptied, vn + 4)
                for t in range(TT):
                    for c in range(2):
                        pe.wait_ge(S_.emptied, sn + 2 * t + c - 3)
                        b = S_.bank(S_.at[name] + 2 * t + c)
                        for f in range(4):
                            last = mm(b[:, :], hact[:, parity, f, t * P:t * P + P],
                                      down[:, f, c * 512:c * 512 + 512], f == 0, f == 3)
                        last.then_inc(S_.filled, 1)

            def experts(units, used, name):
                vn, sn = V.at[name], S_.at[name]
                with pe.Fori(0, units // 2) as i:
                    for s in range(2):
                        k = [used[3 * s + j] + i + 1 for j in range(3)]
                        expert(s, k, name, vn + 8 * i + 4 * s, sn + 8 * i + 4 * s)

            pe.wait_ge(normed, 2)
            turn(V.at["ln2"])
            V.landed(pe, V.at["ln2"] + 3)
            pe.wait_ge(router_in, 16)
            b = V.claim(pe, V.at["route1"])
            for t in range(TT):
                last = project(b[:, t * 36:t * 36 + 36], wr, t, 0, 36)
            last.then_inc(V.filled, 1)
            experts(N_E1, moe1_use, "moe1")

            pe.wait_ge(normed, 3)
            turn(V.at["att"])
            V.landed(pe, V.at["att"] + 3)
            for i in range(2):
                w = arrived(pe, f"a{i}")
                for j in range(2):
                    b = S_.claim(pe, S_.at["sqk"] + 2 * i + j)
                    for k in range(2):
                        last = project_T(b[:, k * T:k * T + T], w, (2 * j + k) * P)
                    last.then_inc(S_.filled, 1)
            w = arrived(pe, "a2")
            for t in range(TT):
                project(S_.claim(pe, S_.at["sv"] + t)[:, :], w, t, 0, 512).then_inc(S_.filled, 1)
            w = arrived(pe, "a3")
            for t in range(TT):
                project(S_.claim(pe, S_.at["lat"] + t)[:, 0:416], w, t, 0, 416).then_inc(S_.filled, 1)
            pe.wait_ge(lat_ready, 1)
            for j in range(2):
                b = V.claim(pe, V.at["lat"] + j)
                for k in range(2 - j):
                    for t in range(TT):
                        c = (2 * j + k) * P
                        last = nc.tensor.transpose(b[:, k * T + t * P:k * T + t * P + P], lat[:, t, c:c + P], ident)
                last.then_inc(V.filled, 1)
            V.landed(pe, V.at["lat"] + 1)
            pe.wait_ge(up_in, 32)
            for t in range(TT):
                for c in range(2):
                    b = V.claim(pe, V.at["q_up"] + 2 * t + c)
                    for k in range(2):
                        last = mm(b[:, 0:384], latT[:, k, t * P:t * P + P], wq_up[:, k, c * 384:c * 384 + 384],
                                  k == 0, k == 1)
                    last.then_inc(V.filled, 1)
            for t in range(TT):
                for c in range(2):
                    b = V.claim(pe, V.at["kv_up"] + 2 * t + c)
                    mm(b[:, :], latT[:, 2, t * P:t * P + P], wkv_up[:, c * 512:c * 512 + 512]).then_inc(V.filled, 1)
            pe.wait_ge(heads_ready, 1)
            for i, src in enumerate((qh, kh)):
                for j in range(4):
                    b = S_.claim(pe, S_.at["headsT"] + 4 * i + j)
                    for k in range(2):
                        for t in range(TT):
                            last = nc.tensor.transpose(b[0:MQK, k * T + t * P:k * T + t * P + P],
                                                       src[:, t, 2 * j + k, :], ident)
                    last.then_inc(S_.filled, 1)
            for h in range(NH):
                o, hp = 64 * (h % 2), h // 2
                b = V.claim(pe, V.at["stick"] + 2 * h)
                for k in range(2):
                    last = mm(b[:, k * T:k * T + T], sqkT[o:o + 64, 4 + hp, k * P:k * P + P], sqkT[o:o + 64, hp, :])
                last.then_inc(V.filled, 1)
                pe.wait_ge(fails, h + 1)
                b = V.claim(pe, V.at["stick"] + 2 * h + 1)
                mm(b[:, 0:T], cst("after"), lf[:, 0, :], True, False)
                mm(b[:, 0:T], cst("ones"), lf[:, 1, :], False, True)
                mm(b[:, T:2 * T], cst("after"), lf[:, 1, :]).then_inc(V.filled, 1)
                if h % 2 == 0:
                    b = S_.claim(pe, S_.at[f"st{hp}"])
                    pair = b
                pe.wait_ge(w_ready, h + 1)
                for k in range(2):
                    last = mm(pair[o:o + 64, 0:T], sV[:, k, h * 64:h * 64 + 64], wT[:, k, :], k == 0, k == 1)
                if h % 2:
                    last.then_inc(S_.filled, 1)
                else:
                    last.then_inc(w_read, 1)
            for h in range(NH):
                o, hp = 64 * (h % 2), h // 2
                if h == 0:
                    S_.landed(pe, S_.at["headsT"] + 7)
                b = V.claim(pe, V.at["mla"] + h)
                for q in range(2):
                    last = mm(b[:, q * T:q * T + T], qhT[:, h, q * P:q * P + P], khT[:, h, :])
                last.then_inc(V.filled, 1)
                pe.wait_ge(p_ready, h + 1)
                b = S_.claim(pe, S_.at[f"ml{hp}"] + h % 2)
                nc.tensor.transpose(b[:, 0:P], za[:, 0, 0:P], ident)
                nc.tensor.transpose(b[:, P:2 * P], za[:, 0, T:T + P], ident)
                nc.tensor.transpose(b[:, 2 * P:3 * P], za[:, 0, T + P:2 * T], ident).then_inc(S_.filled, 1)
                S_.landed(pe, S_.at[f"ml{hp}"] + h % 2)
                if h % 2 == 0:
                    continue
                b = S_.claim(pe, S_.at[f"ml{hp}"] + 2)
                for k in range(2):
                    o = 64 * k
                    src = pTt[:, k, :]
                    mm(b[o:o + 64, 0:T], mV[:, 0, h - 1 + k, :], src[:, 0:T], True, False)
                    last = mm(b[o:o + 64, P:T], mV[:, 1, h - 1 + k, :], src[:, T:T + P], False, True)
                last.then_inc(S_.filled, 1)
            S_.landed(pe, S_.at["ml3"] + 2)
            out_proj(("p0", "p1"), V.at["wout2"])

            pe.wait_ge(normed, 4)
            turn(V.at["dffn"])
            V.landed(pe, V.at["dffn"] + 3)
            for u in range(NFC):
                k = [loads[f"f{u}_{j}"][1] for j in range(3)]
                expert(u % 2, k, "ffn", V.at["ffn"] + 4 * u, S_.at["ffn"] + 4 * u)

            pe.wait_ge(normed, 5)
            turn(V.at["ssm"])
            V.landed(pe, V.at["ssm"] + 3)
            w = arrived(pe, "s0")
            for j in range(2):
                b = V.claim(pe, V.at["u"] + j)
                for k in range(2):
                    last = project_T(b[:, k * T:k * T + T], w, (2 * j + k) * P)
                last.then_inc(V.filled, 1)
            V.landed(pe, V.at["u"] + 1)
            pe.wait_ge(ssm_in, 32)
            for j in range(16):
                o = 32 * (j % 4)
                b = V.claim(pe, V.at["s5"] + 2 * j)
                for k in range(2):
                    last = mm(b[:, k * T:k * T + T], bT[o:o + 32, j // 4, k, :], uT[o:o + 32, j // 4, :])
                last.then_inc(V.filled, 1)
                if j == 0:
                    pe.wait_ge(s5_mat, 1)
                pe.wait_ge(s5_h, j + 1)
                b = V.claim(pe, V.at["s5"] + 2 * j + 1)
                mm(b[o:o + 32, 0:T], cT[:, j, 0, :], hst[:, 0, :], True, False)
                mm(b[o:o + 32, 0:T], cT[:, j, 1, :], hst[:, 1, :], False, True).then_inc(V.filled, 1)
            pe.wait_ge(y_gelu, 1)
            for n, name in enumerate(("s2", "s1")):
                arrived(pe, name)
            gl = [slot[loads[n][0]][:].rearrange("p a b -> p (a b)").rearrange("p (t n) -> p t n", t=4)
                  for n in ("s1", "s2")]
            for t in range(TT):
                for c in range(2):
                    for r, ring in ((1, S_), (0, V)):
                        b = ring.claim(pe, ring.at["glu"] + 2 * t + c)
                        for k in range(4):
                            last = mm(b[:, :], yT[:, k, t * P:t * P + P], gl[r][:, k, c * 512:c * 512 + 512],
                                      k == 0, k == 3)
                        last.then_inc(ring.filled, 1)

            pe.wait_ge(normed, 6)
            turn(V.at["moe"])
            V.landed(pe, V.at["moe"] + 3)
            pe.wait_ge(router_in, 32)
            b = V.claim(pe, V.at["route2"])
            for t in range(TT):
                last = project(b[:, t * 8:t * 8 + 8], wr, t, 0, 8)
            last.then_inc(V.filled, 1)
            experts(N_E2 * NFC, moe2_use, "moe2")

        @block.scalar
        def _(act):
            own = Own(act, act_own)

            def f(o, i, func, bias=0.0, scale=1.0, **k):
                return nc.scalar.activation(o, i, func, bias=bias, scale=scale, **k)

            def root(name, o, i):
                act.wait_ge(meansq, ROOTS.index(name) + 1)
                f(o, i, ACT.Sqrt).then_inc(rooted, 1)

            def empty(n, *moves):
                b = S_.take(act, n)
                for o, pick, scale in moves:
                    last = f(o, pick(b), ACT.Copy, scale=scale)
                last.then_inc(S_.emptied, 1)

            whole = lambda b: b[:, :]

            root("ln1", st[:, 4:6], st[:, 2:4])
            for j in range(2):
                empty(S_.at["gl_qk"] + j, (qkT[:, 2 * j:2 * j + 2, :].rearrange("p a b -> p (a b)"), whole,
                                           0.125 if j == 0 else 1.0))
            for t in range(TT):
                empty(S_.at["gl_v"] + t, (Vg[:, t, :], whole, 1.0))
            empty(S_.at["gl_g"], (glT[:, :], lambda b: b[0:32, 0:T], 1.0))
            for t in range(TT):
                b = S_.take(act, S_.at["gl_og"] + t)
                f(ogs[:, t, :], b[:, :], ACT.Silu).then_inc(S_.emptied, 1)
            for d in range(DIRS):
                V.landed(act, V.at["gl_z"] + d)
                own(f(ge[:, d, :], gz[:, d, :], ACT.Abs))
                own.settle()
                own(f(ge[:, d, :], ge[:, d, :], ACT.Exp, scale=-1.0))
                own.settle()
                f(ge[:, d, :], ge[:, d, :], ACT.Ln, bias=1.0).then_inc(gl_val, 1)
            for d in range(DIRS):
                end = 0 if d else CH - 1
                cend = gc[:, :, :].rearrange("p k (c s) -> p (k c) s", s=CH)[:, :, end]
                flat = gc[:, :, :].rearrange("p a b -> p (a b)")
                act.wait_ge(gl_arg, d + 1)
                f(gP[:, 0, :], flat, ACT.Exp, scale=1 / 16)
                f(gP[:, 1, :], flat, ACT.Exp, scale=-1 / 16)
                f(gP[:, 2, :], gce[:, :, :].rearrange("p a b -> p (a b)"), ACT.Exp, scale=1 / 16)
                f(gPc[:, :], cend, ACT.Exp, scale=1 / 16).then_inc(gl_val, 1)
                b = S_.take(act, S_.at[f"gl{d}_kt"])
                f(gKt[:, :, :].rearrange("p a b -> p (a b)"), b[:, :], ACT.Copy).then_inc(S_.emptied, 1)
            root("gla", st[:, 24:32], st[:, 16:24])

            act.wait_ge(shifted, 8)
            f(pT[:, 12, :], pT[:, 12, :], ACT.Tanh).then_inc(lora_act, 1)
            f(pT[:, 14, :], pT[:, 14, :], ACT.Sigmoid).then_inc(lora_act, 1)
            for t in range(TT):
                empty(S_.at["vt"] + t, (Vt[:, t, :], whole, 1.0))
            root("kk", sca[:, 2, :], sca[:, 2, :])
            for d in range(DIRS):
                for i, name in enumerate(("w0", "a0")):
                    for j in range(2):
                        b = S_.take(act, S_.at[f"rw{d}_lora"] + 2 * i + j)
                        for k in range(2):
                            c = 2 * j + k
                            last = f(sca[:, i, c * T:c * T + T], b[:, k * T:k * T + T], ACT.Sigmoid,
                                     bias=pcol(name, 4 * d + c))
                        last.then_inc(S_.emptied, 1)
                act.wait_ge(cum, d + 1)
                end = 0 if d else CH - 1
                c4 = sca[:, 2, :].rearrange("p (k t c) -> p k t c", k=4, t=TT)
                f(AR[:, :, :, 0, :], BK[:, 1, :, :].rearrange("p k (t c) -> p k t c", t=TT), ACT.Exp, scale=-EXPM)
                f(AR[:, :, :, 1, :], c4, ACT.Exp, scale=-EXPM)
                f(BK[:, 0, :, :].rearrange("p a b -> p (a b)"), sca[:, 2, :], ACT.Exp, scale=EXPM)
                f(BKh[:, 0, :, :], BKh[:, 1, :, :], ACT.Exp, scale=-EXPM)
                f(Pc[:, :], sca[:, 2, :].rearrange("p (k s) -> p k s", s=CH)[:, :, end], ACT.Exp,
                  scale=-EXPM).then_inc(cum_exp, 1)
                for t in range(TT):
                    s = S_.at[f"rw{d}_t{t}"]
                    by_head = lambda b: b[:, :].rearrange("p (h c) -> p h c", h=NH)
                    empty(s, (AM[:, :, 0:64], by_head, 1.0))
                    empty(s + 1, (BKt[:, 0, :], whole, 1.0))
                    empty(s + 2, (BKt[:, 1, :], whole, 1.0))
                    empty(s + 3, (AM[:, :, 64:128], by_head, 1.0))
                    for g in range(2):
                        empty(s + 4 + g, (TAM[:, 4 * g:4 * g + 4, :].rearrange("p a b -> p (a b)"), whole, -1.0))
                    for c in range(2):
                        empty(s + 6 + c, (Hc[:, 2 * t + c].rearrange("p a b -> p (a b)"), lambda b: b[:, 0:256], 1.0))
            root("gn", st[:, 64:80], st[:, 48:64])

            def gates(base, n):
                for h in range(4):
                    act.wait_ge(V.filled, n + h + 1)
                    act.wait_ge(V.emptied, n + h - 1)
                    b = V.bank(base + h)
                    f(sg[:, h % 2, :], b[:, 0:T], ACT.Silu).then_inc(silu_done, 1)

            root("ln2", st[:, 4:6], st[:, 2:4])
            act.wait_ge(logit_max, 1)
            for t in range(TT):
                f(lg[:, t, 0:4], lg[:, t, 0:4], ACT.Exp, bias=st[:, 10 + t:11 + t], accum_out=st[:, 12 + t:13 + t])
                f(wexp[:, t, :], lm[:, t, :], ACT.Exp, bias=st[:, 14 + t:15 + t])
                f(st[:, 18 + t:19 + t], top[:, t, 1:2], ACT.Exp, bias=st[:, 14 + t:15 + t]).then_inc(logit_exp, 1)
            with act.Fori(0, N_E1) as i:
                gates(V.at["moe1"], V.at["moe1"] + 4 * i)
            root("lnf", st[:, 4:6], st[:, 2:4])

            root("att", st[:, 4:6], st[:, 2:4])
            for j in range(4):
                empty(S_.at["sqk"] + j, (sqkT[:, 2 * j:2 * j + 2, :].rearrange("p a b -> p (a b)"), whole,
                                         0.125 if j < 2 else 1.0))
            for t in range(TT):
                empty(S_.at["sv"] + t, (sV[:, t, :], whole, 1.0))
            for t in range(TT):
                empty(S_.at["lat"] + t, (lat[:, t, :], lambda b: b[:, 0:416], 1.0))
            root("lat", st[:, 20:24], st[:, 16:20])
            root("heads", stt[:, 4:8, :], stt[:, 0:4, :])
            for i, o in enumerate((qhT, khT)):
                for j in range(4):
                    empty(S_.at["headsT"] + 4 * i + j, (o[:, 2 * j:2 * j + 2, :].rearrange("p a b -> p (a b)"),
                                                        lambda b: b[0:MQK, :], 1.0))
            for h in range(NH):
                act.wait_ge(z_ready, h + 1)
                own(f(za[:, 1, :], za[:, 0, :], ACT.Abs))
                own.settle()
                own(f(za[:, 1, :], za[:, 1, :], ACT.Exp, scale=-1.0))
                own.settle()
                f(za[:, 1, :], za[:, 1, :], ACT.Ln, bias=1.0).then_inc(z_soft, 1)
                act.wait_ge(w_arg, h + 1)
                f(za[:, 2, :], za[:, 2, :], ACT.Exp).then_inc(w_exp, 1)
                if h % 2:
                    empty(S_.at[f"st{h // 2}"], (hT[:, h // 2, :], lambda b: b[:, 0:T], 1.0))
            for h in range(NH):
                act.wait_ge(maxed, h + 1)
                for q in range(2):
                    last = f(za[:, 0, q * T:q * T + T], za[:, 1, q * T:q * T + T], ACT.Exp,
                             bias=st[:, 24 + q:25 + q], scale=MQK ** -0.5, accum_out=st[:, 26 + q:27 + q])
                last.then_inc(p_exp, 1)
                s = S_.at[f"ml{h // 2}"]
                empty(s + h % 2, (pTt[:, h % 2, :], lambda b: b[:, 0:3 * P], 1.0))
                if h % 2:
                    empty(s + 2, (hT[:, 4 + h // 2, :], lambda b: b[:, 0:T], 1.0))

            root("dffn", st[:, 4:6], st[:, 2:4])
            for u in range(NFC):
                gates(V.at["ffn"], V.at["ffn"] + 4 * u)
            root("ssm", st[:, 4:6], st[:, 2:4])
            p16 = lambda i: par16[:, i, :]
            f(p16(0), pcol("ldt", 0, 16), ACT.Exp).then_inc(s5_val, 1)
            act.wait_ge(s5_arg, 1)
            f(p16(3), p16(2), ACT.Exp)
            f(p16(5), p16(4), ACT.Sin)
            f(p16(7), p16(6), ACT.Sin).then_inc(s5_val, 1)
            act.wait_ge(y_sum, 1)
            f(yT[:, :, :], yT[:, :, :], ACT.Gelu_apprx_tanh).then_inc(y_gelu, 1)
            for t in range(TT):
                for c in range(2):
                    n = 2 * t + c
                    b = S_.take(act, S_.at["glu"] + n)
                    if n:
                        V.landed(act, V.at["glu"] + n - 1)
                    f(gsig, b[:, :], ACT.Sigmoid).then_inc(S_.emptied, 1)
            root("moe", st[:, 4:6], st[:, 2:4])
            act.wait_ge(logit_max, 2)
            for t in range(TT):
                f(wexp[:, t, 0:8], lm[:, t, 0:8], ACT.Exp, bias=st[:, 14 + t:15 + t])
                f(st[:, 18 + t:19 + t], top[:, t, 1:2], ACT.Exp, bias=st[:, 14 + t:15 + t]).then_inc(logit_exp, 1)
            with act.Fori(0, N_E2 * NFC) as i:
                gates(V.at["moe2"], V.at["moe2"] + 4 * i)

        @block.vector
        def _(dve):
            own = Own(dve, dve_own)
            vec = nc.vector

            def tt(o, x, y, op):
                return vec.tensor_tensor(o, x, y, op)

            def ts(o, x, s1, op0, s2=None, op1=None):
                return vec.tensor_scalar(o, x, s1, s2, op0, op1) if op1 is not None else \
                    vec.tensor_scalar(o, x, s1, None, op0)

            def stt_(o, x, s, y, op0, op1):
                return vec.scalar_tensor_tensor(out=o, in0=x, scalar=s, in1=y, op0=op0, op1=op1)

            def do(ins):
                own(ins)
                own.settle()

            def signal(ins, s, value):
                ins.then_inc(s, 1)
                dve.wait_ge(s, value)

            def flat(x):
                return x.rearrange("p a b -> p (a b)")

            def spread(col, n):
                return col.unsqueeze(2).to_broadcast([col.shape[0], col.shape[1], n])

            def tiled(x, n):
                return x.unsqueeze(1).to_broadcast([x.shape[0], n, x.shape[1]])

            def rooted_(name):
                dve.wait_ge(rooted, ROOTS.index(name) + 1)

            def mean_square(name, i, o, n, eps):
                signal(ts(o, i, 1.0 / n, ALU.mult, eps, ALU.add), meansq, ROOTS.index(name) + 1)

            def norm(name, dst=None):
                own.settle()
                for t in range(TT):
                    own(vec.tensor_tensor_reduce(out=xn[:, t, :], in0=x_sb[:, t, :], in1=x_sb[:, t, :], scale=1.0,
                                                 scalar=0.0, op0=ALU.mult, op1=ALU.add, accum_out=st[:, t:t + 1]))
                own.settle()
                mean_square(name, st[:, 0:2], st[:, 2:4], D, EPS)
                rooted_(name)
                do(vec.reciprocal(st[:, 6:8], st[:, 4:6]))
                for t in range(TT):
                    ins = ts((dst or xn)[:, t, :], x_sb[:, t, :], st[:, 6 + t:7 + t], ALU.mult)
                    if t == 0 or dst is not None:
                        own(ins)
                if dst is None:
                    ins.then_inc(normed, 1)
                own.settle()

            def turned(n, gain=None):
                for j in range(4):
                    b = V.take(dve, n + j)
                    for k in range(2):
                        c = 2 * j + k
                        if gain:
                            last = ts(hT[:, c, :], b[:, k * T:k * T + T], pcol(gain, c), ALU.mult)
                        else:
                            last = vec.tensor_copy(hT[:, c, :], b[:, k * T:k * T + T])
                    last.then_inc(V.emptied, 1)

            def add_out(n):
                for c in range(2):
                    for t in range(TT):
                        b = V.take(dve, n + 2 * c + t)
                        o = x_sb[:, t, c * 512:c * 512 + 512]
                        tt(o, b[:, :], o, ALU.add).then_inc(V.emptied, 1)
                V.landed(dve, n + 3)

            dve.wait_ge(x_in, 16)
            norm("ln1")
            dve.wait_ge(misc_in, 64)
            turned(V.at["ln1"], "ln1")

            for d in range(DIRS):
                b = V.take(dve, V.at["gl_z"] + d)
                for k in range(2):
                    last = ts(gz[:, d, k * T:k * T + T], b[:, k * T:k * T + T], pcol("gb", 2 * d + k), ALU.add)
                last.then_inc(V.emptied, 1)
            for d in range(DIRS):
                V.landed(dve, V.at["gl_z"] + d)
                dve.wait_ge(gl_val, d + 1)
                do(stt_(gz[:, d, :], gz[:, d, :], 0.0, ge[:, d, :], ALU.min, ALU.subtract))
            for d in range(DIRS):
                order = list(range(NCH))[::1 - 2 * d]
                way = slice(None, None, -1) if d else slice(None)
                end = 0 if d else CH - 1
                for k in range(2):
                    own(vec.tensor_tensor_scan(gc[:, k, way], cst("reset", d, T)[:, way],
                                               gz[:, d, k * T:k * T + T][:, way], 0.0, ALU.mult, ALU.add))
                own.settle()
                by_chunk = gc[:, :, :].rearrange("p k (c s) -> p (k c) s", s=CH)
                tt(gce[:, :, :].rearrange("p k (c s) -> p (k c) s", s=CH), spread(by_chunk[:, :, end], CH), by_chunk,
                   ALU.subtract).then_inc(gl_arg, 1)
                S_.landed(dve, S_.at["gl_qk"] + 1)
                dve.wait_ge(gl_val, DIRS + d + 1)
                own(tt(flat(gR[:, :, :]), gP[:, 0, :], flat(qkT[:, 0:2, :]), ALU.mult))
                own(tt(flat(gK[:, :, :]), gP[:, 1, :], flat(qkT[:, 2:4, :]), ALU.mult))
                own.settle()
                tt(flat(gKh[:, :, :]), gP[:, 2, :], flat(qkT[:, 2:4, :]), ALU.mult).then_inc(gl_ops, 1)
                for e in range(2):
                    b = V.take(dve, V.at[f"gl{d}_q"] + e)
                    for t in range(TT):
                        last = tt(gQ[:, t, e:4:2, :], b[:, t * 256:t * 256 + 256].rearrange("p (h c) -> p h c", h=2),
                                  tiled(cst("mask2", 2 * d + 1, P), 2), ALU.mult)
                    last.then_inc(V.emptied, 1)
                for c in range(2):
                    b = V.take(dve, V.at[f"gl{d}_h"] + c)
                    vec.tensor_copy(gH[:, c:4:2].rearrange("p a b c -> p a (b c)"),
                                    b[:, :].rearrange("p (a b) -> p a b", a=2)).then_inc(V.emptied, 1)
                V.landed(dve, V.at[f"gl{d}_h"] + 1)
                do(vec.tensor_copy(gS[:, order[1]], gH[:, order[0]]))
                for i in (1, 2):
                    for k in range(2):
                        c = order[i]
                        ins = stt_(gS[:, order[i + 1], k, :], gS[:, c, k, :], gPc[:, k * NCH + c:k * NCH + c + 1],
                                   gH[:, c, k, :], ALU.mult, ALU.add)
                        if (i, k) == (2, 1):
                            ins.then_inc(gl_ops, 1)
                        else:
                            own(ins)
                    if i == 1:
                        own.settle()
                own.settle()
                for e in range(2):
                    b = V.take(dve, V.at[f"gl{d}_y"] + e)
                    o = Yg[:, :, :].rearrange("p t (k e c) -> p t k e c", k=2, e=2)[:, :, :, e, :]
                    x = b[:, :].rearrange("p (t k c) -> p t k c", t=TT, k=2)
                    if d:
                        tt(o, x, o, ALU.add).then_inc(V.emptied, 1)
                    else:
                        vec.tensor_copy(o, x).then_inc(V.emptied, 1)
                V.landed(dve, V.at[f"gl{d}_y"] + 1)
            do(tt(Yq[:, :, :], Yg[:, :, :], Yg[:, :, :], ALU.mult))
            do(vec.tensor_reduce(st[:, 8:16], Yq[:, :, :].rearrange("p t (h c) -> p (t h) c", h=4), AXX, ALU.add))
            mean_square("gla", st[:, 8:16], st[:, 16:24], P, EPS)
            rooted_("gla")
            do(vec.reciprocal(st[:, 32:40], st[:, 24:32]))
            do(tt(Yg[:, :, :].rearrange("p t (h c) -> p (t h) c", h=4),
                  Yg[:, :, :].rearrange("p t (h c) -> p (t h) c", h=4), spread(st[:, 32:40], P), ALU.mult))
            do(tt(Yg[:, :, :], Yg[:, :, :], tiled(row("gnorm"), TT), ALU.mult))
            S_.landed(dve, S_.at["gl_og"] + 1)
            signal(tt(xn[:, :, W:D], Yg[:, :, :], ogs[:, :, :], ALU.mult), mixed, 1)

            raw = sca[:, 0, 0:2 * (T + 2)].rearrange("p (a b) -> p a b", a=2)
            both = sca[:, 1, 0:2 * T].rearrange("p (a b) -> p a b", a=2)
            do(vec.memset(raw[:, :, :], 0.0))
            own(ts(mus[:, 0, :], pcol("mu", 0, 15), -1.0, ALU.mult, 1.0, ALU.add))
            do(ts(mus[:, 1, :], pcol("mu", 0, 15), 0.5, ALU.mult))
            do(ts(omka[:, :], pcol("k_a", 0, 4), -1.0, ALU.mult, 1.0, ALU.add))
            for j in range(8):
                m = 2 if j < 7 else 1
                b = V.take(dve, V.at["rw_p"] + j)
                vec.tensor_copy(raw[:, 0:m, 1:T + 1],
                                b[:, 0:m * T].rearrange("p (a b) -> p a b", a=m)).then_inc(V.emptied, 1)
                V.landed(dve, V.at["rw_p"] + j)
                own(tt(both[:, 0:m, :], raw[:, 0:m, 0:T], raw[:, 0:m, 2:T + 2], ALU.add))
                for k in range(m):
                    c = 2 * j + k
                    own(ts(pT[:, c, :], raw[:, k, 1:T + 1], mus[:, 0, c:c + 1], ALU.mult))
                own.settle()
                for k in range(m):
                    c = 2 * j + k
                    ins = stt_(pT[:, c, :], both[:, k, :], mus[:, 1, c:c + 1], pT[:, c, :], ALU.mult, ALU.add)
                    if k < m - 1:
                        own(ins)
                signal(ins, shifted, j + 1)
                own.settle()
            for k in range(4):
                own(ts(kk[:, k, :], pT[:, 4 + k, :], pcol("k_k", k), ALU.mult))
            own.settle()
            tt(kds, kk[:, :, :], kk[:, :, :], ALU.mult).then_inc(kk_sq, 1)
            for j in range(2):
                b = V.take(dve, V.at["kk"] + j)
                ts(sca[:, 2, j * 512:j * 512 + 512], b[:, :], 1e-24, ALU.max).then_inc(V.emptied, 1)
                V.landed(dve, V.at["kk"] + j)
            signal(vec.memset(st[:, 93:94], 0.0), meansq, ROOTS.index("kk") + 1)
            rooted_("kk")
            do(vec.reciprocal(sca[:, 2, :], sca[:, 2, :]))
            do(tt(flat(kk[:, :, :]), flat(kk[:, :, :]), sca[:, 2, :], ALU.mult))

            for d in range(DIRS):
                order = list(range(NCH))[::1 - 2 * d]
                way = slice(None, None, -1) if d else slice(None)
                end = 0 if d else CH - 1
                S_.landed(dve, S_.at[f"rw{d}_lora"] + 3)
                for k in range(4):
                    c = slice(k * T, k * T + T)
                    own(vec.tensor_tensor_scan(sca[:, 2, c][:, way], cst("reset", d, T)[:, way],
                                               sca[:, 0, c][:, way], 0.0, ALU.mult, ALU.add))
                own.settle()
                own(tt(flat(BK[:, 1]), sca[:, 2, :], sca[:, 0, :], ALU.subtract))
                own.settle()
                by_chunk = sca[:, 2, :].rearrange("p (k s) -> p k s", s=CH)
                signal(tt(flat(BKh[:, 1]).rearrange("p (k s) -> p k s", s=CH), spread(by_chunk[:, :, end], CH),
                          by_chunk, ALU.subtract), cum, d + 1)
                for k in range(4):
                    c = slice(k * T, k * T + T)
                    own(ts(sca[:, 0, c], sca[:, 1, c], pcol("k_a", k), ALU.mult, omka[:, k:k + 1], ALU.add))
                own.settle()
                own(tt(sca[:, 0, :], sca[:, 0, :], flat(pT[:, 4:8, :]), ALU.mult))
                do(tt(sca[:, 1, :], sca[:, 1, :], flat(kk[:, :, :]), ALU.mult))
                if d:
                    do(tt(flat(kds), flat(kds), sca[:, 0, :], ALU.add))
                else:
                    do(vec.tensor_copy(flat(kds), sca[:, 0, :]))
                dve.wait_ge(cum_exp, d + 1)
                kk4 = kk[:, :, :].rearrange("p k (t c) -> p k t c", t=TT)
                r4 = pT[:, 0:4, :].rearrange("p k (t c) -> p k t c", t=TT)
                own(tt(AR[:, :, :, 0, :], AR[:, :, :, 0, :], kk4, ALU.mult))
                own(tt(AR[:, :, :, 1, :], AR[:, :, :, 1, :], r4, ALU.mult))
                own(tt(flat(BK[:, 1]), flat(BK[:, 0]), sca[:, 0, :], ALU.mult))
                own(tt(flat(BKh[:, 1]), flat(BKh[:, 0]), sca[:, 0, :], ALU.mult))
                own.settle()
                own(tt(flat(BK[:, 0]), flat(BK[:, 0]), sca[:, 1, :], ALU.mult))
                signal(tt(flat(BKh[:, 0]), flat(BKh[:, 0]), sca[:, 1, :], ALU.mult), rw_ops, d + 1)
                own.settle()
                lev, levt = (("levb", "levf") if d else ("levf", "levb"))
                for t in range(TT):
                    v = V.at[f"rw{d}_t{t}"]
                    for i, dst in enumerate((LN, MQ)):
                        for j in range(4):
                            b = V.take(dve, v + 4 * i + j)
                            h = 4 * (j % 2) + j // 2
                            tt(dst[:, h:h + 3:2].rearrange("p h a b -> p h (a b)"),
                               b[:, :].rearrange("p (h c) -> p h c", h=2),
                               tiled(cst("mask2", d, 2 * P), 2), ALU.mult).then_inc(V.emptied, 1)
                    for g in range(2):
                        b = V.take(dve, v + 8 + g)
                        tt(L1[:, g:NH:2, :], b[:, :].rearrange("p (h c) -> p h c", h=4),
                           tiled(cst("mask2", 2 * (1 - d), P), 4), ALU.mult).then_inc(V.emptied, 1)
                    V.landed(dve, v + 9)
                    own(tt(X, L1[:, :, :], tiled(cst(lev, 0, P), NH), ALU.mult))
                    own(tt(XT, LN[:, :, 0, :], tiled(cst(levt, 0, P), NH), ALU.mult))
                    own.settle()
                    own(tt(X, tiled(ident, NH), X, ALU.subtract))
                    own.settle()
                    signal(tt(XT, tiled(ident, NH), XT, ALU.subtract), inv_start, 2 * d + t + 1)
                    n = v + 10
                    for l in range(2, NLEV + 1):
                        for g in range(2):
                            b = V.take(dve, n)
                            tt(WM[:, 4 * g:4 * g + 4, :], b[:, :].rearrange("p (h c) -> p h c", h=4),
                               tiled(cst(lev, l - 1, P), 4), ALU.mult).then_inc(V.emptied, 1)
                            n += 1
                        for g in range(2):
                            for dst in ((X, XT) if l < NLEV else (XT,)):
                                b = V.take(dve, n)
                                o = dst[:, 4 * g:4 * g + 4, :]
                                V.landed(dve, n - 1)
                                tt(o, o, b[:, :].rearrange("p (h c) -> p h c", h=4),
                                   ALU.subtract).then_inc(V.emptied, 1)
                                n += 1
                    b = V.take(dve, n)
                    tt(Rf[:, t], b[:, :].rearrange("p (k c) -> p k c", k=4), AR[:, :, t, 1, :],
                       ALU.add).then_inc(V.emptied, 1)
                    for c in range(2):
                        b = V.take(dve, n + 1 + c)
                        for k in range(4):
                            g = 2 * t + c
                            last = stt_(GT[:, g, k, :], cst("eye2"), Pc[:, k * NCH + g:k * NCH + g + 1],
                                        b[:, k * 64:k * 64 + 64], ALU.mult, ALU.add)
                        last.then_inc(V.emptied, 1)
                    n += 1
                    b = V.take(dve, n + 2)
                    if d:
                        tt(Yr[:, t, :], b[:, :], Yr[:, t, :], ALU.add).then_inc(V.emptied, 1)
                    else:
                        vec.tensor_copy(Yr[:, t, :], b[:, :]).then_inc(V.emptied, 1)
                    V.landed(dve, n + 2)
                S_.landed(dve, S_.at[f"rw{d}_t1"] + 7)
                for i in range(2):
                    b = V.take(dve, V.at[f"rw{d}_s"] + i)
                    tt(S[:, order[i + 2]].rearrange("p a b -> p (a b)"), b[:, 0:256],
                       Hc[:, order[i + 1]].rearrange("p a b -> p (a b)"), ALU.add).then_inc(V.emptied, 1)
                for e in range(2):
                    b = V.take(dve, V.at[f"rw{d}_y"] + e)
                    for t in range(TT):
                        lo, hi = 0, P
                        if order[0] // 2 == t:
                            lo, hi = (0, 64) if order[0] % 2 else (64, P)
                        o = Yr[lo:hi, t, :].rearrange("p (k e c) -> p k e c", k=4, e=2)[:, :, e, :]
                        last = tt(o, b[lo:hi, t * 256:t * 256 + 256].rearrange("p (k c) -> p k c", k=4), o, ALU.add)
                    last.then_inc(V.emptied, 1)
                V.landed(dve, V.at[f"rw{d}_y"] + 1)
            for k in range(4):
                own(stt_(kds[:, k, :], pT[:, k, :], pcol("r_k", k), kds[:, k, :], ALU.mult, ALU.mult))
            own.settle()
            signal(vec.memset(st[:, 92:93], 0.0), kk_sq, 2)
            scr = BK[:, 0].rearrange("p a b -> p (a b)")
            heads = lambda x: x.rearrange("p t (h c) -> p t h c", h=NH)
            scr_h = scr.rearrange("p (t h c) -> p t h c", t=TT, h=NH)
            sp4 = lambda c: c.rearrange("p (t h) -> p t h", t=TT).unsqueeze(3).to_broadcast([P, TT, NH, HD])
            yh = heads(Yr)
            do(vec.tensor_reduce(st[:, 48:64], yh, AXX, ALU.add))
            do(ts(st[:, 48:64], st[:, 48:64], 1.0 / HD, ALU.mult))
            for t in range(TT):
                own(tt(yh[:, t], yh[:, t], spread(st[:, 48 + 8 * t:56 + 8 * t], HD), ALU.subtract))
            own.settle()
            do(tt(scr.rearrange("p (t c) -> p t c", t=TT), Yr, Yr, ALU.mult))
            do(vec.tensor_reduce(st[:, 48:64], scr_h, AXX, ALU.add))
            mean_square("gn", st[:, 48:64], st[:, 48:64], HD, GN_EPS)
            b = V.take(dve, V.at["bonus"])
            vec.tensor_copy(bon[:, :, :].rearrange("p a b -> p (a b)"), b[:, 0:TT * NH]).then_inc(V.emptied, 1)
            V.landed(dve, V.at["bonus"])
            rooted_("gn")
            do(vec.reciprocal(st[:, 48:64], st[:, 64:80]))
            for t in range(TT):
                own(tt(yh[:, t], yh[:, t], spread(st[:, 48 + 8 * t:56 + 8 * t], HD), ALU.mult))
                own(tt(scr_h[:, t], heads(Vt)[:, t], spread(bon[:, t, :], HD), ALU.mult))
            own.settle()
            do(tt(Yr, Yr, tiled(row("ln_w"), TT), ALU.mult))
            do(tt(Yr, Yr, tiled(row("ln_b"), TT), ALU.add))
            do(tt(Yr, Yr, scr.rearrange("p (t c) -> p t c", t=TT), ALU.add))
            for t in range(TT):
                b = V.take(dve, V.at["gate"] + t)
                tt(Yr[:, t, :], b[:, :], Yr[:, t, :], ALU.mult).then_inc(V.emptied, 1)
            V.landed(dve, V.at["gate"] + 1)
            signal(vec.memset(st[:, 92:93], 0.0), mixed, 2)
            turned(V.at["mixT"])
            add_out(V.at["wout"])

            norm("ln2")
            turned(V.at["ln2"], "ln2")

            def top_two(k, n, t, group):
                do(ts(wexp[:, t, 0:n], wexp[:, t, 0:n], st[:, 20 + t:21 + t], ALU.mult))
                do(stt_(wexp[:, t, 0:n], lm[:, t, 0:n], top[:, t, 1:2], wexp[:, t, 0:n], ALU.is_ge, ALU.mult))

            b = V.take(dve, V.at["route1"])
            tt(lg[:, :, :], b[:, 0:72].rearrange("p (t c) -> p t c", t=TT), tiled(row("rb"), TT),
               ALU.add).then_inc(V.emptied, 1)
            V.landed(dve, V.at["route1"])
            for t in range(TT):
                do(vec.tensor_reduce(st[:, 8 + t:9 + t], lg[:, t, 0:4], AXX, ALU.max))
                do(ts(st[:, 80:84], lg[:, t, 0:4], st[:, 8 + t:9 + t], ALU.is_ge))
                do(ts(st[:, 80:84], st[:, 80:84], 1e30, ALU.mult, -1e30, ALU.add))
                do(tt(lm[:, t, :].rearrange("p (g e) -> p g e", g=4), lg[:, t, 4:36].rearrange("p (g e) -> p g e", g=4),
                      spread(st[:, 80:84], 8), ALU.add))
                do(vec.max(top[:, t, :], lm[:, t, :]))
                do(ts(st[:, 14 + t:15 + t], top[:, t, 0:1], -1.0, ALU.mult))
            signal(ts(st[:, 10:12], st[:, 8:10], -1.0, ALU.mult), logit_max, 1)
            dve.wait_ge(logit_exp, 2)
            do(ts(st[:, 18:20], st[:, 18:20], 1.0, ALU.add))
            do(tt(st[:, 18:20], st[:, 18:20], st[:, 12:14], ALU.mult))
            do(vec.reciprocal(st[:, 20:22], st[:, 18:20]))
            for t in range(TT):
                top_two(0, 32, t, True)

            def unit(base, sbase, n, sn, silus, parity, weight):
                for f in range(4):
                    dve.wait_ge(V.filled, n + f + 1)
                    dve.wait_ge(silu_done, silus + f + 1)
                    b = V.bank(base + f)
                    tt(hact[:, parity, f, :], b[:, T:2 * T], sg[:, f % 2, :], ALU.mult).then_inc(V.emptied, 1)
                dve.wait_ge(S_.emptied, sn)
                for t in range(TT):
                    for c in range(2):
                        dve.wait_ge(S_.filled, sn + 2 * t + c + 1)
                        b = S_.bank(sbase + 2 * t + c)
                        o = x_sb[:, t, c * 512:c * 512 + 512]
                        stt_(o, b[:, :], weight(t), o, ALU.mult, ALU.add).then_inc(S_.emptied, 1)

            with dve.Fori(0, N_E1 // 2) as i:
                for s in range(2):
                    e = 2 * i + s
                    unit(V.at["moe1"], S_.at["moe1"], V.at["moe1"] + 4 * e, S_.at["moe1"] + 4 * e, 4 * e, s,
                         lambda t: wexp[:, t, bass.ds(e, 1)])
            dve.wait_ge(S_.emptied, S_.at["moe1"] + 4 * N_E1)
            norm("lnf", x_sb)
            signal(tt(x_sb[:, :, :], x_sb[:, :, :], tiled(row("lnf"), TT), ALU.mult), mixed, 3)

            norm("att")
            turned(V.at["att"], "att")
            S_.landed(dve, S_.at["lat"] + 1)
            for t in range(TT):
                for i, (lo, n) in enumerate(((0, 256), (256, 128))):
                    own(vec.tensor_tensor_reduce(out=sqr[:, lo:lo + n], in0=lat[:, t, lo:lo + n],
                                                 in1=lat[:, t, lo:lo + n], scale=1.0 / n, scalar=0.0, op0=ALU.mult,
                                                 op1=ALU.add, accum_out=st[:, 8 + 2 * t + i:9 + 2 * t + i]))
                own.settle()
            mean_square("lat", st[:, 8:12], st[:, 16:20], 1, EPS)
            rooted_("lat")
            do(vec.reciprocal(st[:, 20:24], st[:, 20:24]))
            for t in range(TT):
                for i, (lo, n) in enumerate(((0, 256), (256, 128))):
                    x = lat[:, t, lo:lo + n]
                    do(ts(x, x, st[:, 20 + 2 * t + i:21 + 2 * t + i], ALU.mult))
            vec.memset(st[:, 92:93], 0.0).then_inc(lat_ready, 1)
            dve.wait_ge(lat_ready, 1)
            for k in range(3):
                j = V.at["lat"] + k // 2
                b = V.take(dve, j)
                ins = ts(latT[:, k, :], b[:, (k % 2) * T:(k % 2) * T + T],
                         pcol("qlat", k) if k < 2 else pcol("kvlat"), ALU.mult)
                if k:
                    ins.then_inc(V.emptied, 1)
            for t in range(TT):
                for c in range(2):
                    b = V.take(dve, V.at["q_up"] + 2 * t + c)
                    vec.tensor_copy(qh[:, t, 4 * c:4 * c + 4, :],
                                    b[:, 0:384].rearrange("p (h c) -> p h c", h=4)).then_inc(V.emptied, 1)
            for t in range(TT):
                own(vec.tensor_copy(kh[:, t, :, MN:MQK], tiled(lat[:, t, 384:416], NH)))
                for c in range(2):
                    b = V.take(dve, V.at["kv_up"] + 2 * t + c)
                    x = b[:, :].rearrange("p (h c) -> p h c", h=4)
                    vec.tensor_copy(kh[:, t, 4 * c:4 * c + 4, 0:MN], x[:, :, 0:MN])
                    vec.tensor_copy(mV[:, t, 4 * c:4 * c + 4, :], x[:, :, MN:P]).then_inc(V.emptied, 1)
            own.settle()
            V.landed(dve, V.at["kv_up"] + 3)
            sqh = sqr[:, :].rearrange("p (h c) -> p h c", h=NH)
            for i, x in enumerate((qh, kh)):
                for t in range(TT):
                    do(tt(sqh, x[:, t], x[:, t], ALU.mult))
                    do(vec.tensor_reduce(stt[:, 2 * i + t, :], sqh, AXX, ALU.add))
            mean_square("heads", stt[:, 0:4, :], stt[:, 0:4, :], MQK, EPS)
            rooted_("heads")
            do(vec.reciprocal(stt[:, 0:4, :], stt[:, 4:8, :]))
            rope = cst("rope").rearrange("p (t s c) -> p t s c", t=TT, s=2)
            hf = MR // 2
            rpv = [rp[:, i, :].rearrange("p (h c) -> p h c", h=NH) for i in range(3)]
            for i, x in enumerate((qh, kh)):
                for t in range(TT):
                    do(tt(x[:, t], x[:, t], spread(stt[:, 2 * i + t, :], MQK), ALU.mult))
                    do(tt(x[:, t], x[:, t], tiled(row("kn" if i else "qn"), NH), ALU.mult))
                    r1, r2 = x[:, t, :, MN:MN + hf], x[:, t, :, MN + hf:MQK]
                    co, si = tiled(rope[:, t, 0, :], NH), tiled(rope[:, t, 1, :], NH)
                    own(tt(rpv[0], r1, si, ALU.mult))
                    own(tt(rpv[1], r2, si, ALU.mult))
                    own.settle()
                    own(tt(r1, r1, co, ALU.mult))
                    own(tt(r2, r2, co, ALU.mult))
                    own.settle()
                    own(tt(r1, r1, rpv[1], ALU.subtract))
                    do(tt(r2, r2, rpv[0], ALU.add))
            signal(vec.memset(st[:, 92:93], 0.0), heads_ready, 1)
            for h in range(NH):
                if h == 0:
                    V.landed(dve, V.at["kv_up"] + 3)
                n = V.at["stick"] + 2 * h
                b = V.take(dve, n)
                own(vec.tensor_copy(za[:, 0, :], b[:, :]))
                own.settle()
                vec.memset(st[:, 92:93], 0.0).then_inc(V.emptied, 1)
                signal(vec.memset(st[:, 91:92], 0.0), z_ready, h + 1)
                dve.wait_ge(z_soft, h + 1)
                z2 = za[:, 0, :].rearrange("p (a b) -> p a b", a=2)
                l2 = za[:, 1, :].rearrange("p (a b) -> p a b", a=2)
                do(stt_(lf[:, :, :], z2, 0.0, l2, ALU.max, ALU.add))
                own(tt(lf[:, 0, 0:P], lf[:, 0, 0:P], cst("before"), ALU.mult))
                own(vec.memset(lf[:, 1, 0:P], 0.0))
                own.settle()
                signal(tt(lf[:, 1, P:T], lf[:, 1, P:T], cst("before"), ALU.mult), fails, h + 1)
                do(stt_(za[:, 2, :], za[:, 0, :], 0.0, za[:, 1, :], ALU.min, ALU.subtract))
                b = V.take(dve, n + 1)
                tt(za[:, 2, :], za[:, 2, :], b[:, :], ALU.subtract).then_inc(V.emptied, 1)
                V.landed(dve, n + 1)
                signal(vec.memset(st[:, 91:92], 0.0), w_arg, h + 1)
                dve.wait_ge(w_exp, h + 1)
                if h % 2:
                    dve.wait_ge(w_read, h // 2 + 1)
                elif h:
                    dve.wait_ge(S_.filled, S_.at[f"st{h // 2 - 1}"] + 1)
                e2 = za[:, 2, :].rearrange("p (a b) -> p a b", a=2)
                own(tt(wT[:, 0, 0:P], e2[:, 0, 0:P], cst("before"), ALU.mult))
                own(vec.tensor_copy(wT[:, 0, P:T], e2[:, 0, P:T]))
                own(vec.memset(wT[:, 1, 0:P], 0.0))
                own.settle()
                signal(tt(wT[:, 1, P:T], e2[:, 1, P:T], cst("before"), ALU.mult), w_ready, h + 1)
            dve.wait_ge(S_.filled, S_.at["st3"] + 1)
            for h in range(NH):
                b = V.take(dve, V.at["mla"] + h)
                own(tt(za[:, 1, 0:P], b[:, 0:P], cst("causal"), ALU.add))
                own(ts(za[:, 1, P:T], b[:, P:T], 0.0, ALU.mult, -1e30, ALU.add))
                own(vec.tensor_copy(za[:, 1, T:T + P], b[:, T:T + P]))
                own.settle()
                tt(za[:, 1, T + P:2 * T], b[:, T + P:2 * T], cst("causal"), ALU.add).then_inc(V.emptied, 1)
                V.landed(dve, V.at["mla"] + h)
                do(vec.tensor_reduce(st[:, 22:24], za[:, 1, :].rearrange("p (a b) -> p a b", a=2), AXX, ALU.max))
                if h:
                    dve.wait_ge(S_.filled, S_.at[f"ml{(h - 1) // 2}"] + (h - 1) % 2 + 1)
                signal(ts(st[:, 24:26], st[:, 22:24], -(MQK ** -0.5), ALU.mult), maxed, h + 1)
                dve.wait_ge(p_exp, h + 1)
                do(vec.reciprocal(st[:, 28:30], st[:, 26:28]))
                own(ts(za[:, 0, 0:T], za[:, 0, 0:T], st[:, 28:29], ALU.mult))
                own.settle()
                signal(ts(za[:, 0, T:2 * T], za[:, 0, T:2 * T], st[:, 29:30], ALU.mult), p_ready, h + 1)
            add_out(V.at["wout2"])

            norm("dffn")
            turned(V.at["dffn"], "dffn")
            for u in range(NFC):
                unit(V.at["ffn"], S_.at["ffn"], V.at["ffn"] + 4 * u, S_.at["ffn"] + 4 * u, 4 * (N_E1 + u), u % 2,
                     lambda t: 1.0)
            dve.wait_ge(S_.emptied, S_.at["ffn"] + 4 * NFC)
            signal(vec.memset(st[:, 92:93], 0.0), mixed, 4)

            norm("ssm")
            turned(V.at["ssm"], "ssm")
            for j in range(2):
                b = V.take(dve, V.at["u"] + j)
                vec.tensor_copy(uT[:, 2 * j:2 * j + 2, :].rearrange("p a b -> p (a b)"), b[:, :]).then_inc(V.emptied, 1)
            V.landed(dve, V.at["u"] + 1)
            q = lambda i: par16[:, i, :]
            dve.wait_ge(s5_val, 1)
            do(ts(q(1), pcol("lre", 0, 16), -1e-4, ALU.min))
            do(tt(q(2), q(1), q(0), ALU.mult))
            do(tt(q(4), pcol("lim", 0, 16), q(0), ALU.mult))
            do(ts(q(6), q(4), float(np.pi / 2), ALU.add))
            magic = 12582912.0
            pi_hi = float(np.float32(6.28125))
            pi_lo = float(2 * np.pi - 6.28125)
            for i in (4, 6):
                do(ts(q(8), q(i), float(1 / (2 * np.pi)), ALU.mult, magic, ALU.add))
                do(ts(q(8), q(8), magic, ALU.subtract))
                do(stt_(q(i), q(8), -pi_hi, q(i), ALU.mult, ALU.add))
                do(stt_(q(i), q(8), -pi_lo, q(i), ALU.mult, ALU.add))
                do(ts(q(i), q(i), 3.1415925, ALU.min, -3.1415925, ALU.max))
            signal(vec.memset(st[:, 92:93], 0.0), s5_arg, 1)
            dve.wait_ge(s5_val, 2)
            im = pcol("lim", 0, 16)
            do(tt(q(9), q(3), q(7), ALU.mult))
            do(ts(q(9), q(9), -1.0, ALU.add))
            do(tt(q(10), q(3), q(5), ALU.mult))
            do(tt(q(11), q(1), q(1), ALU.mult))
            do(tt(q(8), im, im, ALU.mult))
            do(tt(q(11), q(11), q(8), ALU.add))
            do(vec.reciprocal(q(11), q(11)))
            do(tt(q(12), q(9), q(1), ALU.mult))
            do(tt(q(8), q(10), im, ALU.mult))
            do(tt(q(12), q(12), q(8), ALU.add))
            do(tt(q(12), q(12), q(11), ALU.mult))
            do(tt(q(13), q(10), q(1), ALU.mult))
            do(tt(q(8), q(9), im, ALU.mult))
            do(tt(q(13), q(13), q(8), ALU.subtract))
            do(tt(q(13), q(13), q(11), ALU.mult))
            dve.wait_ge(ssm_in, 32)
            cr, ci = spread(q(12), 32), spread(q(13), 32)
            t0 = vst[:, 0:2, :].rearrange("p a b -> p (a b)").rearrange("p (a b) -> p a b", a=16)
            t1 = vst[:, 2:4, :].rearrange("p a b -> p (a b)").rearrange("p (a b) -> p a b", a=16)
            own(tt(t0, cT[:, :, 0, :], ci, ALU.mult))
            own(tt(t1, cT[:, :, 1, :], ci, ALU.mult))
            own.settle()
            own(tt(cT[:, :, 0, :], cT[:, :, 0, :], cr, ALU.mult))
            own(tt(cT[:, :, 1, :], cT[:, :, 1, :], cr, ALU.mult))
            own.settle()
            own(tt(cT[:, :, 0, :], cT[:, :, 0, :], t1, ALU.subtract))
            do(tt(cT[:, :, 1, :], cT[:, :, 1, :], t0, ALU.add))
            do(ts(cT[:, :, 1, :], cT[:, :, 1, :], -1.0, ALU.mult))
            signal(vec.memset(st[:, 92:93], 0.0), s5_mat, 1)
            own(vec.memset(rot[:, 0, :, 0:1], 1.0))
            own(vec.memset(rot[:, 1, :, 0:1], 0.0))
            own.settle()
            do(vec.tensor_copy(q(14), q(7)))
            do(vec.tensor_copy(q(15), q(5)))
            n = 1
            while n < T:
                c, s = spread(q(14), n), spread(q(15), n)
                re, mi = rot[:, 0, :, 0:n], rot[:, 1, :, 0:n]
                ra, rb = rot[:, 0, :, n:2 * n], rot[:, 1, :, n:2 * n]
                own(tt(rtm[:, 0, :, 0:n], mi, s, ALU.mult))
                own(tt(rtm[:, 1, :, 0:n], mi, c, ALU.mult))
                own(tt(ra, re, c, ALU.mult))
                own(tt(rb, re, s, ALU.mult))
                own.settle()
                own(tt(ra, ra, rtm[:, 0, :, 0:n], ALU.subtract))
                own(tt(rb, rb, rtm[:, 1, :, 0:n], ALU.add))
                do(tt(q(16), q(15), q(15), ALU.mult))
                do(tt(q(15), q(15), q(14), ALU.mult))
                do(ts(q(15), q(15), 2.0, ALU.mult))
                do(tt(q(14), q(14), q(14), ALU.mult))
                do(tt(q(14), q(14), q(16), ALU.subtract))
                n *= 2
            for j in range(16):
                o = 32 * (j % 4)
                n = V.at["s5"] + 2 * j
                b = V.take(dve, n)
                co, si = rot[:, 0, j, :], rot[:, 1, j, :]
                v0, v1 = vst[:, 0, :], vst[:, 1, :]
                own(tt(v0, b[:, 0:T], co, ALU.mult))
                own(tt(vst[:, 2, :], b[:, T:2 * T], si, ALU.mult))
                own(tt(v1, b[:, T:2 * T], co, ALU.mult))
                own.settle()
                tt(vst[:, 3, :], b[:, 0:T], si, ALU.mult).then_inc(V.emptied, 1)
                V.landed(dve, n)
                own(tt(v0, v0, vst[:, 2, :], ALU.add))
                do(tt(v1, v1, vst[:, 3, :], ALU.subtract))
                dec = q(3)[:, j:j + 1].to_broadcast([P, T])
                own(vec.tensor_tensor_scan(vst[:, 2, :], dec, v0, 0.0, ALU.mult, ALU.add))
                do(vec.tensor_tensor_scan(vst[:, 3, :], dec, v1, 0.0, ALU.mult, ALU.add))
                g0, g1_ = vst[:, 2, :], vst[:, 3, :]
                if j:
                    V.landed(dve, n - 1)
                own(tt(hst[:, 0, :], g0, co, ALU.mult))
                own(tt(v0, g1_, si, ALU.mult))
                own(tt(hst[:, 1, :], g0, si, ALU.mult))
                own(tt(v1, g1_, co, ALU.mult))
                own.settle()
                own(tt(hst[:, 0, :], hst[:, 0, :], v0, ALU.subtract))
                own.settle()
                signal(tt(hst[:, 1, :], hst[:, 1, :], v1, ALU.add), s5_h, j + 1)
                b = V.take(dve, n + 1)
                stt_(yT[o:o + 32, j // 4, :], uT[o:o + 32, j // 4, :], pcol("sd", j // 4)[o:o + 32, :], b[o:o + 32, 0:T],
                     ALU.mult, ALU.add).then_inc(V.emptied, 1)
                V.landed(dve, n + 1)
            signal(vec.memset(st[:, 92:93], 0.0), y_sum, 1)
            for t in range(TT):
                for c in range(2):
                    n = 2 * t + c
                    b = V.take(dve, V.at["glu"] + n)
                    S_.landed(dve, S_.at["glu"] + n)
                    o = x_sb[:, t, c * 512:c * 512 + 512]
                    do(tt(gsig2, b[:, :], gsig, ALU.mult))
                    tt(o, o, gsig2, ALU.add).then_inc(V.emptied, 1)
                    V.landed(dve, V.at["glu"] + n)

            norm("moe")
            turned(V.at["moe"], "moe")
            b = V.take(dve, V.at["route2"])
            vec.tensor_copy(lm[:, :, 0:8], b[:, 0:16].rearrange("p (t c) -> p t c", t=TT)).then_inc(V.emptied, 1)
            V.landed(dve, V.at["route2"])
            for t in range(TT):
                do(vec.max(top[:, t, :], lm[:, t, 0:8]))
                do(ts(st[:, 14 + t:15 + t], top[:, t, 0:1], -1.0, ALU.mult))
            signal(vec.memset(st[:, 92:93], 0.0), logit_max, 2)
            dve.wait_ge(logit_exp, 4)
            do(ts(st[:, 18:20], st[:, 18:20], 1.0, ALU.add))
            do(vec.reciprocal(st[:, 20:22], st[:, 18:20]))
            for t in range(TT):
                top_two(0, 8, t, True)
            with dve.Fori(0, N_E2 * NFC // 2) as i:
                for s in range(2):
                    u = 2 * i + s
                    e = u // NFC
                    unit(V.at["moe2"], S_.at["moe2"], V.at["moe2"] + 4 * u, S_.at["moe2"] + 4 * u,
                         4 * (N_E1 + NFC) + 4 * u, s, lambda t: wexp[:, t, bass.ds(e, 1)])
            dve.wait_ge(S_.emptied, S_.at["moe2"] + 4 * N_E2 * NFC)
            vec.memset(st[:, 92:93], 0.0).then_inc(out_ready, 1)


_RAW = ["x", "w_in", "rw_g2", "w_out", "moe_w_gate", "moe_w_up", "moe_w_down", "att_w_in_2", "att_w_q_up_2",
        "att_w_kv_up_2", "att_w_out_2", "dffn_w_gate_2", "dffn_w_up_2", "dffn_w_down_2", "ssm_w_in_2",
        "ssm_w_glu_2", "moe_router_2", "moe_w_gate_2", "moe_w_up_2", "moe_w_down_2"]


def layout(x):
    col = lambda v: v.reshape(-1, P).T
    f = np.float32
    par = [x["ln1_w"], x["rw_mu"], x["rw_w0_f"], x["rw_w0_b"], x["rw_a0_f"], x["rw_a0_b"], x["rw_k_k"],
           x["rw_k_a"], x["rw_r_k"], x["gla_gb_f"], x["gla_gb_b"], x["ln2_w"], x["att_norm_2"],
           x["att_q_latent_norm_2"], x["att_kv_latent_norm_2"], x["dffn_norm_2"], x["ssm_norm_2"], x["moe_norm_2"],
           x["ssm_d_2"], x["ssm_a_re_2"], x["ssm_a_im_2"], np.broadcast_to(x["ssm_log_dt_2"][0][:, None], (32, 64))]
    rows = [x["rw_ln_w"], x["rw_ln_b"], x["gla_norm_w"], x["ln_f_w"], x["att_q_norm_2"], x["att_k_norm_2"],
            x["moe_b_coarse"], x["moe_b_fine"]]
    gw2 = np.zeros((32, 2, 256), f)
    gw2[0:16, 0] = x["gla_gw2_f"][0]
    gw2[16:32, 1] = x["gla_gw2_b"][0]
    bT = np.zeros((4, 2, 16, 4, 2, 2, 64), f)
    cT = np.zeros((2, 64, 16, 2, 2, 16), f)
    for r, (b, c) in enumerate((("ssm_b_re_2", "ssm_c_re_2"), ("ssm_b_im_2", "ssm_c_im_2"))):
        bb = x[b][0].reshape(4, 4, 2, 64, 16)
        cc = x[c][0].reshape(16, 2, 16, 64)
        for g in range(2):
            bT[:, g, :, :, r, g, :] = bb[:, :, g].transpose(1, 3, 0, 2)
            cT[g, :, :, r, g, :] = cc[:, g].transpose(2, 0, 1)
    return {
        "par": np.concatenate([col(v) for v in par], 1),
        "rows": np.concatenate([v.reshape(-1) for v in rows]),
        "con": np.concatenate(list(constants().values()), 1),
        "gw2": gw2,
        "w2": np.concatenate([x["rw_w2_f"][0], x["rw_w2_b"][0]], 0),
        "a2": np.concatenate([x["rw_a2_f"][0], x["rw_a2_b"][0]], 0),
        "wr1": np.concatenate([x["moe_w_coarse"][0], x["moe_w_fine"][0]], 1),
        "bT": bT.reshape(P, 4, 2, P),
        "cT": cT.reshape(P, 16, 2, 32),
    }


def kernel(**inputs):
    import concourse.bacc as _bacc
    from concourse.bass_utils import run_bass_kernel_spmd as _run

    x = {n: np.asarray(v) for n, v in inputs.items()}
    given = {n: x[n] for n in _RAW} | layout(x)
    nc = _bacc.Bacc("TRN2", target_bir_lowering=False, num_devices=1)
    arrays, aps = {}, {}
    for name, v in given.items():
        arrays[f"in_{name}"] = v = np.ascontiguousarray(v)
        aps[name] = nc.dram_tensor(f"in_{name}", v.shape, mybir.dt.from_np(v.dtype), kind="ExternalInput").ap()
    out = nc.dram_tensor("out", (1, T, D), F32, kind="ExternalOutput").ap()
    block_kernel(nc, aps, out)
    r = _run(nc, [arrays], core_ids=[0])
    return r.results[0]["out"]
```

```python
from contextlib import ExitStack

import numpy as np
import concourse.bass as bass
from concourse import mybir

F32 = mybir.dt.float32
ALU = mybir.AluOpType
ACT = mybir.ActivationFunctionType
AXX = mybir.AxisListType.X

P = 128
T = 256
TT = T // P
D = 1024
KT = D // P
CH = 64
NCH = T // CH
HD = 64
NH = 8
HP = NH // 2
NLEV = 6
DIRS = 2
W = NH * HD
EXPM = float(np.exp(np.float32(-0.5)))
EPS = 1e-6
GN_EPS = 64e-5

RW_COLS = 1920
GL_Q = RW_COLS
GL_V = GL_Q + 512
GL_GATE = GL_V + 512
GL_OG = GL_GATE + 32

AT_V = 1024
AT_CQ = 1536
AT_KR = AT_CQ + 256 + 128
MR, MN, MQK = 32, 64, 96

N_E1, F1 = 32, 512
N_E2, F2 = 8, 3584
FC = 512
NFC = F2 // FC
CAP = P

PAR = {}
_n = 0
for _name, _c in (("ln1", 8), ("mu", 15), ("w0", 8), ("a0", 8), ("k_k", 4), ("k_a", 4), ("r_k", 4), ("gb", 4),
                  ("ln2", 8), ("att", 8), ("qlat", 2), ("kvlat", 1), ("dffn", 8), ("ssm", 8), ("moe", 8),
                  ("sd", 4), ("lre", 16), ("lim", 16), ("ldt", 16)):
    PAR[_name] = (_n, _c)
    _n += _c
NPAR = _n
ROW = {}
_n = 0
for _name, _c in (("ln_w", 512), ("ln_b", 512), ("gnorm", 512), ("lnf", 1024), ("qn", 96), ("kn", 96),
                  ("rb", 36)):
    ROW[_name] = (_n, _c)
    _n += _c
NROW = _n


def constants():
    i = np.arange(P)
    r, c = i[:, None], i[None, :]
    same = (r // CH) == (c // CH)
    up = same & (r < c)
    dn = same & (r > c)
    eye = r == c
    k = {"ident": eye}
    k["mask2"] = np.concatenate([up, up | eye, dn, dn | eye], 1)
    lev = []
    for l in range(1, NLEV + 1):
        b = 2 ** l
        lev.append((r // b == c // b) & (r % b >= b // 2) & (c % b < b // 2))
    k["levf"] = np.concatenate(lev, 1)
    k["levb"] = np.concatenate([m.T for m in lev], 1)
    k["headones"] = (r // HD) == (c // HD)
    t = np.arange(T)
    k["reset"] = np.concatenate([np.tile(t % CH != 0, (P, 1)), np.tile(t % CH != CH - 1, (P, 1))], 1)
    k["iota"] = np.tile(np.arange(CAP), (P, 1))
    k["before"] = r < c
    k["after"] = r > c
    k["ones"] = np.ones((P, P))
    k["eye2"] = (r % HD) == i[None, :HD]
    k["causal"] = np.where(c <= r, 0.0, -1e30)
    half = MR // 2
    inv = np.float32(10000.0) ** (-np.arange(0, MR, 2, dtype=np.float32) / np.float32(MR))
    ang = np.arange(T, dtype=np.float32)[:, None] * inv[None, :]
    rope = np.stack([np.cos(ang), np.sin(ang)], 1).reshape(TT, P, 2 * half).transpose(1, 0, 2)
    k["rope"] = rope.reshape(P, TT * 2 * half)
    return {n: np.ascontiguousarray(a, np.float32) for n, a in k.items()}


CONST_COLS = {n: a.shape[1] for n, a in constants().items()}
C0 = {}
_n = 0
for _name, _c in CONST_COLS.items():
    C0[_name] = (_n, _c)
    _n += _c
NCONST = _n


class Ring:

    def __init__(self, banks, filled, emptied, stages):
        self.banks, self.filled, self.emptied = banks, filled, emptied
        self.at, n = {}, 0
        for name, count in stages:
            self.at[name] = n
            n += count
        self.total = n

    def bank(self, n):
        return self.banks[n % 4]

    def claim(self, pe, n):
        if n >= 4:
            pe.wait_ge(self.emptied, n - 3)
        return self.banks[n % 4]

    def take(self, eng, n):
        eng.wait_ge(self.filled, n + 1)
        return self.banks[n % 4]

    def landed(self, eng, n):
        eng.wait_ge(self.emptied, n + 1)


class Own:

    def __init__(self, eng, sem):
        self.eng, self.sem, self.n = eng, sem, 0

    def __call__(self, ins):
        ins.then_inc(self.sem, 1)
        self.n += 1
        return self.n

    def settle(self):
        if self.n:
            self.eng.wait_ge(self.sem, self.n)


def block_kernel(nc, a, out):
    ctx = ExitStack()
    with ctx:
        def sb(name, shape, dt=F32, stack=None):
            return (stack or ctx).enter_context(nc.sbuf_tensor(name, shape, dt))

        def sem(name):
            return ctx.enter_context(nc.semaphore(name))

        par = sb("par", [P, NPAR])
        rows = sb("rows", [P, NROW])
        con = sb("con", [P, NCONST])
        x_sb = sb("x_sb", [P, TT, D])
        xn = sb("xn", [P, TT, D])
        hT = sb("hT", [P, KT, T])
        st = sb("st", [P, 96])
        slot = [sb(f"slot{i}", [P, KT, FC]) for i in range(3)]

        def pcol(name, i=0, n=1):
            o = PAR[name][0] + i
            return par[:, o:o + n]

        def row(name):
            o, n = ROW[name]
            return rows[:, o:o + n]

        def cst(name, i=0, n=None):
            o, m = C0[name]
            n = m if n is None else n
            return con[:, o + i * n:o + i * n + n]

        ident = cst("ident")
        psum = [ctx.enter_context(nc.psum_tensor(f"ps{i}", [P, 512], F32)) for i in range(8)]

        gla = ExitStack()
        qkT = sb("qkT", [P, 4, T], stack=gla)
        Vg = sb("Vg", [P, TT, W], stack=gla)
        glT = sb("glT", [32, T], stack=gla)
        gw2 = sb("gw2", [32, DIRS, T], stack=gla)
        ogs = sb("ogs", [P, TT, W], stack=gla)
        gz = sb("gz", [P, DIRS, 2 * T], stack=gla)
        ge = sb("ge", [P, DIRS, 2 * T], stack=gla)
        gc = sb("gc", [P, 2, T], stack=gla)
        gce = sb("gce", [P, 2, T], stack=gla)
        gP = sb("gP", [P, 3, 2 * T], stack=gla)
        gPc = sb("gPc", [P, 2 * NCH], stack=gla)
        gR = sb("gR", [P, 2, T], stack=gla)
        gK = sb("gK", [P, 2, T], stack=gla)
        gKh = sb("gKh", [P, 2, T], stack=gla)
        gKt = sb("gKt", [P, TT, 2 * P], stack=gla)
        gQ = sb("gQ", [P, TT, 4, P], stack=gla)
        gH = sb("gH", [P, NCH, 2, P], stack=gla)
        gS = sb("gS", [P, NCH, 2, P], stack=gla)
        Yg = sb("Yg", [P, TT, W], stack=gla)
        Yq = sb("Yq", [P, TT, W], stack=gla)
        gla.close()

        rw = ExitStack()
        pT = sb("pT", [P, 15, T], stack=rw)
        kk = sb("kk", [P, 4, T], stack=rw)
        w2 = sb("w2", [P, W], stack=rw)
        a2 = sb("a2", [P, W], stack=rw)
        g2 = sb("g2", [P, W], stack=rw)
        omka = sb("omka", [P, 4], stack=rw)
        mus = sb("mus", [P, 2, 15], stack=rw)
        Vt = hT[:, 0:4, :].rearrange("p a b -> p (a b)").rearrange("p (t w) -> p t w", t=TT)
        kds = hT[:, 4:8, :]
        Yr = xn[:, :, 0:W]
        bon = sb("bon", [P, TT, NH], stack=rw)
        sca = sb("sca", [P, 3, 4 * T], stack=rw)
        Pc = sb("Pc", [P, 4 * NCH], stack=rw)
        AR = sb("AR", [P, 4, TT, 2, P], stack=rw)
        BK = sb("BK", [P, 2, 4, T], stack=rw)
        BKh = sb("BKh", [P, 2, 4, T], stack=rw)
        BKt = sb("BKt", [P, 2, W], stack=rw)
        AM = sb("AM", [P, NH, P], stack=rw)
        LN = sb("LN", [P, NH, 2, P], stack=rw)
        MQ = sb("MQ", [P, NH, 2, P], stack=rw)
        L1 = sb("L1", [P, NH, P], stack=rw)
        X = sca[:, 0, :].rearrange("p (h c) -> p h c", h=NH)
        XT = sca[:, 1, :].rearrange("p (h c) -> p h c", h=NH)
        WM = sca[:, 2, :].rearrange("p (h c) -> p h c", h=NH)
        TAM = L1
        Rf = sb("Rf", [P, TT, 4, P], stack=rw)
        GT = sb("GT", [P, NCH, 4, HD], stack=rw)
        Hc = sb("Hc", [P, NCH, 4, HD], stack=rw)
        S = sb("S", [P, NCH, 4, HD], stack=rw)
        rw.close()

        slot += [sb(f"slot{i}", [P, KT, FC]) for i in range(3, 6)]
        att = ExitStack()
        sqkT = sb("sqkT", [P, 8, T], stack=att)
        sV = sb("sV", [P, TT, W], stack=att)
        lat = sb("lat", [P, TT, 416], stack=att)
        latT = sb("latT", [P, 3, T], stack=att)
        wq_up = sb("wq_up", [P, 2, NH * MQK], stack=att)
        wkv_up = sb("wkv_up", [P, NH * P], stack=att)
        qh = xn[:, :, 0:NH * MQK].rearrange("p t (h c) -> p t h c", h=NH)
        kh = sb("kh", [P, TT, NH, MQK], stack=att)
        mV = sb("mV", [P, TT, NH, HD], stack=att)
        qhT = sb("qhT", [MQK, NH, T], stack=att)
        khT = sb("khT", [MQK, NH, T], stack=att)
        rp = sb("rp", [P, 3, NH * MR // 2], stack=att)
        sqr = sb("sqr", [P, NH * MQK], stack=att)
        stt = sb("stt", [P, 8, NH], stack=att)
        za = wq_up[:, :, :].rearrange("p a b -> p (a b)").rearrange("p (a b) -> p a b", a=3)
        lf = wkv_up[:, 0:2 * T].rearrange("p (a b) -> p a b", a=2)
        wT = wkv_up[:, 2 * T:4 * T].rearrange("p (a b) -> p a b", a=2)
        pTt = wkv_up[:, 0:6 * P].rearrange("p (a b) -> p a b", a=2)
        att.close()

        ssm = ExitStack()
        uT = sb("uT", [P, 4, T], stack=ssm)
        bT = sb("bT", [P, 4, 2, P], stack=ssm)
        cT = sb("cT", [P, 16, 2, 32], stack=ssm)
        par16 = sb("par16", [P, 24, 16], stack=ssm)
        pi16 = sb("pi16", [P, 16], mybir.dt.int32, stack=ssm)
        rot = sb("rot", [P, 2, 16, T], stack=ssm)
        rtm = sb("rtm", [P, 2, 16, T // 2], stack=ssm)
        yT = hT[:, 0:4, :]
        vst = xn[:, 0, :].rearrange("p (a b) -> p a b", a=4)
        hst = xn[:, 1, 0:2 * T].rearrange("p (a b) -> p a b", a=2)
        gsig = xn[:, 1, 512:1024]
        gsig2 = hT[:, 4:6, :].rearrange("p a b -> p (a b)")
        ssm.close()

        ffn = ExitStack()
        sg = sb("sg", [P, 2, T], stack=ffn)
        hact = sb("hact", [P, 2, 4, T], stack=ffn)
        wr = sb("wr", [P, KT, 48], stack=ffn)
        lg = sb("lg", [P, TT, 36], stack=ffn)
        lm = sb("lm", [P, TT, 32], stack=ffn)
        top = sb("top", [P, TT, 8], stack=ffn)
        wexp = sb("wexp", [P, TT, N_E1], stack=ffn)
        msk = sb("msk", [P, TT, N_E1], stack=ffn)
        rank = sb("rank", [P, TT, N_E1], stack=ffn)
        cnt = sb("cnt", [P, 2], stack=ffn)
        over = sb("over", [P, 1], mybir.dt.int32, stack=ffn)
        sel = sb("sel", [P, 2, TT, CAP], stack=ffn)
        selT = sb("selT", [CAP, T], stack=ffn)
        xgT = sb("xgT", [P, 2, KT, CAP], stack=ffn)
        sgx = sb("sgx", [CAP, FC], stack=ffn)
        hsb = sb("hsb", [CAP, FC], stack=ffn)
        hTs = sb("hTs", [P, 4, CAP], stack=ffn)
        yacc = sb("yacc", [CAP, D], stack=ffn)
        ffn.close()

        misc_in = sem("misc_in")
        x_in = sem("x_in")
        lora_in = sem("lora_in")
        up_in = sem("up_in")
        ssm_in = sem("ssm_in")
        router_in = sem("router_in")
        slot_in = [sem(f"slot_in{i}") for i in range(6)]
        v_filled, v_emptied = sem("v_filled"), sem("v_emptied")
        s_filled, s_emptied = sem("s_filled"), sem("s_emptied")
        dve_own, act_own = sem("dve_own"), sem("act_own")
        meansq = sem("meansq")
        rooted = sem("rooted")
        normed = sem("normed")
        gl_arg = sem("gl_arg")
        gl_val = sem("gl_val")
        gl_ops = sem("gl_ops")
        shifted = sem("shifted")
        lora_act = sem("lora_act")
        kk_sq = sem("kk_sq")
        cum = sem("cum")
        cum_exp = sem("cum_exp")
        rw_ops = sem("rw_ops")
        inv_start = sem("inv_start")
        mixed = sem("mixed")
        w_read = sem("w_read")
        lat_ready = sem("lat_ready")
        heads_ready = sem("heads_ready")
        z_ready = sem("z_ready")
        z_soft = sem("z_soft")
        fails = sem("fails")
        w_arg = sem("w_arg")
        w_exp = sem("w_exp")
        w_ready = sem("w_ready")
        maxed = sem("maxed")
        p_exp = sem("p_exp")
        p_ready = sem("p_ready")
        logit_max = sem("logit_max")
        logit_exp = sem("logit_exp")
        silu_done = sem("silu_done")
        ranked = sem("ranked")
        route_known = sem("route_known")
        gu_read = sem("gu_read")
        down_read = sem("down_read")
        s5_arg = sem("s5_arg")
        s5_val = sem("s5_val")
        s5_mat = sem("s5_mat")
        s5_h = sem("s5_h")
        y_sum = sem("y_sum")
        y_gelu = sem("y_gelu")
        glu_sig = sem("glu_sig")
        out_ready = sem("out_ready")
        out_done = sem("out_done")

        inv_items = 4 + 4 + 2 + (NLEV - 1) * 2 + (NLEV - 2) * 2 + (NLEV - 1) * 2 + 4
        V = Ring(psum[0:4], v_filled, v_emptied, [
            ("ln1", 4), ("gl_z", 2)]
            + [(f"gl{d}_{n}", c) for d in range(DIRS) for n, c in (("q", 2), ("h", 2), ("y", 2))]
            + [("rw_p", 8), ("kk", 2)]
            + [(f"rw{d}_{n}", c) for d in range(DIRS) for n, c in (("t0", inv_items), ("t1", inv_items), ("s", 2), ("y", 2))]
            + [("bonus", 1), ("gate", 2), ("mixT", 4), ("wout", 4), ("ln2", 4), ("route1", 1), ("rank1", 1),
               ("att", 4), ("lat", 2), ("q_up", 4), ("kv_up", 4), ("stick", 16), ("mla", 8), ("wout2", 4),
               ("dffn", 4), ("ffn", 4 * NFC), ("ssm", 4), ("u", 2), ("s5", 32), ("glu", 4),
               ("moe", 4), ("route2", 1), ("rank2", 1)])
        S_ = Ring(psum[4:8], s_filled, s_emptied, [
            ("gl_qk", 2), ("gl_v", 2), ("gl_g", 1), ("gl_og", 2), ("gl0_kt", 1), ("gl1_kt", 1),
            ("vt", 2)]
            + [(f"rw{d}_{n}", c) for d in range(DIRS) for n, c in (("lora", 4), ("t0", 8), ("t1", 8))]
            + [("sqk", 4), ("sv", 2), ("lat", 2), ("headsT", 8)]
            + [(f"st{h}", 1) for h in range(HP)]
            + [(f"ml{h}", c) for h in range(HP) for c in (3,)]
            + [("ffn", 4 * NFC), ("glu", 4)])

        class Experts:

            def __init__(self, name, count, nfc, done, used, last_s):
                self.name, self.count, self.nfc, self.done, self.used, self.last_s = \
                    name, count, nfc, done, used, last_s
                self.hid_filled, self.hid_emptied = sem(name + "_hid_filled"), sem(name + "_hid_emptied")
                self.out_filled, self.out_emptied = sem(name + "_out_filled"), sem(name + "_out_emptied")
                self.dense_silu = sem(name + "_dense_silu")
                self.x_filled, self.x_emptied = sem(name + "_x_filled"), sem(name + "_x_emptied")
                self.y_filled, self.y_emptied = sem(name + "_y_filled"), sem(name + "_y_emptied")
                self.z_filled, self.z_emptied = sem(name + "_z_filled"), sem(name + "_z_emptied")
                self.silu, self.sel_ready = sem(name + "_silu"), sem(name + "_sel_ready")
                full = self.items(False, False)
                self.len = len(full)
                self.first_len = self.len - 1
                self.back = {n: i - self.len for i, n in enumerate(full)}

            def items(self, first, last):
                out = []
                for c in range(self.nfc):
                    out += [f"gate{c}"] + [f"hT{c}"] * (not (first and c == 0)) + [f"up{c}"]
                    if c == self.nfc - 1 and not last:
                        out += ["ga", "gb"]
                    if c == min(1, self.nfc - 1):
                        out += ["selT"]
                return out

            def walk(self, eng, expert):
                expert(0, 0, 2, True, False)
                base = 2 + self.first_len
                with eng.Fori(0, self.count // 2 - 1) as i:
                    expert(i, 1, base + 2 * self.len * i, False, False)
                    expert(i, 2, base + 2 * self.len * i + self.len, False, False)
                i = self.count // 2 - 1
                expert(i, 1, base + 2 * self.len * i, False, True)
                return base + 2 * self.len * i + self.len - 2

            def phase(self, k, first):
                return 2 if first else (2 + self.first_len + (self.len if k == 2 else 0)) % 4


        loads, uses = {}, [0] * 6

        def use(name, i):
            uses[i] += 1
            loads[name] = (i, uses[i])

        for n, i in (("g0", 0), ("g1", 1), ("g2", 2), ("g3", 0), ("r0", 1), ("r1", 2), ("r2", 0), ("r3", 1),
                     ("o0", 2), ("o1", 0)):
            use(n, i)
        moe1_use = list(uses)
        uses = [u + N_E1 // 2 for u in uses]
        for n, i in (("a0", 0), ("a1", 1), ("a2", 2), ("a3", 3), ("p0", 4), ("p1", 5)):
            use(n, i)
        ffn_use = list(uses)
        for u in range(NFC):
            for j in range(3):
                use(f"f{u}_{j}", 3 * (u % 2) + j)
        for n, i in (("s0", 3), ("s1", 4), ("s2", 5)):
            use(n, i)
        moe2_use = list(uses)

        moe1 = Experts("moe1", N_E1, 1, 0, moe1_use, S_.at["rw1_t1"] + 7)
        moe2 = Experts("moe2", N_E2, NFC, N_E1 + NFC, moe2_use, S_.at["glu"] + 3)

        def either(eng, x, dense, gathered):
            eng.wait_ge(route_known, 1 if x is moe1 else 2)
            flag = eng.value_load(over[0:1, 0:1], min_val=0, max_val=1)
            with eng.If(flag > 0):
                dense(x)
            with eng.Else():
                gathered(x)

        def arrived(eng, name):
            i, n = loads[name]
            eng.wait_ge(slot_in[i], 16 * n)
            return slot[i]

        win = a["w_in"][0].rearrange("(t p) n -> p t n", p=P)
        ROOTS = ["ln1", "gla", "kk", "gn", "ln2", "lnf", "att", "lat", "heads", "dffn", "ssm", "moe"]
        NORMS = ["ln1", "ln2", "att", "dffn", "ssm", "moe"]
        block = ctx.enter_context(nc.Block())

        @block.sync
        def _(sp):
            def load(name, src, ring=None, item=None):
                if isinstance(ring, Ring):
                    sp.wait_ge(ring.filled, item + 1)
                elif ring is not None:
                    sp.wait_ge(ring, item)
                i, n = loads[name]
                sp.dma_start(slot[i][:, 0:src.shape[1], 0:src.shape[2]], src).then_inc(slot_in[i], 16)

            sp.dma_start(x_sb[:], a["x"][0].rearrange("(t p) d -> p t d", p=P)).then_inc(x_in, 16)
            sp.dma_start(par[:], a["par"]).then_inc(misc_in, 16)
            sp.dma_start(con[:], a["con"]).then_inc(misc_in, 16)
            load("g0", win[:, :, GL_Q:GL_Q + 512])
            load("g1", win[:, :, GL_V:GL_V + 512])
            load("g2", win[:, :, GL_GATE:GL_GATE + 32])
            sp.dma_start(rows[:], a["rows"].partition_broadcast(P)).then_inc(misc_in, 16)
            sp.dma_start(gw2[:], a["gw2"]).then_inc(misc_in, 16)
            load("g3", win[:, :, GL_OG:GL_OG + 512], S_, S_.at["gl_qk"] + 1)
            load("r0", win[:, :, 0:512], S_, S_.at["gl_v"] + 1)
            load("r1", win[:, :, 512:1024], S_, S_.at["gl_g"])
            load("r2", win[:, :, 1024:1536], S_, S_.at["gl_og"] + 1)
            sp.wait_ge(mixed, 1)
            sp.dma_start(w2[:], a["w2"]).then_inc(lora_in, 16)
            sp.dma_start(a2[:], a["a2"]).then_inc(lora_in, 16)
            sp.dma_start(g2[:], a["rw_g2"][0]).then_inc(lora_in, 16)
            load("r3", win[:, :, 1536:RW_COLS], V, V.at["rw_p"] + 1)
            wo = a["w_out"][0].rearrange("(t p) n -> p t n", p=P)
            load("o0", wo[:, :, 0:512], V, V.at["rw_p"] + 3)
            load("o1", wo[:, :, 512:1024], V, V.at["rw_p"] + 5)

            def unit(parity, gate, up, down, vwait, swait):
                s = 3 * parity
                if vwait is not None:
                    sp.wait_ge(gu_read, vwait)
                sp.dma_start(slot[s][:], gate.rearrange("(t p) n -> p t n", p=P)).then_inc(slot_in[s], 16)
                sp.dma_start(slot[s + 1][:], up.rearrange("(t p) n -> p t n", p=P)).then_inc(slot_in[s + 1], 16)
                if swait is not None:
                    sp.wait_ge(down_read, swait)
                sp.dma_start(slot[s + 2][:].rearrange("p a b -> p (a b)").rearrange("p (t n) -> p t n", t=4),
                             down.rearrange("(t p) n -> p t n", p=P)).then_inc(slot_in[s + 2], 16)

            g1, u1, d1 = a["moe_w_gate"][0], a["moe_w_up"][0], a["moe_w_down"][0]
            sp.wait_ge(mixed, 2)
            sp.wait_ge(v_filled, V.at["wout"] + 4)
            sp.dma_start(wr[:, :, 0:36], a["wr1"].rearrange("(t p) n -> p t n", p=P)).then_inc(router_in, 16)
            unit(0, g1[0], u1[0], d1[0], None, None)
            unit(1, g1[1], u1[1], d1[1], None, None)
            with sp.Fori(1, N_E1 // 2) as i:
                for s in range(2):
                    e = 2 * i + s
                    unit(s, g1[bass.ds(e, 1), :, :].rearrange("o k n -> (o k) n"),
                         u1[bass.ds(e, 1), :, :].rearrange("o k n -> (o k) n"),
                         d1[bass.ds(e, 1), :, :].rearrange("o k n -> (o k) n"),
                         2 * i + s - 1, 2 * i + s - 1)
            aw = a["att_w_in_2"][0].rearrange("(t p) n -> p t n", p=P)
            load("a0", aw[:, :, 0:512], gu_read, N_E1 - 1)
            load("a1", aw[:, :, 512:1024])
            load("a2", aw[:, :, 1024:1536], down_read, N_E1 - 1)
            load("a3", aw[:, :, 1536:1952], gu_read, N_E1)
            ow = a["att_w_out_2"][0].rearrange("(t p) n -> p t n", p=P)
            load("p0", ow[:, :, 0:512])
            load("p1", ow[:, :, 512:1024], down_read, N_E1)
            sp.wait_ge(mixed, 3)
            sp.dma_start(wq_up[:], a["att_w_q_up_2"][0].rearrange("(t p) n -> p t n", p=P)).then_inc(up_in, 16)
            sp.dma_start(wkv_up[:], a["att_w_kv_up_2"][0]).then_inc(up_in, 16)
            fg, fu, fd = a["dffn_w_gate_2"][0], a["dffn_w_up_2"][0], a["dffn_w_down_2"][0]
            for u in range(NFC):
                c = slice(u * FC, u * FC + FC)
                if u == 0:
                    vw, sw = None, None
                    sp.wait_ge(s_filled, S_.at["sv"] + 2)
                elif u == 1:
                    vw, sw = None, None
                    sp.wait_ge(v_filled, V.at["wout2"] + 4)
                else:
                    vw, sw = N_E1 + u - 1, N_E1 + u - 1
                unit(u % 2, fg[:, c], fu[:, c], fd[c, :], vw, sw)
            sp.wait_ge(mixed, 4)
            sp.dma_start(bT[:], a["bT"]).then_inc(ssm_in, 16)
            sp.dma_start(cT[:], a["cT"]).then_inc(ssm_in, 16)
            load("s0", a["ssm_w_in_2"][0].rearrange("(t p) n -> p t n", p=P), gu_read, N_E1 + NFC - 1)
            glu = a["ssm_w_glu_2"][0].rearrange("(t p) n -> p t n", p=P)
            for n, k in (("s1", 0), ("s2", 1)):
                i, _ = loads[n]
                sp.wait_ge(down_read, N_E1 + NFC - 1)
                sp.dma_start(slot[i][:].rearrange("p a b -> p (a b)").rearrange("p (t n) -> p t n", t=4),
                             glu[:, :, k * D:k * D + D]).then_inc(slot_in[i], 16)
            g2_, u2_, d2_ = a["moe_w_gate_2"][0], a["moe_w_up_2"][0], a["moe_w_down_2"][0]
            unit(0, g2_[0][:, 0:FC], u2_[0][:, 0:FC], d2_[0][0:FC, :], N_E1 + NFC, N_E1 + NFC)
            sp.wait_ge(v_emptied, V.at["glu"] + 4)
            sp.wait_ge(s_filled, S_.at["glu"] + 4)
            unit(1, g2_[0][:, FC:2 * FC], u2_[0][:, FC:2 * FC], d2_[0][FC:2 * FC, :], None, None)
            sp.dma_start(wr[:, :, 0:8], a["moe_router_2"][0].rearrange("(t p) n -> p t n", p=P)).then_inc(router_in, 16)
            with sp.Fori(1, N_E2 * NFC // 2) as i:
                for s in range(2):
                    n = 2 * i + s
                    e, c = n // NFC, (n % NFC) * FC
                    unit(s, g2_[bass.ds(e, 1), :, bass.ds(c, FC)].rearrange("o k n -> (o k) n"),
                         u2_[bass.ds(e, 1), :, bass.ds(c, FC)].rearrange("o k n -> (o k) n"),
                         d2_[bass.ds(e, 1), bass.ds(c, FC), :].rearrange("o k n -> (o k) n"),
                         N_E1 + NFC + n - 1, N_E1 + NFC + n - 1)
            sp.wait_ge(out_ready, 1)
            sp.dma_start(out[0].rearrange("(t p) d -> p t d", p=P), x_sb[:]).then_inc(out_done, 16)
            sp.wait_ge(out_done, 16)

        @block.tensor
        def _(pe):
            def mm(o, l, r, start=True, stop=True):
                return nc.tensor.matmul(o, l, r, start=start, stop=stop)

            def turn(n):
                for j in range(4):
                    b = V.claim(pe, n + j)
                    for k in range(2):
                        for t in range(TT):
                            c = (2 * j + k) * P
                            last = nc.tensor.transpose(b[:, k * T + t * P:k * T + t * P + P],
                                                       xn[:, t, c:c + P], ident)
                    last.then_inc(V.filled, 1)

            def project_T(o, w, c, width=P):
                for k in range(KT):
                    last = mm(o, w[:, k, c:c + width], hT[:, k, :], k == 0, k == KT - 1)
                return last

            def project(o, w, t, c, n):
                for k in range(KT):
                    last = mm(o, hT[:, k, t * P:t * P + P], w[:, k, c:c + n], k == 0, k == KT - 1)
                return last

            pe.wait_ge(misc_in, 64)
            pe.wait_ge(normed, 1)
            turn(V.at["ln1"])
            V.landed(pe, V.at["ln1"] + 3)
            w = arrived(pe, "g0")
            for j in range(2):
                b = S_.claim(pe, S_.at["gl_qk"] + j)
                for k in range(2):
                    last = project_T(b[:, k * T:k * T + T], w, (2 * j + k) * P)
                last.then_inc(S_.filled, 1)
            w = arrived(pe, "g1")
            for t in range(TT):
                project(S_.claim(pe, S_.at["gl_v"] + t)[:, :], w, t, 0, 512).then_inc(S_.filled, 1)
            w = arrived(pe, "g2")
            project_T(S_.claim(pe, S_.at["gl_g"])[0:32, 0:T], w, 0, 32).then_inc(S_.filled, 1)
            w = arrived(pe, "g3")
            for t in range(TT):
                project(S_.claim(pe, S_.at["gl_og"] + t)[:, :], w, t, 0, 512).then_inc(S_.filled, 1)
            S_.landed(pe, S_.at["gl_g"])
            for d in range(DIRS):
                b = V.claim(pe, V.at["gl_z"] + d)
                for k in range(2):
                    last = mm(b[:, k * T:k * T + T], gw2[:, d, k * P:k * P + P], glT[:, :])
                last.then_inc(V.filled, 1)

            for d in range(DIRS):
                order = list(range(NCH))[::1 - 2 * d]
                pe.wait_ge(gl_ops, 2 * d + 1)
                b = S_.claim(pe, S_.at[f"gl{d}_kt"])
                for t in range(TT):
                    for k in range(2):
                        last = nc.tensor.transpose(b[:, t * T + k * P:t * T + k * P + P],
                                                   gKh[:, k, t * P:t * P + P], ident)
                last.then_inc(S_.filled, 1)
                for e in range(2):
                    b = V.claim(pe, V.at[f"gl{d}_q"] + e)
                    o = 64 * e
                    for t in range(TT):
                        for k in range(2):
                            q = (2 * t + k) * P
                            last = mm(b[:, q:q + P], gK[o:o + 64, k, t * P:t * P + P],
                                      gR[o:o + 64, k, t * P:t * P + P])
                    last.then_inc(V.filled, 1)
                S_.landed(pe, S_.at[f"gl{d}_kt"])
                for c in range(2):
                    b = V.claim(pe, V.at[f"gl{d}_h"] + c)
                    for t in range(TT):
                        for h in range(4):
                            o = 64 * (h % 2)
                            last = mm(b[o:o + 64, t * 256 + (h // 2) * P:t * 256 + (h // 2) * P + P],
                                      gKt[64 * c:64 * c + 64, t, h * 64:h * 64 + 64],
                                      Vg[64 * c:64 * c + 64, t, h * P:h * P + P])
                    last.then_inc(V.filled, 1)
                pe.wait_ge(gl_ops, 2 * d + 2)
                for e in range(2):
                    b = V.claim(pe, V.at[f"gl{d}_y"] + e)
                    o = 64 * e
                    for t in range(TT):
                        for k in range(2):
                            h, q = 2 * k + e, (2 * t + k) * P
                            for c in range(2):
                                g = 2 * t + c
                                first = g == order[0]
                                last = mm(b[64 * c:64 * c + 64, q:q + P], gQ[:, t, h, 64 * c:64 * c + 64],
                                          Vg[:, t, h * P:h * P + P], True, first)
                                if not first:
                                    last = mm(b[64 * c:64 * c + 64, q:q + P], gR[o:o + 64, k, g * 64:g * 64 + 64],
                                              gS[o:o + 64, g, k, :], False, True)
                    last.then_inc(V.filled, 1)

            for j in range(8):
                w = arrived(pe, f"r{j // 2}")
                b = V.claim(pe, V.at["rw_p"] + j)
                for k in range(2):
                    c = 2 * j + k
                    if c < 15:
                        last = project_T(b[:, k * T:k * T + T], w, (c % 4) * P)
                last.then_inc(V.filled, 1)
            pe.wait_ge(shifted, 8)
            for t in range(TT):
                b = S_.claim(pe, S_.at["vt"] + t)
                for k in range(4):
                    last = nc.tensor.transpose(b[:, k * P:k * P + P], pT[:, 8 + k, t * P:t * P + P], ident)
                last.then_inc(S_.filled, 1)
            pe.wait_ge(kk_sq, 1)
            for j in range(2):
                b = V.claim(pe, V.at["kk"] + j)
                for k in range(2):
                    last = mm(b[:, k * T:k * T + T], cst("headones"), kds[:, 2 * j + k, :])
                last.then_inc(V.filled, 1)
            pe.wait_ge(lora_in, 48)
            pe.wait_ge(lora_act, 2)

            for d in range(DIRS):
                order = list(range(NCH))[::1 - 2 * d]
                lo = 64 * d
                for i, (wt, src) in enumerate(((w2, 12), (a2, 13))):
                    for j in range(2):
                        b = S_.claim(pe, S_.at[f"rw{d}_lora"] + 2 * i + j)
                        for k in range(2):
                            c = (2 * j + k) * P
                            last = mm(b[:, k * T:k * T + T], wt[lo:lo + 64, c:c + P], pT[lo:lo + 64, src, :])
                        last.then_inc(S_.filled, 1)
                pe.wait_ge(rw_ops, d + 1)
                for t in range(TT):
                    v, s = V.at[f"rw{d}_t{t}"], S_.at[f"rw{d}_t{t}"]
                    tk = slice(t * P, t * P + P)
                    for j in range(3):
                        b = S_.claim(pe, s + j)
                        for k in range(4):
                            src = AR[:, k, t, 0, :] if j == 0 else BKh[:, j - 1, k, tk]
                            last = nc.tensor.transpose(b[:, k * P:k * P + P], src, ident)
                        last.then_inc(S_.filled, 1)
                    for i in range(2):
                        for j in range(4):
                            b = V.claim(pe, v + 4 * i + j)
                            o = 64 * (j // 2)
                            for k in range(2):
                                hp = 2 * (j % 2) + k
                                last = mm(b[:, k * 256:k * 256 + 256], BK[o:o + 64, i, hp, tk],
                                          AR[o:o + 64, hp, t, :, :].rearrange("p a b -> p (a b)"))
                            last.then_inc(V.filled, 1)
                    for e in range(2):
                        b = V.claim(pe, v + 8 + e)
                        o = 64 * e
                        for k in range(4):
                            last = mm(b[:, k * P:k * P + P], AR[o:o + 64, k, t, 0, :], BK[o:o + 64, 0, k, tk])
                        last.then_inc(V.filled, 1)
                    n = v + 10
                    pe.wait_ge(inv_start, 2 * d + t + 1)
                    prev = [None, None]
                    for l in range(2, NLEV + 1):
                        wm_at = n
                        for g in range(2):
                            if prev[g] is not None:
                                V.landed(pe, prev[g])
                            b = V.claim(pe, n)
                            n += 1
                            for q in range(4):
                                h = 4 * g + q
                                last = mm(b[:, q * P:q * P + P], LN[:, h, 0, :], X[:, h, :])
                            last.then_inc(V.filled, 1)
                        for g in range(2):
                            V.landed(pe, wm_at + g)
                            if l < NLEV:
                                b = V.claim(pe, n)
                                n += 1
                                for q in range(4):
                                    h = 4 * g + q
                                    last = mm(b[:, q * P:q * P + P], XT[:, h, :], WM[:, h, :])
                                last.then_inc(V.filled, 1)
                            b = V.claim(pe, n)
                            for q in range(4):
                                h = 4 * g + q
                                last = mm(b[:, q * P:q * P + P], WM[:, h, :], XT[:, h, :])
                            last.then_inc(V.filled, 1)
                            prev[g] = n
                            n += 1
                    if d == 0 and t == 0:
                        S_.landed(pe, S_.at["vt"] + 1)
                    V.landed(pe, v + 9)
                    b = S_.claim(pe, s + 3)
                    for h in range(NH):
                        last = mm(b[:, h * 64:h * 64 + 64], MQ[:, h, 0, :], Vt[:, t, h * 64:h * 64 + 64])
                    last.then_inc(S_.filled, 1)
                    S_.landed(pe, s + 3)
                    for g in range(2):
                        V.landed(pe, prev[g])
                        b = S_.claim(pe, s + 4 + g)
                        for q in range(4):
                            h = 4 * g + q
                            last = mm(b[:, q * P:q * P + P], XT[:, h, :], AM[:, h, :])
                        last.then_inc(S_.filled, 1)
                    S_.landed(pe, s + 5)
                    b = V.claim(pe, n)
                    for h in range(NH):
                        o = 64 * (h % 2)
                        last = mm(b[o:o + 64, (h // 2) * P:(h // 2) * P + P], TAM[:, h, 0:64], LN[:, h, 1, :])
                    last.then_inc(V.filled, 1)
                    for c in range(2):
                        b = V.claim(pe, n + 1 + c)
                        r = slice(64 * c, 64 * c + 64)
                        for h in range(NH):
                            o = 64 * (h % 2)
                            q = (h // 2) * 64
                            last = mm(b[o:o + 64, q:q + 64], TAM[r, h, 0:64], BKt[r, 0, h * 64:h * 64 + 64])
                        last.then_inc(V.filled, 1)
                    for c in range(2):
                        b = S_.claim(pe, s + 6 + c)
                        r = slice(64 * c, 64 * c + 64)
                        for h in range(NH):
                            o = 64 * (h % 2)
                            q = (h // 2) * 64
                            mm(b[o:o + 64, q:q + 64], BKt[r, 1, h * 64:h * 64 + 64],
                               Vt[r, t, h * 64:h * 64 + 64], True, False)
                            last = mm(b[o:o + 64, q:q + 64], BKt[r, 0, h * 64:h * 64 + 64],
                                      TAM[r, h, 64:128], False, True)
                        last.then_inc(S_.filled, 1)
                    n += 1
                    b = V.claim(pe, n + 2)
                    for h in range(NH):
                        c = slice(h * 64, h * 64 + 64)
                        mm(b[:, c], MQ[:, h, 1, :], Vt[:, t, c], True, False)
                        last = mm(b[:, c], LN[:, h, 1, :], TAM[:, h, 64:128], False, True)
                    last.then_inc(V.filled, 1)
                    V.landed(pe, n + 2)
                S_.landed(pe, S_.at[f"rw{d}_t1"] + 7)
                for i in range(2):
                    c0 = order[i + 1]
                    src = Hc[:, order[0]] if i == 0 else S[:, c0]
                    if i:
                        V.landed(pe, V.at[f"rw{d}_s"] + i - 1)
                    b = V.claim(pe, V.at[f"rw{d}_s"] + i)
                    for h in range(NH):
                        o = 64 * (h % 2)
                        last = mm(b[o:o + 64, (h // 2) * 64:(h // 2) * 64 + 64], GT[o:o + 64, c0, h // 2, :],
                                  src[o:o + 64, h // 2, :])
                    last.then_inc(V.filled, 1)
                V.landed(pe, V.at[f"rw{d}_s"] + 1)
                for e in range(2):
                    b = V.claim(pe, V.at[f"rw{d}_y"] + e)
                    o = 64 * e
                    for g in order[1:]:
                        t, c = g // 2, g % 2
                        src = Hc[:, order[0]] if g == order[1] else S[:, g]
                        for k in range(4):
                            last = mm(b[64 * c:64 * c + 64, t * 256 + k * 64:t * 256 + k * 64 + 64],
                                      Rf[o:o + 64, t, k, 64 * c:64 * c + 64], src[o:o + 64, k, :])
                    last.then_inc(V.filled, 1)
            pe.wait_ge(kk_sq, 2)
            b = V.claim(pe, V.at["bonus"])
            for t in range(TT):
                for k in range(4):
                    last = mm(b[:, t * NH + 2 * k:t * NH + 2 * k + 2], kds[:, k, t * P:t * P + P],
                              cst("headones")[:, 0:128:64])
            last.then_inc(V.filled, 1)
            for t in range(TT):
                b = V.claim(pe, V.at["gate"] + t)
                mm(b[:, :], pT[:, 14, t * P:t * P + P], g2[:, :]).then_inc(V.filled, 1)

            pe.wait_ge(mixed, 2)
            turn(V.at["mixT"])
            V.landed(pe, V.at["mixT"] + 3)

            def out_proj(names, n):
                for c, name in enumerate(names):
                    w = arrived(pe, name)
                    for t in range(TT):
                        project(V.claim(pe, n + 2 * c + t)[:, :], w, t, 0, 512).then_inc(V.filled, 1)

            out_proj(("o0", "o1"), V.at["wout"])

            def expert(parity, loaded, hid, out_, vn, sn):
                vf, ve, vp = hid
                sf, se, sp_ = out_
                gate, up, down = slot[3 * parity:3 * parity + 3]
                down = down[:].rearrange("p a b -> p (a b)").rearrange("p (t n) -> p t n", t=4)
                pe.wait_ge(slot_in[3 * parity], 16 * loaded[0])
                pe.wait_ge(slot_in[3 * parity + 1], 16 * loaded[1])
                for f in range(4):
                    pe.wait_ge(ve, vn + f - 3)
                    b = V.bank(vp + f)
                    project_T(b[:, 0:T], gate, f * P)
                    project_T(b[:, T:2 * T], up, f * P).then_inc(vf, 1)
                pe.wait_ge(slot_in[3 * parity + 2], 16 * loaded[2])
                pe.wait_ge(ve, vn + 4)
                for t in range(TT):
                    for c in range(2):
                        pe.wait_ge(se, sn + 2 * t + c - 3)
                        b = S_.bank(sp_ + 2 * t + c)
                        for f in range(4):
                            last = mm(b[:, :], hact[:, parity, f, t * P:t * P + P],
                                      down[:, f, c * 512:c * 512 + 512], f == 0, f == 3)
                        last.then_inc(sf, 1)

            def dense(x):
                with pe.Fori(0, x.count * x.nfc // 2) as i:
                    for s in range(2):
                        k = [x.used[3 * s + j] + i + 1 for j in range(3)]
                        expert(s, k, (x.hid_filled, x.hid_emptied, 0), (x.out_filled, x.out_emptied, 0),
                               8 * i + 4 * s + 4, 8 * i + 4 * s + 4)

            def gathered(x):
                def gather(n, b, bank):
                    for j in range(2):
                        if n is not None:
                            pe.wait_ge(x.x_emptied, n + j - 3)
                        o = psum[(bank + j) % 4]
                        for k in range(4):
                            c = (4 * j + k) * P
                            for t in range(TT):
                                last = mm(o[:, k * CAP:k * CAP + CAP], xn[:, t, c:c + P], sel[:, b, t, :],
                                          t == 0, t == 1)
                        last.then_inc(x.x_filled, 1)

                def turn_hidden(n, bank, up_item):
                    pe.wait_ge(x.x_emptied, up_item + 1)
                    o = psum[bank % 4]
                    for f in range(4):
                        last = nc.tensor.transpose(o[:, f * CAP:f * CAP + CAP], hsb[:, f * P:f * P + P], ident)
                    last.then_inc(x.x_filled, 1)

                def down_proj(n, c, parity, arrived_, before):
                    w = slot[3 * parity + 2][:].rearrange("p a b -> p (a b)").rearrange("p (t n) -> p t n", t=4)
                    pe.wait_ge(slot_in[3 * parity + 2], 16 * arrived_)
                    pe.wait_ge(x.x_emptied, n + 1)
                    if c == 0 and before is not None:
                        pe.wait_ge(x.y_emptied, 2 * before + 2)
                    for h in range(2):
                        for f in range(4):
                            last = mm(psum[4 + h][:, :], hTs[:, f, :], w[:, f, h * 512:h * 512 + 512],
                                      c == 0 and f == 0, c == x.nfc - 1 and f == 3)
                        if c == x.nfc - 1:
                            last.then_inc(x.y_filled, 1)

                def scatter(e):
                    pe.wait_ge(x.y_emptied, 2 * e + 4)
                    for j in range(4):
                        pe.wait_ge(x.z_emptied, 4 * e + j + 1)
                        t, c = j // 2, j % 2
                        mm(psum[6 + j % 2][:, :], selT[:, t * P:t * P + P],
                           yacc[:, c * 512:c * 512 + 512]).then_inc(x.z_filled, 1)

                def used(i, k, c, j):
                    u = k * x.nfc + c
                    return x.used[3 * (u % 2) + j] + x.nfc * i + u // 2 + 1

                def one(i, k, base, first, last):
                    at = {n: j for j, n in enumerate(x.items(first, last))}
                    ph = x.phase(k, first)
                    b = k % 2
                    e = 2 * i + k
                    for c in range(x.nfc):
                        par = (k * x.nfc + c) % 2
                        n = base + at[f"gate{c}"]
                        if c == 0:
                            pe.wait_ge(x.x_emptied, 2 if first else base + x.back["gb"] + 1)
                        pe.wait_ge(x.x_emptied, n - 3) if not (first and c == 0) else None
                        pe.wait_ge(slot_in[3 * par], 16 * used(i, k, c, 0))
                        for q in range(KT):
                            r = mm(psum[(ph + at[f"gate{c}"]) % 4][:, :], xgT[:, b, q, :], slot[3 * par][:, q, :],
                                   q == 0, q == KT - 1)
                        r.then_inc(x.x_filled, 1)
                        if f"hT{c}" in at:
                            n = base + at[f"hT{c}"]
                            pe.wait_ge(x.x_emptied, n - 3)
                            turn_hidden(n, ph + at[f"hT{c}"],
                                        base + (at[f"up{c - 1}"] if c else x.back[f"up{x.nfc - 1}"]))
                        n = base + at[f"up{c}"]
                        if not (first and c == 0):
                            pe.wait_ge(x.x_emptied, n - 3)
                        pe.wait_ge(slot_in[3 * par + 1], 16 * used(i, k, c, 1))
                        for q in range(KT):
                            r = mm(psum[(ph + at[f"up{c}"]) % 4][:, :], xgT[:, b, q, :], slot[3 * par + 1][:, q, :],
                                   q == 0, q == KT - 1)
                        r.then_inc(x.x_filled, 1)
                        if f"hT{c}" in at:
                            ki, cc = (k, c - 1) if c else (k - 1, x.nfc - 1)
                            down_proj(base + at[f"hT{c}"], cc, 1 - par,
                                      used(i, ki, cc, 2), (e if c else e - 1) if not first else None)
                        if c == x.nfc - 1 and not last:
                            pe.wait_ge(x.sel_ready, e + 2)
                            gather(base + at["ga"], 1 - b, ph + at["ga"])
                        if c == min(1, x.nfc - 1):
                            if not first:
                                scatter(e - 1)
                            pe.wait_ge(x.x_emptied, base + at["selT"] - 3)
                            o = psum[(ph + at["selT"]) % 4]
                            for t in range(TT):
                                r = nc.tensor.transpose(o[:, t * P:t * P + P], sel[:, b, t, :], ident)
                            r.then_inc(x.x_filled, 1)

                pe.wait_ge(x.sel_ready, 1)
                gather(None, 0, 0)
                n = x.walk(pe, one)
                pe.wait_ge(x.x_emptied, n - 3)
                up_item = n - len(x.items(False, True)) + x.items(False, True).index(f"up{x.nfc - 1}")
                turn_hidden(n, x.phase(1, False) + len(x.items(False, True)), up_item)
                i = x.count // 2 - 1
                down_proj(n, x.nfc - 1, (x.nfc + x.nfc - 1) % 2, used(i, 1, x.nfc - 1, 2), x.count - 1)
                scatter(x.count - 1)

            def experts(x, rank_item):
                pe.wait_ge(ranked, 1 if x is moe1 else 2)
                b = V.claim(pe, rank_item)
                n = x.count
                mm(b[:, 0:n], cst("before"), msk[:, 0, 0:n])
                mm(b[:, n:2 * n], cst("before"), msk[:, 1, 0:n], True, False)
                mm(b[:, n:2 * n], cst("ones"), msk[:, 0, 0:n], False, True)
                mm(b[:, 2 * n:3 * n], cst("ones"), msk[:, 0, 0:n], True, False)
                mm(b[:, 2 * n:3 * n], cst("ones"), msk[:, 1, 0:n], False, True).then_inc(V.filled, 1)
                V.landed(pe, rank_item)
                S_.landed(pe, x.last_s)
                either(pe, x, dense, gathered)

            pe.wait_ge(normed, 2)
            turn(V.at["ln2"])
            V.landed(pe, V.at["ln2"] + 3)
            pe.wait_ge(router_in, 16)
            b = V.claim(pe, V.at["route1"])
            for t in range(TT):
                last = project(b[:, t * 36:t * 36 + 36], wr, t, 0, 36)
            last.then_inc(V.filled, 1)
            experts(moe1, V.at["rank1"])

            pe.wait_ge(normed, 3)
            turn(V.at["att"])
            V.landed(pe, V.at["att"] + 3)
            for i in range(2):
                w = arrived(pe, f"a{i}")
                for j in range(2):
                    b = S_.claim(pe, S_.at["sqk"] + 2 * i + j)
                    for k in range(2):
                        last = project_T(b[:, k * T:k * T + T], w, (2 * j + k) * P)
                    last.then_inc(S_.filled, 1)
            w = arrived(pe, "a2")
            for t in range(TT):
                project(S_.claim(pe, S_.at["sv"] + t)[:, :], w, t, 0, 512).then_inc(S_.filled, 1)
            w = arrived(pe, "a3")
            for t in range(TT):
                project(S_.claim(pe, S_.at["lat"] + t)[:, 0:416], w, t, 0, 416).then_inc(S_.filled, 1)
            pe.wait_ge(lat_ready, 1)
            for j in range(2):
                b = V.claim(pe, V.at["lat"] + j)
                for k in range(2 - j):
                    for t in range(TT):
                        c = (2 * j + k) * P
                        last = nc.tensor.transpose(b[:, k * T + t * P:k * T + t * P + P], lat[:, t, c:c + P], ident)
                last.then_inc(V.filled, 1)
            V.landed(pe, V.at["lat"] + 1)
            pe.wait_ge(up_in, 32)
            for t in range(TT):
                for c in range(2):
                    b = V.claim(pe, V.at["q_up"] + 2 * t + c)
                    for k in range(2):
                        last = mm(b[:, 0:384], latT[:, k, t * P:t * P + P], wq_up[:, k, c * 384:c * 384 + 384],
                                  k == 0, k == 1)
                    last.then_inc(V.filled, 1)
            for t in range(TT):
                for c in range(2):
                    b = V.claim(pe, V.at["kv_up"] + 2 * t + c)
                    mm(b[:, :], latT[:, 2, t * P:t * P + P], wkv_up[:, c * 512:c * 512 + 512]).then_inc(V.filled, 1)
            pe.wait_ge(heads_ready, 1)
            for i, src in enumerate((qh, kh)):
                for j in range(4):
                    b = S_.claim(pe, S_.at["headsT"] + 4 * i + j)
                    for k in range(2):
                        for t in range(TT):
                            last = nc.tensor.transpose(b[0:MQK, k * T + t * P:k * T + t * P + P],
                                                       src[:, t, 2 * j + k, :], ident)
                    last.then_inc(S_.filled, 1)
            for h in range(NH):
                o, hp = 64 * (h % 2), h // 2
                b = V.claim(pe, V.at["stick"] + 2 * h)
                for k in range(2):
                    last = mm(b[:, k * T:k * T + T], sqkT[o:o + 64, 4 + hp, k * P:k * P + P], sqkT[o:o + 64, hp, :])
                last.then_inc(V.filled, 1)
                pe.wait_ge(fails, h + 1)
                b = V.claim(pe, V.at["stick"] + 2 * h + 1)
                mm(b[:, 0:T], cst("after"), lf[:, 0, :], True, False)
                mm(b[:, 0:T], cst("ones"), lf[:, 1, :], False, True)
                mm(b[:, T:2 * T], cst("after"), lf[:, 1, :]).then_inc(V.filled, 1)
                if h % 2 == 0:
                    b = S_.claim(pe, S_.at[f"st{hp}"])
                    pair = b
                pe.wait_ge(w_ready, h + 1)
                for k in range(2):
                    last = mm(pair[o:o + 64, 0:T], sV[:, k, h * 64:h * 64 + 64], wT[:, k, :], k == 0, k == 1)
                if h % 2:
                    last.then_inc(S_.filled, 1)
                else:
                    last.then_inc(w_read, 1)
            for h in range(NH):
                o, hp = 64 * (h % 2), h // 2
                if h == 0:
                    S_.landed(pe, S_.at["headsT"] + 7)
                b = V.claim(pe, V.at["mla"] + h)
                for q in range(2):
                    last = mm(b[:, q * T:q * T + T], qhT[:, h, q * P:q * P + P], khT[:, h, :])
                last.then_inc(V.filled, 1)
                pe.wait_ge(p_ready, h + 1)
                b = S_.claim(pe, S_.at[f"ml{hp}"] + h % 2)
                nc.tensor.transpose(b[:, 0:P], za[:, 0, 0:P], ident)
                nc.tensor.transpose(b[:, P:2 * P], za[:, 0, T:T + P], ident)
                nc.tensor.transpose(b[:, 2 * P:3 * P], za[:, 0, T + P:2 * T], ident).then_inc(S_.filled, 1)
                S_.landed(pe, S_.at[f"ml{hp}"] + h % 2)
                if h % 2 == 0:
                    continue
                b = S_.claim(pe, S_.at[f"ml{hp}"] + 2)
                for k in range(2):
                    o = 64 * k
                    src = pTt[:, k, :]
                    mm(b[o:o + 64, 0:T], mV[:, 0, h - 1 + k, :], src[:, 0:T], True, False)
                    last = mm(b[o:o + 64, P:T], mV[:, 1, h - 1 + k, :], src[:, T:T + P], False, True)
                last.then_inc(S_.filled, 1)
            S_.landed(pe, S_.at["ml3"] + 2)
            out_proj(("p0", "p1"), V.at["wout2"])

            pe.wait_ge(normed, 4)
            turn(V.at["dffn"])
            V.landed(pe, V.at["dffn"] + 3)
            for u in range(NFC):
                k = [loads[f"f{u}_{j}"][1] for j in range(3)]
                expert(u % 2, k, (V.filled, V.emptied, V.at["ffn"]), (S_.filled, S_.emptied, S_.at["ffn"]),
                       V.at["ffn"] + 4 * u, S_.at["ffn"] + 4 * u)

            pe.wait_ge(normed, 5)
            turn(V.at["ssm"])
            V.landed(pe, V.at["ssm"] + 3)
            w = arrived(pe, "s0")
            for j in range(2):
                b = V.claim(pe, V.at["u"] + j)
                for k in range(2):
                    last = project_T(b[:, k * T:k * T + T], w, (2 * j + k) * P)
                last.then_inc(V.filled, 1)
            V.landed(pe, V.at["u"] + 1)
            pe.wait_ge(ssm_in, 32)
            for j in range(16):
                o = 32 * (j % 4)
                b = V.claim(pe, V.at["s5"] + 2 * j)
                for k in range(2):
                    last = mm(b[:, k * T:k * T + T], bT[o:o + 32, j // 4, k, :], uT[o:o + 32, j // 4, :])
                last.then_inc(V.filled, 1)
                if j == 0:
                    pe.wait_ge(s5_mat, 1)
                pe.wait_ge(s5_h, j + 1)
                b = V.claim(pe, V.at["s5"] + 2 * j + 1)
                mm(b[o:o + 32, 0:T], cT[:, j, 0, :], hst[:, 0, :], True, False)
                mm(b[o:o + 32, 0:T], cT[:, j, 1, :], hst[:, 1, :], False, True).then_inc(V.filled, 1)
            pe.wait_ge(y_gelu, 1)
            for n, name in enumerate(("s2", "s1")):
                arrived(pe, name)
            gl = [slot[loads[n][0]][:].rearrange("p a b -> p (a b)").rearrange("p (t n) -> p t n", t=4)
                  for n in ("s1", "s2")]
            for t in range(TT):
                for c in range(2):
                    for r, ring in ((1, S_), (0, V)):
                        b = ring.claim(pe, ring.at["glu"] + 2 * t + c)
                        for k in range(4):
                            last = mm(b[:, :], yT[:, k, t * P:t * P + P], gl[r][:, k, c * 512:c * 512 + 512],
                                      k == 0, k == 3)
                        last.then_inc(ring.filled, 1)

            pe.wait_ge(normed, 6)
            turn(V.at["moe"])
            V.landed(pe, V.at["moe"] + 3)
            pe.wait_ge(router_in, 32)
            b = V.claim(pe, V.at["route2"])
            for t in range(TT):
                last = project(b[:, t * 8:t * 8 + 8], wr, t, 0, 8)
            last.then_inc(V.filled, 1)
            experts(moe2, V.at["rank2"])

        @block.scalar
        def _(act):
            own = Own(act, act_own)

            def f(o, i, func, bias=0.0, scale=1.0, **k):
                return nc.scalar.activation(o, i, func, bias=bias, scale=scale, **k)

            def root(name, o, i):
                act.wait_ge(meansq, ROOTS.index(name) + 1)
                f(o, i, ACT.Sqrt).then_inc(rooted, 1)

            def empty(n, *moves):
                b = S_.take(act, n)
                for o, pick, scale in moves:
                    last = f(o, pick(b), ACT.Copy, scale=scale)
                last.then_inc(S_.emptied, 1)

            whole = lambda b: b[:, :]

            root("ln1", st[:, 4:6], st[:, 2:4])
            for j in range(2):
                empty(S_.at["gl_qk"] + j, (qkT[:, 2 * j:2 * j + 2, :].rearrange("p a b -> p (a b)"), whole,
                                           0.125 if j == 0 else 1.0))
            for t in range(TT):
                empty(S_.at["gl_v"] + t, (Vg[:, t, :], whole, 1.0))
            empty(S_.at["gl_g"], (glT[:, :], lambda b: b[0:32, 0:T], 1.0))
            for t in range(TT):
                b = S_.take(act, S_.at["gl_og"] + t)
                f(ogs[:, t, :], b[:, :], ACT.Silu).then_inc(S_.emptied, 1)
            for d in range(DIRS):
                V.landed(act, V.at["gl_z"] + d)
                own(f(ge[:, d, :], gz[:, d, :], ACT.Abs))
                own.settle()
                own(f(ge[:, d, :], ge[:, d, :], ACT.Exp, scale=-1.0))
                own.settle()
                f(ge[:, d, :], ge[:, d, :], ACT.Ln, bias=1.0).then_inc(gl_val, 1)
            for d in range(DIRS):
                end = 0 if d else CH - 1
                cend = gc[:, :, :].rearrange("p k (c s) -> p (k c) s", s=CH)[:, :, end]
                flat = gc[:, :, :].rearrange("p a b -> p (a b)")
                act.wait_ge(gl_arg, d + 1)
                f(gP[:, 0, :], flat, ACT.Exp, scale=1 / 16)
                f(gP[:, 1, :], flat, ACT.Exp, scale=-1 / 16)
                f(gP[:, 2, :], gce[:, :, :].rearrange("p a b -> p (a b)"), ACT.Exp, scale=1 / 16)
                f(gPc[:, :], cend, ACT.Exp, scale=1 / 16).then_inc(gl_val, 1)
                b = S_.take(act, S_.at[f"gl{d}_kt"])
                f(gKt[:, :, :].rearrange("p a b -> p (a b)"), b[:, :], ACT.Copy).then_inc(S_.emptied, 1)
            root("gla", st[:, 24:32], st[:, 16:24])

            act.wait_ge(shifted, 8)
            f(pT[:, 12, :], pT[:, 12, :], ACT.Tanh).then_inc(lora_act, 1)
            f(pT[:, 14, :], pT[:, 14, :], ACT.Sigmoid).then_inc(lora_act, 1)
            for t in range(TT):
                empty(S_.at["vt"] + t, (Vt[:, t, :], whole, 1.0))
            root("kk", sca[:, 2, :], sca[:, 2, :])
            for d in range(DIRS):
                for i, name in enumerate(("w0", "a0")):
                    for j in range(2):
                        b = S_.take(act, S_.at[f"rw{d}_lora"] + 2 * i + j)
                        for k in range(2):
                            c = 2 * j + k
                            last = f(sca[:, i, c * T:c * T + T], b[:, k * T:k * T + T], ACT.Sigmoid,
                                     bias=pcol(name, 4 * d + c))
                        last.then_inc(S_.emptied, 1)
                act.wait_ge(cum, d + 1)
                end = 0 if d else CH - 1
                c4 = sca[:, 2, :].rearrange("p (k t c) -> p k t c", k=4, t=TT)
                f(AR[:, :, :, 0, :], BK[:, 1, :, :].rearrange("p k (t c) -> p k t c", t=TT), ACT.Exp, scale=-EXPM)
                f(AR[:, :, :, 1, :], c4, ACT.Exp, scale=-EXPM)
                f(BK[:, 0, :, :].rearrange("p a b -> p (a b)"), sca[:, 2, :], ACT.Exp, scale=EXPM)
                f(BKh[:, 0, :, :], BKh[:, 1, :, :], ACT.Exp, scale=-EXPM)
                f(Pc[:, :], sca[:, 2, :].rearrange("p (k s) -> p k s", s=CH)[:, :, end], ACT.Exp,
                  scale=-EXPM).then_inc(cum_exp, 1)
                for t in range(TT):
                    s = S_.at[f"rw{d}_t{t}"]
                    by_head = lambda b: b[:, :].rearrange("p (h c) -> p h c", h=NH)
                    empty(s, (AM[:, :, 0:64], by_head, 1.0))
                    empty(s + 1, (BKt[:, 0, :], whole, 1.0))
                    empty(s + 2, (BKt[:, 1, :], whole, 1.0))
                    empty(s + 3, (AM[:, :, 64:128], by_head, 1.0))
                    for g in range(2):
                        empty(s + 4 + g, (TAM[:, 4 * g:4 * g + 4, :].rearrange("p a b -> p (a b)"), whole, -1.0))
                    for c in range(2):
                        empty(s + 6 + c, (Hc[:, 2 * t + c].rearrange("p a b -> p (a b)"), lambda b: b[:, 0:256], 1.0))
            root("gn", st[:, 64:80], st[:, 48:64])

            def gates(phase, n, credit, filled, emptied, done):
                for h in range(4):
                    act.wait_ge(filled, n + h + 1)
                    act.wait_ge(emptied, n + h - 1 + credit)
                    b = V.bank(phase + h)
                    f(sg[:, h % 2, :], b[:, 0:T], ACT.Silu).then_inc(done, 1)

            def dense(x):
                with act.Fori(0, x.count * x.nfc) as i:
                    gates(0, 4 * i, 4, x.hid_filled, x.hid_emptied, x.dense_silu)

            def gathered(x):
                def one(i, k, base, first, last):
                    at = {n: j for j, n in enumerate(x.items(first, last))}
                    ph = x.phase(k, first)
                    for c in range(x.nfc):
                        act.wait_ge(x.x_filled, base + at[f"gate{c}"] + 1)
                        if not (first and c == 0):
                            up = at[f"up{c - 1}"] if c else x.back[f"up{x.nfc - 1}"]
                            act.wait_ge(x.x_emptied, base + up + 1)
                        f(sgx[:, :], psum[(ph + at[f"gate{c}"]) % 4][:, :], ACT.Silu).then_inc(x.silu, 1)
                x.walk(act, one)

            root("ln2", st[:, 4:6], st[:, 2:4])
            act.wait_ge(logit_max, 1)
            for t in range(TT):
                f(lg[:, t, 0:4], lg[:, t, 0:4], ACT.Exp, bias=st[:, 10 + t:11 + t], accum_out=st[:, 12 + t:13 + t])
                f(wexp[:, t, :], lm[:, t, :], ACT.Exp, bias=st[:, 14 + t:15 + t])
                f(st[:, 18 + t:19 + t], top[:, t, 1:2], ACT.Exp, bias=st[:, 14 + t:15 + t]).then_inc(logit_exp, 1)
            either(act, moe1, dense, gathered)
            root("lnf", st[:, 4:6], st[:, 2:4])

            root("att", st[:, 4:6], st[:, 2:4])
            for j in range(4):
                empty(S_.at["sqk"] + j, (sqkT[:, 2 * j:2 * j + 2, :].rearrange("p a b -> p (a b)"), whole,
                                         0.125 if j < 2 else 1.0))
            for t in range(TT):
                empty(S_.at["sv"] + t, (sV[:, t, :], whole, 1.0))
            for t in range(TT):
                empty(S_.at["lat"] + t, (lat[:, t, :], lambda b: b[:, 0:416], 1.0))
            root("lat", st[:, 20:24], st[:, 16:20])
            root("heads", stt[:, 4:8, :], stt[:, 0:4, :])
            for i, o in enumerate((qhT, khT)):
                for j in range(4):
                    empty(S_.at["headsT"] + 4 * i + j, (o[:, 2 * j:2 * j + 2, :].rearrange("p a b -> p (a b)"),
                                                        lambda b: b[0:MQK, :], 1.0))
            for h in range(NH):
                act.wait_ge(z_ready, h + 1)
                own(f(za[:, 1, :], za[:, 0, :], ACT.Abs))
                own.settle()
                own(f(za[:, 1, :], za[:, 1, :], ACT.Exp, scale=-1.0))
                own.settle()
                f(za[:, 1, :], za[:, 1, :], ACT.Ln, bias=1.0).then_inc(z_soft, 1)
                act.wait_ge(w_arg, h + 1)
                f(za[:, 2, :], za[:, 2, :], ACT.Exp).then_inc(w_exp, 1)
                if h % 2:
                    empty(S_.at[f"st{h // 2}"], (hT[:, h // 2, :], lambda b: b[:, 0:T], 1.0))
            for h in range(NH):
                act.wait_ge(maxed, h + 1)
                for q in range(2):
                    last = f(za[:, 0, q * T:q * T + T], za[:, 1, q * T:q * T + T], ACT.Exp,
                             bias=st[:, 24 + q:25 + q], scale=MQK ** -0.5, accum_out=st[:, 26 + q:27 + q])
                last.then_inc(p_exp, 1)
                s = S_.at[f"ml{h // 2}"]
                empty(s + h % 2, (pTt[:, h % 2, :], lambda b: b[:, 0:3 * P], 1.0))
                if h % 2:
                    empty(s + 2, (hT[:, 4 + h // 2, :], lambda b: b[:, 0:T], 1.0))

            root("dffn", st[:, 4:6], st[:, 2:4])
            for u in range(NFC):
                gates(V.at["ffn"], V.at["ffn"] + 4 * u, 0, V.filled, V.emptied, silu_done)
            root("ssm", st[:, 4:6], st[:, 2:4])
            p16 = lambda i: par16[:, i, :]
            f(p16(0), pcol("ldt", 0, 16), ACT.Exp).then_inc(s5_val, 1)
            act.wait_ge(s5_arg, 1)
            f(p16(3), p16(2), ACT.Exp)
            f(p16(5), p16(4), ACT.Sin)
            f(p16(7), p16(6), ACT.Sin).then_inc(s5_val, 1)
            act.wait_ge(y_sum, 1)
            f(yT[:, :, :], yT[:, :, :], ACT.Gelu_apprx_tanh).then_inc(y_gelu, 1)
            for t in range(TT):
                for c in range(2):
                    n = 2 * t + c
                    b = S_.take(act, S_.at["glu"] + n)
                    if n:
                        V.landed(act, V.at["glu"] + n - 1)
                    f(gsig, b[:, :], ACT.Sigmoid).then_inc(S_.emptied, 1)
            root("moe", st[:, 4:6], st[:, 2:4])
            act.wait_ge(logit_max, 2)
            for t in range(TT):
                f(wexp[:, t, 0:8], lm[:, t, 0:8], ACT.Exp, bias=st[:, 14 + t:15 + t])
                f(st[:, 18 + t:19 + t], top[:, t, 1:2], ACT.Exp, bias=st[:, 14 + t:15 + t]).then_inc(logit_exp, 1)
            either(act, moe2, dense, gathered)

        @block.vector
        def _(dve):
            own = Own(dve, dve_own)
            vec = nc.vector

            def tt(o, x, y, op):
                return vec.tensor_tensor(o, x, y, op)

            def ts(o, x, s1, op0, s2=None, op1=None):
                return vec.tensor_scalar(o, x, s1, s2, op0, op1) if op1 is not None else \
                    vec.tensor_scalar(o, x, s1, None, op0)

            def stt_(o, x, s, y, op0, op1):
                return vec.scalar_tensor_tensor(out=o, in0=x, scalar=s, in1=y, op0=op0, op1=op1)

            def do(ins):
                own(ins)
                own.settle()

            def signal(ins, s, value):
                ins.then_inc(s, 1)
                dve.wait_ge(s, value)

            def flat(x):
                return x.rearrange("p a b -> p (a b)")

            def spread(col, n):
                return col.unsqueeze(2).to_broadcast([col.shape[0], col.shape[1], n])

            def tiled(x, n):
                return x.unsqueeze(1).to_broadcast([x.shape[0], n, x.shape[1]])

            def rooted_(name):
                dve.wait_ge(rooted, ROOTS.index(name) + 1)

            def mean_square(name, i, o, n, eps):
                signal(ts(o, i, 1.0 / n, ALU.mult, eps, ALU.add), meansq, ROOTS.index(name) + 1)

            def norm(name, dst=None):
                own.settle()
                for t in range(TT):
                    own(vec.tensor_tensor_reduce(out=xn[:, t, :], in0=x_sb[:, t, :], in1=x_sb[:, t, :], scale=1.0,
                                                 scalar=0.0, op0=ALU.mult, op1=ALU.add, accum_out=st[:, t:t + 1]))
                own.settle()
                mean_square(name, st[:, 0:2], st[:, 2:4], D, EPS)
                rooted_(name)
                do(vec.reciprocal(st[:, 6:8], st[:, 4:6]))
                for t in range(TT):
                    ins = ts((dst or xn)[:, t, :], x_sb[:, t, :], st[:, 6 + t:7 + t], ALU.mult)
                    if t == 0 or dst is not None:
                        own(ins)
                if dst is None:
                    ins.then_inc(normed, 1)
                own.settle()

            def turned(n, gain=None):
                for j in range(4):
                    b = V.take(dve, n + j)
                    for k in range(2):
                        c = 2 * j + k
                        if gain:
                            last = ts(hT[:, c, :], b[:, k * T:k * T + T], pcol(gain, c), ALU.mult)
                        else:
                            last = vec.tensor_copy(hT[:, c, :], b[:, k * T:k * T + T])
                    last.then_inc(V.emptied, 1)

            def add_out(n):
                for c in range(2):
                    for t in range(TT):
                        b = V.take(dve, n + 2 * c + t)
                        o = x_sb[:, t, c * 512:c * 512 + 512]
                        tt(o, b[:, :], o, ALU.add).then_inc(V.emptied, 1)
                V.landed(dve, n + 3)

            dve.wait_ge(x_in, 16)
            norm("ln1")
            dve.wait_ge(misc_in, 64)
            turned(V.at["ln1"], "ln1")

            for d in range(DIRS):
                b = V.take(dve, V.at["gl_z"] + d)
                for k in range(2):
                    last = ts(gz[:, d, k * T:k * T + T], b[:, k * T:k * T + T], pcol("gb", 2 * d + k), ALU.add)
                last.then_inc(V.emptied, 1)
            for d in range(DIRS):
                V.landed(dve, V.at["gl_z"] + d)
                dve.wait_ge(gl_val, d + 1)
                do(stt_(gz[:, d, :], gz[:, d, :], 0.0, ge[:, d, :], ALU.min, ALU.subtract))
            for d in range(DIRS):
                order = list(range(NCH))[::1 - 2 * d]
                way = slice(None, None, -1) if d else slice(None)
                end = 0 if d else CH - 1
                for k in range(2):
                    own(vec.tensor_tensor_scan(gc[:, k, way], cst("reset", d, T)[:, way],
                                               gz[:, d, k * T:k * T + T][:, way], 0.0, ALU.mult, ALU.add))
                own.settle()
                by_chunk = gc[:, :, :].rearrange("p k (c s) -> p (k c) s", s=CH)
                tt(gce[:, :, :].rearrange("p k (c s) -> p (k c) s", s=CH), spread(by_chunk[:, :, end], CH), by_chunk,
                   ALU.subtract).then_inc(gl_arg, 1)
                S_.landed(dve, S_.at["gl_qk"] + 1)
                dve.wait_ge(gl_val, DIRS + d + 1)
                own(tt(flat(gR[:, :, :]), gP[:, 0, :], flat(qkT[:, 0:2, :]), ALU.mult))
                own(tt(flat(gK[:, :, :]), gP[:, 1, :], flat(qkT[:, 2:4, :]), ALU.mult))
                own.settle()
                tt(flat(gKh[:, :, :]), gP[:, 2, :], flat(qkT[:, 2:4, :]), ALU.mult).then_inc(gl_ops, 1)
                for e in range(2):
                    b = V.take(dve, V.at[f"gl{d}_q"] + e)
                    for t in range(TT):
                        last = tt(gQ[:, t, e:4:2, :], b[:, t * 256:t * 256 + 256].rearrange("p (h c) -> p h c", h=2),
                                  tiled(cst("mask2", 2 * d + 1, P), 2), ALU.mult)
                    last.then_inc(V.emptied, 1)
                for c in range(2):
                    b = V.take(dve, V.at[f"gl{d}_h"] + c)
                    vec.tensor_copy(gH[:, c:4:2].rearrange("p a b c -> p a (b c)"),
                                    b[:, :].rearrange("p (a b) -> p a b", a=2)).then_inc(V.emptied, 1)
                V.landed(dve, V.at[f"gl{d}_h"] + 1)
                do(vec.tensor_copy(gS[:, order[1]], gH[:, order[0]]))
                for i in (1, 2):
                    for k in range(2):
                        c = order[i]
                        ins = stt_(gS[:, order[i + 1], k, :], gS[:, c, k, :], gPc[:, k * NCH + c:k * NCH + c + 1],
                                   gH[:, c, k, :], ALU.mult, ALU.add)
                        if (i, k) == (2, 1):
                            ins.then_inc(gl_ops, 1)
                        else:
                            own(ins)
                    if i == 1:
                        own.settle()
                own.settle()
                for e in range(2):
                    b = V.take(dve, V.at[f"gl{d}_y"] + e)
                    o = Yg[:, :, :].rearrange("p t (k e c) -> p t k e c", k=2, e=2)[:, :, :, e, :]
                    x = b[:, :].rearrange("p (t k c) -> p t k c", t=TT, k=2)
                    if d:
                        tt(o, x, o, ALU.add).then_inc(V.emptied, 1)
                    else:
                        vec.tensor_copy(o, x).then_inc(V.emptied, 1)
                V.landed(dve, V.at[f"gl{d}_y"] + 1)
            do(tt(Yq[:, :, :], Yg[:, :, :], Yg[:, :, :], ALU.mult))
            do(vec.tensor_reduce(st[:, 8:16], Yq[:, :, :].rearrange("p t (h c) -> p (t h) c", h=4), AXX, ALU.add))
            mean_square("gla", st[:, 8:16], st[:, 16:24], P, EPS)
            rooted_("gla")
            do(vec.reciprocal(st[:, 32:40], st[:, 24:32]))
            do(tt(Yg[:, :, :].rearrange("p t (h c) -> p (t h) c", h=4),
                  Yg[:, :, :].rearrange("p t (h c) -> p (t h) c", h=4), spread(st[:, 32:40], P), ALU.mult))
            do(tt(Yg[:, :, :], Yg[:, :, :], tiled(row("gnorm"), TT), ALU.mult))
            S_.landed(dve, S_.at["gl_og"] + 1)
            signal(tt(xn[:, :, W:D], Yg[:, :, :], ogs[:, :, :], ALU.mult), mixed, 1)

            raw = sca[:, 0, 0:2 * (T + 2)].rearrange("p (a b) -> p a b", a=2)
            both = sca[:, 1, 0:2 * T].rearrange("p (a b) -> p a b", a=2)
            do(vec.memset(raw[:, :, :], 0.0))
            own(ts(mus[:, 0, :], pcol("mu", 0, 15), -1.0, ALU.mult, 1.0, ALU.add))
            do(ts(mus[:, 1, :], pcol("mu", 0, 15), 0.5, ALU.mult))
            do(ts(omka[:, :], pcol("k_a", 0, 4), -1.0, ALU.mult, 1.0, ALU.add))
            for j in range(8):
                m = 2 if j < 7 else 1
                b = V.take(dve, V.at["rw_p"] + j)
                vec.tensor_copy(raw[:, 0:m, 1:T + 1],
                                b[:, 0:m * T].rearrange("p (a b) -> p a b", a=m)).then_inc(V.emptied, 1)
                V.landed(dve, V.at["rw_p"] + j)
                own(tt(both[:, 0:m, :], raw[:, 0:m, 0:T], raw[:, 0:m, 2:T + 2], ALU.add))
                for k in range(m):
                    c = 2 * j + k
                    own(ts(pT[:, c, :], raw[:, k, 1:T + 1], mus[:, 0, c:c + 1], ALU.mult))
                own.settle()
                for k in range(m):
                    c = 2 * j + k
                    ins = stt_(pT[:, c, :], both[:, k, :], mus[:, 1, c:c + 1], pT[:, c, :], ALU.mult, ALU.add)
                    if k < m - 1:
                        own(ins)
                signal(ins, shifted, j + 1)
                own.settle()
            for k in range(4):
                own(ts(kk[:, k, :], pT[:, 4 + k, :], pcol("k_k", k), ALU.mult))
            own.settle()
            tt(kds, kk[:, :, :], kk[:, :, :], ALU.mult).then_inc(kk_sq, 1)
            for j in range(2):
                b = V.take(dve, V.at["kk"] + j)
                ts(sca[:, 2, j * 512:j * 512 + 512], b[:, :], 1e-24, ALU.max).then_inc(V.emptied, 1)
                V.landed(dve, V.at["kk"] + j)
            signal(vec.memset(st[:, 93:94], 0.0), meansq, ROOTS.index("kk") + 1)
            rooted_("kk")
            do(vec.reciprocal(sca[:, 2, :], sca[:, 2, :]))
            do(tt(flat(kk[:, :, :]), flat(kk[:, :, :]), sca[:, 2, :], ALU.mult))

            for d in range(DIRS):
                order = list(range(NCH))[::1 - 2 * d]
                way = slice(None, None, -1) if d else slice(None)
                end = 0 if d else CH - 1
                S_.landed(dve, S_.at[f"rw{d}_lora"] + 3)
                for k in range(4):
                    c = slice(k * T, k * T + T)
                    own(vec.tensor_tensor_scan(sca[:, 2, c][:, way], cst("reset", d, T)[:, way],
                                               sca[:, 0, c][:, way], 0.0, ALU.mult, ALU.add))
                own.settle()
                own(tt(flat(BK[:, 1]), sca[:, 2, :], sca[:, 0, :], ALU.subtract))
                own.settle()
                by_chunk = sca[:, 2, :].rearrange("p (k s) -> p k s", s=CH)
                signal(tt(flat(BKh[:, 1]).rearrange("p (k s) -> p k s", s=CH), spread(by_chunk[:, :, end], CH),
                          by_chunk, ALU.subtract), cum, d + 1)
                for k in range(4):
                    c = slice(k * T, k * T + T)
                    own(ts(sca[:, 0, c], sca[:, 1, c], pcol("k_a", k), ALU.mult, omka[:, k:k + 1], ALU.add))
                own.settle()
                own(tt(sca[:, 0, :], sca[:, 0, :], flat(pT[:, 4:8, :]), ALU.mult))
                do(tt(sca[:, 1, :], sca[:, 1, :], flat(kk[:, :, :]), ALU.mult))
                if d:
                    do(tt(flat(kds), flat(kds), sca[:, 0, :], ALU.add))
                else:
                    do(vec.tensor_copy(flat(kds), sca[:, 0, :]))
                dve.wait_ge(cum_exp, d + 1)
                kk4 = kk[:, :, :].rearrange("p k (t c) -> p k t c", t=TT)
                r4 = pT[:, 0:4, :].rearrange("p k (t c) -> p k t c", t=TT)
                own(tt(AR[:, :, :, 0, :], AR[:, :, :, 0, :], kk4, ALU.mult))
                own(tt(AR[:, :, :, 1, :], AR[:, :, :, 1, :], r4, ALU.mult))
                own(tt(flat(BK[:, 1]), flat(BK[:, 0]), sca[:, 0, :], ALU.mult))
                own(tt(flat(BKh[:, 1]), flat(BKh[:, 0]), sca[:, 0, :], ALU.mult))
                own.settle()
                own(tt(flat(BK[:, 0]), flat(BK[:, 0]), sca[:, 1, :], ALU.mult))
                signal(tt(flat(BKh[:, 0]), flat(BKh[:, 0]), sca[:, 1, :], ALU.mult), rw_ops, d + 1)
                own.settle()
                lev, levt = (("levb", "levf") if d else ("levf", "levb"))
                for t in range(TT):
                    v = V.at[f"rw{d}_t{t}"]
                    for i, dst in enumerate((LN, MQ)):
                        for j in range(4):
                            b = V.take(dve, v + 4 * i + j)
                            h = 4 * (j % 2) + j // 2
                            tt(dst[:, h:h + 3:2].rearrange("p h a b -> p h (a b)"),
                               b[:, :].rearrange("p (h c) -> p h c", h=2),
                               tiled(cst("mask2", d, 2 * P), 2), ALU.mult).then_inc(V.emptied, 1)
                    for g in range(2):
                        b = V.take(dve, v + 8 + g)
                        tt(L1[:, g:NH:2, :], b[:, :].rearrange("p (h c) -> p h c", h=4),
                           tiled(cst("mask2", 2 * (1 - d), P), 4), ALU.mult).then_inc(V.emptied, 1)
                    V.landed(dve, v + 9)
                    own(tt(X, L1[:, :, :], tiled(cst(lev, 0, P), NH), ALU.mult))
                    own(tt(XT, LN[:, :, 0, :], tiled(cst(levt, 0, P), NH), ALU.mult))
                    own.settle()
                    own(tt(X, tiled(ident, NH), X, ALU.subtract))
                    own.settle()
                    signal(tt(XT, tiled(ident, NH), XT, ALU.subtract), inv_start, 2 * d + t + 1)
                    n = v + 10
                    for l in range(2, NLEV + 1):
                        for g in range(2):
                            b = V.take(dve, n)
                            tt(WM[:, 4 * g:4 * g + 4, :], b[:, :].rearrange("p (h c) -> p h c", h=4),
                               tiled(cst(lev, l - 1, P), 4), ALU.mult).then_inc(V.emptied, 1)
                            n += 1
                        for g in range(2):
                            for dst in ((X, XT) if l < NLEV else (XT,)):
                                b = V.take(dve, n)
                                o = dst[:, 4 * g:4 * g + 4, :]
                                V.landed(dve, n - 1)
                                tt(o, o, b[:, :].rearrange("p (h c) -> p h c", h=4),
                                   ALU.subtract).then_inc(V.emptied, 1)
                                n += 1
                    b = V.take(dve, n)
                    tt(Rf[:, t], b[:, :].rearrange("p (k c) -> p k c", k=4), AR[:, :, t, 1, :],
                       ALU.add).then_inc(V.emptied, 1)
                    for c in range(2):
                        b = V.take(dve, n + 1 + c)
                        for k in range(4):
                            g = 2 * t + c
                            last = stt_(GT[:, g, k, :], cst("eye2"), Pc[:, k * NCH + g:k * NCH + g + 1],
                                        b[:, k * 64:k * 64 + 64], ALU.mult, ALU.add)
                        last.then_inc(V.emptied, 1)
                    n += 1
                    b = V.take(dve, n + 2)
                    if d:
                        tt(Yr[:, t, :], b[:, :], Yr[:, t, :], ALU.add).then_inc(V.emptied, 1)
                    else:
                        vec.tensor_copy(Yr[:, t, :], b[:, :]).then_inc(V.emptied, 1)
                    V.landed(dve, n + 2)
                S_.landed(dve, S_.at[f"rw{d}_t1"] + 7)
                for i in range(2):
                    b = V.take(dve, V.at[f"rw{d}_s"] + i)
                    tt(S[:, order[i + 2]].rearrange("p a b -> p (a b)"), b[:, 0:256],
                       Hc[:, order[i + 1]].rearrange("p a b -> p (a b)"), ALU.add).then_inc(V.emptied, 1)
                for e in range(2):
                    b = V.take(dve, V.at[f"rw{d}_y"] + e)
                    for t in range(TT):
                        lo, hi = 0, P
                        if order[0] // 2 == t:
                            lo, hi = (0, 64) if order[0] % 2 else (64, P)
                        o = Yr[lo:hi, t, :].rearrange("p (k e c) -> p k e c", k=4, e=2)[:, :, e, :]
                        last = tt(o, b[lo:hi, t * 256:t * 256 + 256].rearrange("p (k c) -> p k c", k=4), o, ALU.add)
                    last.then_inc(V.emptied, 1)
                V.landed(dve, V.at[f"rw{d}_y"] + 1)
            for k in range(4):
                own(stt_(kds[:, k, :], pT[:, k, :], pcol("r_k", k), kds[:, k, :], ALU.mult, ALU.mult))
            own.settle()
            signal(vec.memset(st[:, 92:93], 0.0), kk_sq, 2)
            scr = BK[:, 0].rearrange("p a b -> p (a b)")
            heads = lambda x: x.rearrange("p t (h c) -> p t h c", h=NH)
            scr_h = scr.rearrange("p (t h c) -> p t h c", t=TT, h=NH)
            sp4 = lambda c: c.rearrange("p (t h) -> p t h", t=TT).unsqueeze(3).to_broadcast([P, TT, NH, HD])
            yh = heads(Yr)
            do(vec.tensor_reduce(st[:, 48:64], yh, AXX, ALU.add))
            do(ts(st[:, 48:64], st[:, 48:64], 1.0 / HD, ALU.mult))
            for t in range(TT):
                own(tt(yh[:, t], yh[:, t], spread(st[:, 48 + 8 * t:56 + 8 * t], HD), ALU.subtract))
            own.settle()
            do(tt(scr.rearrange("p (t c) -> p t c", t=TT), Yr, Yr, ALU.mult))
            do(vec.tensor_reduce(st[:, 48:64], scr_h, AXX, ALU.add))
            mean_square("gn", st[:, 48:64], st[:, 48:64], HD, GN_EPS)
            b = V.take(dve, V.at["bonus"])
            vec.tensor_copy(bon[:, :, :].rearrange("p a b -> p (a b)"), b[:, 0:TT * NH]).then_inc(V.emptied, 1)
            V.landed(dve, V.at["bonus"])
            rooted_("gn")
            do(vec.reciprocal(st[:, 48:64], st[:, 64:80]))
            for t in range(TT):
                own(tt(yh[:, t], yh[:, t], spread(st[:, 48 + 8 * t:56 + 8 * t], HD), ALU.mult))
                own(tt(scr_h[:, t], heads(Vt)[:, t], spread(bon[:, t, :], HD), ALU.mult))
            own.settle()
            do(tt(Yr, Yr, tiled(row("ln_w"), TT), ALU.mult))
            do(tt(Yr, Yr, tiled(row("ln_b"), TT), ALU.add))
            do(tt(Yr, Yr, scr.rearrange("p (t c) -> p t c", t=TT), ALU.add))
            for t in range(TT):
                b = V.take(dve, V.at["gate"] + t)
                tt(Yr[:, t, :], b[:, :], Yr[:, t, :], ALU.mult).then_inc(V.emptied, 1)
            V.landed(dve, V.at["gate"] + 1)
            signal(vec.memset(st[:, 92:93], 0.0), mixed, 2)
            turned(V.at["mixT"])
            add_out(V.at["wout"])

            norm("ln2")
            turned(V.at["ln2"], "ln2")

            def top_two(k, n, t, group):
                do(ts(wexp[:, t, 0:n], wexp[:, t, 0:n], st[:, 20 + t:21 + t], ALU.mult))
                do(stt_(wexp[:, t, 0:n], lm[:, t, 0:n], top[:, t, 1:2], wexp[:, t, 0:n], ALU.is_ge, ALU.mult))

            b = V.take(dve, V.at["route1"])
            tt(lg[:, :, :], b[:, 0:72].rearrange("p (t c) -> p t c", t=TT), tiled(row("rb"), TT),
               ALU.add).then_inc(V.emptied, 1)
            V.landed(dve, V.at["route1"])
            for t in range(TT):
                do(vec.tensor_reduce(st[:, 8 + t:9 + t], lg[:, t, 0:4], AXX, ALU.max))
                do(ts(st[:, 80:84], lg[:, t, 0:4], st[:, 8 + t:9 + t], ALU.is_ge))
                do(ts(st[:, 80:84], st[:, 80:84], 1e30, ALU.mult, -1e30, ALU.add))
                do(tt(lm[:, t, :].rearrange("p (g e) -> p g e", g=4), lg[:, t, 4:36].rearrange("p (g e) -> p g e", g=4),
                      spread(st[:, 80:84], 8), ALU.add))
                do(vec.max(top[:, t, :], lm[:, t, :]))
                do(ts(st[:, 14 + t:15 + t], top[:, t, 0:1], -1.0, ALU.mult))
            signal(ts(st[:, 10:12], st[:, 8:10], -1.0, ALU.mult), logit_max, 1)
            dve.wait_ge(logit_exp, 2)
            do(ts(st[:, 18:20], st[:, 18:20], 1.0, ALU.add))
            do(tt(st[:, 18:20], st[:, 18:20], st[:, 12:14], ALU.mult))
            do(vec.reciprocal(st[:, 20:22], st[:, 18:20]))
            for t in range(TT):
                top_two(0, 32, t, True)

            def unit(hid, out_, n, sn, credit, silus, parity, weight):
                vf, ve, vp, done = hid
                sf, se, sp_ = out_
                for f in range(4):
                    dve.wait_ge(vf, n + f + 1)
                    dve.wait_ge(done, silus + f + 1)
                    b = V.bank(vp + f)
                    tt(hact[:, parity, f, :], b[:, T:2 * T], sg[:, f % 2, :], ALU.mult).then_inc(ve, 1)
                dve.sem_inc(gu_read, 1)
                dve.wait_ge(se, sn + credit)
                for t in range(TT):
                    for c in range(2):
                        dve.wait_ge(sf, sn + 2 * t + c + 1)
                        b = S_.bank(sp_ + 2 * t + c)
                        o = x_sb[:, t, c * 512:c * 512 + 512]
                        stt_(o, b[:, :], weight(t), o, ALU.mult, ALU.add).then_inc(se, 1)
                dve.sem_inc(down_read, 1)

            def dense(x):
                dve.sem_inc(x.hid_emptied, 4)
                dve.sem_inc(x.out_emptied, 4)
                with dve.Fori(0, x.count * x.nfc // 2) as i:
                    for s in range(2):
                        u = 2 * i + s
                        e = u // x.nfc if x.nfc > 1 else u
                        unit((x.hid_filled, x.hid_emptied, 0, x.dense_silu), (x.out_filled, x.out_emptied, 0),
                             4 * u, 4 * u, 4, 4 * u, s, lambda t: wexp[:, t, bass.ds(e, 1)])
                dve.wait_ge(x.out_emptied, 4 + 4 * x.count * x.nfc)

            def gathered(x):
                gain = "ln2" if x is moe1 else "moe"

                def choose(e, b):
                    for t in range(TT):
                        ins = ts(sel[:, b, t, :], cst("iota"), rank[:, t, bass.ds(e, 1)], ALU.is_equal)
                    ins.then_inc(x.sel_ready, 1)

                def take(n):
                    dve.wait_ge(x.x_filled, n + 1)

                def places(n, bank, b):
                    for j in range(2):
                        take(n + j)
                        for k in range(4):
                            c = 4 * j + k
                            ins = ts(xgT[:, b, c, :], psum[(bank + j) % 4][:, k * CAP:k * CAP + CAP], pcol(gain, c),
                                     ALU.mult)
                        ins.then_inc(x.x_emptied, 1)

                def outputs(e):
                    for h in range(2):
                        dve.wait_ge(x.y_filled, 2 * e + h + 1)
                        vec.tensor_copy(yacc[:, h * 512:h * 512 + 512], psum[4 + h][:, :]).then_inc(x.y_emptied, 1)
                    dve.sem_inc(down_read, min(2, x.nfc))

                def add(e):
                    dve.wait_ge(x.z_emptied, 4 * e + 2)
                    for j in range(4):
                        t, c = j // 2, j % 2
                        dve.wait_ge(x.z_filled, 4 * e + j + 1)
                        o = x_sb[:, t, c * 512:c * 512 + 512]
                        stt_(o, psum[6 + j % 2][:, :], wexp[:, t, bass.ds(e, 1)], o, ALU.mult,
                             ALU.add).then_inc(x.z_emptied, 1)

                def one(i, k, base, first, last):
                    at = {n: j for j, n in enumerate(x.items(first, last))}
                    ph = x.phase(k, first)
                    b = k % 2
                    e = 2 * i + k
                    if not last:
                        choose(e + 1, 1 - b)
                    for c in range(x.nfc):
                        dve.wait_ge(x.silu, x.nfc * e + c + 1)
                        dve.sem_inc(x.x_emptied, 1)
                        if f"hT{c}" in at:
                            take(base + at[f"hT{c}"])
                            vec.tensor_copy(hTs[:, :, :].rearrange("p a b -> p (a b)"),
                                            psum[(ph + at[f"hT{c}"]) % 4][:, :]).then_inc(x.x_emptied, 1)
                            if c >= 2:
                                dve.sem_inc(down_read, 1)
                        take(base + at[f"up{c}"])
                        tt(hsb[:, :], psum[(ph + at[f"up{c}"]) % 4][:, :], sgx[:, :], ALU.mult).then_inc(x.x_emptied, 1)
                        dve.sem_inc(gu_read, 1)
                        if c == 0 and not first:
                            outputs(e - 1)
                        if c == x.nfc - 1 and not last:
                            places(base + at["ga"], ph + at["ga"], 1 - b)
                        if c == min(1, x.nfc - 1):
                            if not first:
                                add(e - 1)
                            take(base + at["selT"])
                            vec.tensor_copy(selT[:, :], psum[(ph + at["selT"]) % 4][:, 0:T]).then_inc(x.x_emptied, 1)

                dve.sem_inc(x.y_emptied, 2)
                dve.sem_inc(x.z_emptied, 2)
                choose(0, 0)
                places(0, 0, 0)
                n = x.walk(dve, one)
                take(n)
                vec.tensor_copy(hTs[:, :, :].rearrange("p a b -> p (a b)"),
                                psum[(x.phase(1, False) + len(x.items(False, True))) % 4][:, :]).then_inc(x.x_emptied, 1)
                outputs(x.count - 1)
                add(x.count - 1)
                dve.wait_ge(x.z_emptied, 4 * x.count + 2)

            def ranks(k, x, item):
                n = x.count
                own.settle()
                for t in range(TT):
                    do(ts(msk[:, t, 0:n], lm[:, t, 0:n], top[:, t, 1:2], ALU.is_ge))
                signal(vec.memset(st[:, 92:93], 0.0), ranked, k)
                b = V.take(dve, item)
                own(vec.tensor_reduce(cnt[:, 0:1], b[:, 2 * n:3 * n], AXX, ALU.max))
                stt_(rank[:, :, 0:n], b[:, 0:2 * n].rearrange("p (t e) -> p t e", t=TT), 1.0, msk[:, :, 0:n],
                     ALU.add, ALU.mult).then_inc(V.emptied, 1)
                V.landed(dve, item)
                own.settle()
                do(ts(rank[:, :, 0:n], rank[:, :, 0:n], -1.0, ALU.add))
                signal(ts(over[:, :], cnt[:, 0:1], CAP + 0.5, ALU.is_ge), route_known, k)

            ranks(1, moe1, V.at["rank1"])
            either(dve, moe1, dense, gathered)
            norm("lnf", x_sb)
            signal(tt(x_sb[:, :, :], x_sb[:, :, :], tiled(row("lnf"), TT), ALU.mult), mixed, 3)

            norm("att")
            turned(V.at["att"], "att")
            S_.landed(dve, S_.at["lat"] + 1)
            for t in range(TT):
                for i, (lo, n) in enumerate(((0, 256), (256, 128))):
                    own(vec.tensor_tensor_reduce(out=sqr[:, lo:lo + n], in0=lat[:, t, lo:lo + n],
                                                 in1=lat[:, t, lo:lo + n], scale=1.0 / n, scalar=0.0, op0=ALU.mult,
                                                 op1=ALU.add, accum_out=st[:, 8 + 2 * t + i:9 + 2 * t + i]))
                own.settle()
            mean_square("lat", st[:, 8:12], st[:, 16:20], 1, EPS)
            rooted_("lat")
            do(vec.reciprocal(st[:, 20:24], st[:, 20:24]))
            for t in range(TT):
                for i, (lo, n) in enumerate(((0, 256), (256, 128))):
                    x = lat[:, t, lo:lo + n]
                    do(ts(x, x, st[:, 20 + 2 * t + i:21 + 2 * t + i], ALU.mult))
            vec.memset(st[:, 92:93], 0.0).then_inc(lat_ready, 1)
            dve.wait_ge(lat_ready, 1)
            for k in range(3):
                j = V.at["lat"] + k // 2
                b = V.take(dve, j)
                ins = ts(latT[:, k, :], b[:, (k % 2) * T:(k % 2) * T + T],
                         pcol("qlat", k) if k < 2 else pcol("kvlat"), ALU.mult)
                if k:
                    ins.then_inc(V.emptied, 1)
            for t in range(TT):
                for c in range(2):
                    b = V.take(dve, V.at["q_up"] + 2 * t + c)
                    vec.tensor_copy(qh[:, t, 4 * c:4 * c + 4, :],
                                    b[:, 0:384].rearrange("p (h c) -> p h c", h=4)).then_inc(V.emptied, 1)
            for t in range(TT):
                own(vec.tensor_copy(kh[:, t, :, MN:MQK], tiled(lat[:, t, 384:416], NH)))
                for c in range(2):
                    b = V.take(dve, V.at["kv_up"] + 2 * t + c)
                    x = b[:, :].rearrange("p (h c) -> p h c", h=4)
                    vec.tensor_copy(kh[:, t, 4 * c:4 * c + 4, 0:MN], x[:, :, 0:MN])
                    vec.tensor_copy(mV[:, t, 4 * c:4 * c + 4, :], x[:, :, MN:P]).then_inc(V.emptied, 1)
            own.settle()
            V.landed(dve, V.at["kv_up"] + 3)
            sqh = sqr[:, :].rearrange("p (h c) -> p h c", h=NH)
            for i, x in enumerate((qh, kh)):
                for t in range(TT):
                    do(tt(sqh, x[:, t], x[:, t], ALU.mult))
                    do(vec.tensor_reduce(stt[:, 2 * i + t, :], sqh, AXX, ALU.add))
            mean_square("heads", stt[:, 0:4, :], stt[:, 0:4, :], MQK, EPS)
            rooted_("heads")
            do(vec.reciprocal(stt[:, 0:4, :], stt[:, 4:8, :]))
            rope = cst("rope").rearrange("p (t s c) -> p t s c", t=TT, s=2)
            hf = MR // 2
            rpv = [rp[:, i, :].rearrange("p (h c) -> p h c", h=NH) for i in range(3)]
            for i, x in enumerate((qh, kh)):
                for t in range(TT):
                    do(tt(x[:, t], x[:, t], spread(stt[:, 2 * i + t, :], MQK), ALU.mult))
                    do(tt(x[:, t], x[:, t], tiled(row("kn" if i else "qn"), NH), ALU.mult))
                    r1, r2 = x[:, t, :, MN:MN + hf], x[:, t, :, MN + hf:MQK]
                    co, si = tiled(rope[:, t, 0, :], NH), tiled(rope[:, t, 1, :], NH)
                    own(tt(rpv[0], r1, si, ALU.mult))
                    own(tt(rpv[1], r2, si, ALU.mult))
                    own.settle()
                    own(tt(r1, r1, co, ALU.mult))
                    own(tt(r2, r2, co, ALU.mult))
                    own.settle()
                    own(tt(r1, r1, rpv[1], ALU.subtract))
                    do(tt(r2, r2, rpv[0], ALU.add))
            signal(vec.memset(st[:, 92:93], 0.0), heads_ready, 1)
            for h in range(NH):
                if h == 0:
                    V.landed(dve, V.at["kv_up"] + 3)
                n = V.at["stick"] + 2 * h
                b = V.take(dve, n)
                own(vec.tensor_copy(za[:, 0, :], b[:, :]))
                own.settle()
                vec.memset(st[:, 92:93], 0.0).then_inc(V.emptied, 1)
                signal(vec.memset(st[:, 91:92], 0.0), z_ready, h + 1)
                dve.wait_ge(z_soft, h + 1)
                z2 = za[:, 0, :].rearrange("p (a b) -> p a b", a=2)
                l2 = za[:, 1, :].rearrange("p (a b) -> p a b", a=2)
                do(stt_(lf[:, :, :], z2, 0.0, l2, ALU.max, ALU.add))
                own(tt(lf[:, 0, 0:P], lf[:, 0, 0:P], cst("before"), ALU.mult))
                own(vec.memset(lf[:, 1, 0:P], 0.0))
                own.settle()
                signal(tt(lf[:, 1, P:T], lf[:, 1, P:T], cst("before"), ALU.mult), fails, h + 1)
                do(stt_(za[:, 2, :], za[:, 0, :], 0.0, za[:, 1, :], ALU.min, ALU.subtract))
                b = V.take(dve, n + 1)
                tt(za[:, 2, :], za[:, 2, :], b[:, :], ALU.subtract).then_inc(V.emptied, 1)
                V.landed(dve, n + 1)
                signal(vec.memset(st[:, 91:92], 0.0), w_arg, h + 1)
                dve.wait_ge(w_exp, h + 1)
                if h % 2:
                    dve.wait_ge(w_read, h // 2 + 1)
                elif h:
                    dve.wait_ge(S_.filled, S_.at[f"st{h // 2 - 1}"] + 1)
                e2 = za[:, 2, :].rearrange("p (a b) -> p a b", a=2)
                own(tt(wT[:, 0, 0:P], e2[:, 0, 0:P], cst("before"), ALU.mult))
                own(vec.tensor_copy(wT[:, 0, P:T], e2[:, 0, P:T]))
                own(vec.memset(wT[:, 1, 0:P], 0.0))
                own.settle()
                signal(tt(wT[:, 1, P:T], e2[:, 1, P:T], cst("before"), ALU.mult), w_ready, h + 1)
            dve.wait_ge(S_.filled, S_.at["st3"] + 1)
            for h in range(NH):
                b = V.take(dve, V.at["mla"] + h)
                own(tt(za[:, 1, 0:P], b[:, 0:P], cst("causal"), ALU.add))
                own(ts(za[:, 1, P:T], b[:, P:T], 0.0, ALU.mult, -1e30, ALU.add))
                own(vec.tensor_copy(za[:, 1, T:T + P], b[:, T:T + P]))
                own.settle()
                tt(za[:, 1, T + P:2 * T], b[:, T + P:2 * T], cst("causal"), ALU.add).then_inc(V.emptied, 1)
                V.landed(dve, V.at["mla"] + h)
                do(vec.tensor_reduce(st[:, 22:24], za[:, 1, :].rearrange("p (a b) -> p a b", a=2), AXX, ALU.max))
                if h:
                    dve.wait_ge(S_.filled, S_.at[f"ml{(h - 1) // 2}"] + (h - 1) % 2 + 1)
                signal(ts(st[:, 24:26], st[:, 22:24], -(MQK ** -0.5), ALU.mult), maxed, h + 1)
                dve.wait_ge(p_exp, h + 1)
                do(vec.reciprocal(st[:, 28:30], st[:, 26:28]))
                own(ts(za[:, 0, 0:T], za[:, 0, 0:T], st[:, 28:29], ALU.mult))
                own.settle()
                signal(ts(za[:, 0, T:2 * T], za[:, 0, T:2 * T], st[:, 29:30], ALU.mult), p_ready, h + 1)
            add_out(V.at["wout2"])

            norm("dffn")
            turned(V.at["dffn"], "dffn")
            for u in range(NFC):
                unit((V.filled, V.emptied, V.at["ffn"], silu_done), (S_.filled, S_.emptied, S_.at["ffn"]),
                     V.at["ffn"] + 4 * u, S_.at["ffn"] + 4 * u, 0, 4 * u, u % 2, lambda t: 1.0)
            dve.wait_ge(S_.emptied, S_.at["ffn"] + 4 * NFC)
            signal(vec.memset(st[:, 92:93], 0.0), mixed, 4)

            norm("ssm")
            turned(V.at["ssm"], "ssm")
            for j in range(2):
                b = V.take(dve, V.at["u"] + j)
                vec.tensor_copy(uT[:, 2 * j:2 * j + 2, :].rearrange("p a b -> p (a b)"), b[:, :]).then_inc(V.emptied, 1)
            V.landed(dve, V.at["u"] + 1)
            q = lambda i: par16[:, i, :]
            dve.wait_ge(s5_val, 1)
            do(ts(q(1), pcol("lre", 0, 16), -1e-4, ALU.min))
            do(tt(q(2), q(1), q(0), ALU.mult))
            do(tt(q(4), pcol("lim", 0, 16), q(0), ALU.mult))
            do(ts(q(6), q(4), float(np.pi / 2), ALU.add))
            magic = 12582912.0
            pi_hi = float(np.float32(6.28125))
            pi_lo = float(2 * np.pi - 6.28125)
            for i in (4, 6):
                do(ts(q(8), q(i), float(1 / (2 * np.pi)), ALU.mult, magic, ALU.add))
                do(ts(q(8), q(8), magic, ALU.subtract))
                do(stt_(q(i), q(8), -pi_hi, q(i), ALU.mult, ALU.add))
                do(stt_(q(i), q(8), -pi_lo, q(i), ALU.mult, ALU.add))
                do(ts(q(i), q(i), 3.1415925, ALU.min, -3.1415925, ALU.max))
            signal(vec.memset(st[:, 92:93], 0.0), s5_arg, 1)
            dve.wait_ge(s5_val, 2)
            im = pcol("lim", 0, 16)
            do(tt(q(9), q(3), q(7), ALU.mult))
            do(ts(q(9), q(9), -1.0, ALU.add))
            do(tt(q(10), q(3), q(5), ALU.mult))
            do(tt(q(11), q(1), q(1), ALU.mult))
            do(tt(q(8), im, im, ALU.mult))
            do(tt(q(11), q(11), q(8), ALU.add))
            do(vec.reciprocal(q(11), q(11)))
            do(tt(q(12), q(9), q(1), ALU.mult))
            do(tt(q(8), q(10), im, ALU.mult))
            do(tt(q(12), q(12), q(8), ALU.add))
            do(tt(q(12), q(12), q(11), ALU.mult))
            do(tt(q(13), q(10), q(1), ALU.mult))
            do(tt(q(8), q(9), im, ALU.mult))
            do(tt(q(13), q(13), q(8), ALU.subtract))
            do(tt(q(13), q(13), q(11), ALU.mult))
            dve.wait_ge(ssm_in, 32)
            cr, ci = spread(q(12), 32), spread(q(13), 32)
            t0 = vst[:, 0:2, :].rearrange("p a b -> p (a b)").rearrange("p (a b) -> p a b", a=16)
            t1 = vst[:, 2:4, :].rearrange("p a b -> p (a b)").rearrange("p (a b) -> p a b", a=16)
            own(tt(t0, cT[:, :, 0, :], ci, ALU.mult))
            own(tt(t1, cT[:, :, 1, :], ci, ALU.mult))
            own.settle()
            own(tt(cT[:, :, 0, :], cT[:, :, 0, :], cr, ALU.mult))
            own(tt(cT[:, :, 1, :], cT[:, :, 1, :], cr, ALU.mult))
            own.settle()
            own(tt(cT[:, :, 0, :], cT[:, :, 0, :], t1, ALU.subtract))
            do(tt(cT[:, :, 1, :], cT[:, :, 1, :], t0, ALU.add))
            do(ts(cT[:, :, 1, :], cT[:, :, 1, :], -1.0, ALU.mult))
            signal(vec.memset(st[:, 92:93], 0.0), s5_mat, 1)
            own(vec.memset(rot[:, 0, :, 0:1], 1.0))
            own(vec.memset(rot[:, 1, :, 0:1], 0.0))
            own.settle()
            do(vec.tensor_copy(q(14), q(7)))
            do(vec.tensor_copy(q(15), q(5)))
            n = 1
            while n < T:
                c, s = spread(q(14), n), spread(q(15), n)
                re, mi = rot[:, 0, :, 0:n], rot[:, 1, :, 0:n]
                ra, rb = rot[:, 0, :, n:2 * n], rot[:, 1, :, n:2 * n]
                own(tt(rtm[:, 0, :, 0:n], mi, s, ALU.mult))
                own(tt(rtm[:, 1, :, 0:n], mi, c, ALU.mult))
                own(tt(ra, re, c, ALU.mult))
                own(tt(rb, re, s, ALU.mult))
                own.settle()
                own(tt(ra, ra, rtm[:, 0, :, 0:n], ALU.subtract))
                own(tt(rb, rb, rtm[:, 1, :, 0:n], ALU.add))
                do(tt(q(16), q(15), q(15), ALU.mult))
                do(tt(q(15), q(15), q(14), ALU.mult))
                do(ts(q(15), q(15), 2.0, ALU.mult))
                do(tt(q(14), q(14), q(14), ALU.mult))
                do(tt(q(14), q(14), q(16), ALU.subtract))
                n *= 2
            for j in range(16):
                o = 32 * (j % 4)
                n = V.at["s5"] + 2 * j
                b = V.take(dve, n)
                co, si = rot[:, 0, j, :], rot[:, 1, j, :]
                v0, v1 = vst[:, 0, :], vst[:, 1, :]
                own(tt(v0, b[:, 0:T], co, ALU.mult))
                own(tt(vst[:, 2, :], b[:, T:2 * T], si, ALU.mult))
                own(tt(v1, b[:, T:2 * T], co, ALU.mult))
                own.settle()
                tt(vst[:, 3, :], b[:, 0:T], si, ALU.mult).then_inc(V.emptied, 1)
                V.landed(dve, n)
                own(tt(v0, v0, vst[:, 2, :], ALU.add))
                do(tt(v1, v1, vst[:, 3, :], ALU.subtract))
                dec = q(3)[:, j:j + 1].to_broadcast([P, T])
                own(vec.tensor_tensor_scan(vst[:, 2, :], dec, v0, 0.0, ALU.mult, ALU.add))
                do(vec.tensor_tensor_scan(vst[:, 3, :], dec, v1, 0.0, ALU.mult, ALU.add))
                g0, g1_ = vst[:, 2, :], vst[:, 3, :]
                if j:
                    V.landed(dve, n - 1)
                own(tt(hst[:, 0, :], g0, co, ALU.mult))
                own(tt(v0, g1_, si, ALU.mult))
                own(tt(hst[:, 1, :], g0, si, ALU.mult))
                own(tt(v1, g1_, co, ALU.mult))
                own.settle()
                own(tt(hst[:, 0, :], hst[:, 0, :], v0, ALU.subtract))
                own.settle()
                signal(tt(hst[:, 1, :], hst[:, 1, :], v1, ALU.add), s5_h, j + 1)
                b = V.take(dve, n + 1)
                stt_(yT[o:o + 32, j // 4, :], uT[o:o + 32, j // 4, :], pcol("sd", j // 4)[o:o + 32, :], b[o:o + 32, 0:T],
                     ALU.mult, ALU.add).then_inc(V.emptied, 1)
                V.landed(dve, n + 1)
            signal(vec.memset(st[:, 92:93], 0.0), y_sum, 1)
            for t in range(TT):
                for c in range(2):
                    n = 2 * t + c
                    b = V.take(dve, V.at["glu"] + n)
                    S_.landed(dve, S_.at["glu"] + n)
                    o = x_sb[:, t, c * 512:c * 512 + 512]
                    do(tt(gsig2, b[:, :], gsig, ALU.mult))
                    tt(o, o, gsig2, ALU.add).then_inc(V.emptied, 1)
                    V.landed(dve, V.at["glu"] + n)

            norm("moe")
            turned(V.at["moe"], "moe")
            b = V.take(dve, V.at["route2"])
            vec.tensor_copy(lm[:, :, 0:8], b[:, 0:16].rearrange("p (t c) -> p t c", t=TT)).then_inc(V.emptied, 1)
            V.landed(dve, V.at["route2"])
            for t in range(TT):
                do(vec.max(top[:, t, :], lm[:, t, 0:8]))
                do(ts(st[:, 14 + t:15 + t], top[:, t, 0:1], -1.0, ALU.mult))
            signal(vec.memset(st[:, 92:93], 0.0), logit_max, 2)
            dve.wait_ge(logit_exp, 4)
            do(ts(st[:, 18:20], st[:, 18:20], 1.0, ALU.add))
            do(vec.reciprocal(st[:, 20:22], st[:, 18:20]))
            for t in range(TT):
                top_two(0, 8, t, True)
            ranks(2, moe2, V.at["rank2"])
            either(dve, moe2, dense, gathered)
            vec.memset(st[:, 92:93], 0.0).then_inc(out_ready, 1)


_RAW = ["x", "w_in", "rw_g2", "w_out", "moe_w_gate", "moe_w_up", "moe_w_down", "att_w_in_2", "att_w_q_up_2",
        "att_w_kv_up_2", "att_w_out_2", "dffn_w_gate_2", "dffn_w_up_2", "dffn_w_down_2", "ssm_w_in_2",
        "ssm_w_glu_2", "moe_router_2", "moe_w_gate_2", "moe_w_up_2", "moe_w_down_2"]


def layout(x):
    col = lambda v: v.reshape(-1, P).T
    f = np.float32
    par = [x["ln1_w"], x["rw_mu"], x["rw_w0_f"], x["rw_w0_b"], x["rw_a0_f"], x["rw_a0_b"], x["rw_k_k"],
           x["rw_k_a"], x["rw_r_k"], x["gla_gb_f"], x["gla_gb_b"], x["ln2_w"], x["att_norm_2"],
           x["att_q_latent_norm_2"], x["att_kv_latent_norm_2"], x["dffn_norm_2"], x["ssm_norm_2"], x["moe_norm_2"],
           x["ssm_d_2"], x["ssm_a_re_2"], x["ssm_a_im_2"], np.broadcast_to(x["ssm_log_dt_2"][0][:, None], (32, 64))]
    rows = [x["rw_ln_w"], x["rw_ln_b"], x["gla_norm_w"], x["ln_f_w"], x["att_q_norm_2"], x["att_k_norm_2"],
            x["moe_b_coarse"], x["moe_b_fine"]]
    gw2 = np.zeros((32, 2, 256), f)
    gw2[0:16, 0] = x["gla_gw2_f"][0]
    gw2[16:32, 1] = x["gla_gw2_b"][0]
    bT = np.zeros((4, 2, 16, 4, 2, 2, 64), f)
    cT = np.zeros((2, 64, 16, 2, 2, 16), f)
    for r, (b, c) in enumerate((("ssm_b_re_2", "ssm_c_re_2"), ("ssm_b_im_2", "ssm_c_im_2"))):
        bb = x[b][0].reshape(4, 4, 2, 64, 16)
        cc = x[c][0].reshape(16, 2, 16, 64)
        for g in range(2):
            bT[:, g, :, :, r, g, :] = bb[:, :, g].transpose(1, 3, 0, 2)
            cT[g, :, :, r, g, :] = cc[:, g].transpose(2, 0, 1)
    return {
        "par": np.concatenate([col(v) for v in par], 1),
        "rows": np.concatenate([v.reshape(-1) for v in rows]),
        "con": np.concatenate(list(constants().values()), 1),
        "gw2": gw2,
        "w2": np.concatenate([x["rw_w2_f"][0], x["rw_w2_b"][0]], 0),
        "a2": np.concatenate([x["rw_a2_f"][0], x["rw_a2_b"][0]], 0),
        "wr1": np.concatenate([x["moe_w_coarse"][0], x["moe_w_fine"][0]], 1),
        "bT": bT.reshape(P, 4, 2, P),
        "cT": cT.reshape(P, 16, 2, 32),
    }


def kernel(**inputs):
    import concourse.bacc as _bacc
    from concourse.bass_utils import run_bass_kernel_spmd as _run

    x = {n: np.asarray(v) for n, v in inputs.items()}
    given = {n: x[n] for n in _RAW} | layout(x)
    nc = _bacc.Bacc("TRN2", target_bir_lowering=False, num_devices=1)
    arrays, aps = {}, {}
    for name, v in given.items():
        arrays[f"in_{name}"] = v = np.ascontiguousarray(v)
        aps[name] = nc.dram_tensor(f"in_{name}", v.shape, mybir.dt.from_np(v.dtype), kind="ExternalInput").ap()
    out = nc.dram_tensor("out", (1, T, D), F32, kind="ExternalOutput").ap()
    block_kernel(nc, aps, out)
    r = _run(nc, [arrays], core_ids=[0])
    return r.results[0]["out"]
```

```python
from contextlib import ExitStack

import numpy as np
import concourse.bass as bass
from concourse import mybir

F32 = mybir.dt.float32
ALU = mybir.AluOpType
ACT = mybir.ActivationFunctionType
AXX = mybir.AxisListType.X

P = 128
T = 256
TT = T // P
D = 1024
KT = D // P
CH = 64
NCH = T // CH
HD = 64
NH = 8
HP = NH // 2
NLEV = 6
DIRS = 2
W = NH * HD
EXPM = float(np.exp(np.float32(-0.5)))
EPS = 1e-6
GN_EPS = 64e-5

RW_COLS = 1920
GL_Q = RW_COLS
GL_V = GL_Q + 512
GL_GATE = GL_V + 512
GL_OG = GL_GATE + 32

AT_V = 1024
AT_CQ = 1536
AT_KR = AT_CQ + 256 + 128
MR, MN, MQK = 32, 64, 96

N_E1, F1 = 32, 512
N_E2, F2 = 8, 3584
FC = 512
NFC = F2 // FC
CAP = P
HALF = CAP // 2

PAR = {}
_n = 0
for _name, _c in (("ln1", 8), ("mu", 15), ("w0", 8), ("a0", 8), ("k_k", 4), ("k_a", 4), ("r_k", 4), ("gb", 4),
                  ("ln2", 8), ("att", 8), ("qlat", 2), ("kvlat", 1), ("dffn", 8), ("ssm", 8), ("moe", 8),
                  ("sd", 4), ("lre", 16), ("lim", 16), ("ldt", 16)):
    PAR[_name] = (_n, _c)
    _n += _c
NPAR = _n
ROW = {}
_n = 0
for _name, _c in (("ln_w", 512), ("ln_b", 512), ("gnorm", 512), ("lnf", 1024), ("qn", 96), ("kn", 96),
                  ("rb", 36)):
    ROW[_name] = (_n, _c)
    _n += _c
NROW = _n


def constants():
    i = np.arange(P)
    r, c = i[:, None], i[None, :]
    same = (r // CH) == (c // CH)
    up = same & (r < c)
    dn = same & (r > c)
    eye = r == c
    k = {"ident": eye}
    k["mask2"] = np.concatenate([up, up | eye, dn, dn | eye], 1)
    lev = []
    for l in range(1, NLEV + 1):
        b = 2 ** l
        lev.append((r // b == c // b) & (r % b >= b // 2) & (c % b < b // 2))
    k["levf"] = np.concatenate(lev, 1)
    k["levb"] = np.concatenate([m.T for m in lev], 1)
    k["headones"] = (r // HD) == (c // HD)
    t = np.arange(T)
    k["reset"] = np.concatenate([np.tile(t % CH != 0, (P, 1)), np.tile(t % CH != CH - 1, (P, 1))], 1)
    k["iota"] = np.tile(np.arange(CAP), (P, 1))
    k["before"] = r < c
    k["after"] = r > c
    k["ones"] = np.ones((P, P))
    k["eye2"] = (r % HD) == i[None, :HD]
    k["causal"] = np.where(c <= r, 0.0, -1e30)
    half = MR // 2
    inv = np.float32(10000.0) ** (-np.arange(0, MR, 2, dtype=np.float32) / np.float32(MR))
    ang = np.arange(T, dtype=np.float32)[:, None] * inv[None, :]
    rope = np.stack([np.cos(ang), np.sin(ang)], 1).reshape(TT, P, 2 * half).transpose(1, 0, 2)
    k["rope"] = rope.reshape(P, TT * 2 * half)
    return {n: np.ascontiguousarray(a, np.float32) for n, a in k.items()}


CONST_COLS = {n: a.shape[1] for n, a in constants().items()}
C0 = {}
_n = 0
for _name, _c in CONST_COLS.items():
    C0[_name] = (_n, _c)
    _n += _c
NCONST = _n


class Ring:

    def __init__(self, banks, filled, emptied, stages):
        self.banks, self.filled, self.emptied = banks, filled, emptied
        self.at, n = {}, 0
        for name, count in stages:
            self.at[name] = n
            n += count
        self.total = n

    def bank(self, n):
        return self.banks[n % 4]

    def claim(self, pe, n):
        if n >= 4:
            pe.wait_ge(self.emptied, n - 3)
        return self.banks[n % 4]

    def take(self, eng, n):
        eng.wait_ge(self.filled, n + 1)
        return self.banks[n % 4]

    def landed(self, eng, n):
        eng.wait_ge(self.emptied, n + 1)


class Own:

    def __init__(self, eng, sem):
        self.eng, self.sem, self.n = eng, sem, 0

    def __call__(self, ins):
        ins.then_inc(self.sem, 1)
        self.n += 1
        return self.n

    def settle(self):
        if self.n:
            self.eng.wait_ge(self.sem, self.n)


def block_kernel(nc, a, out):
    ctx = ExitStack()
    with ctx:
        def sb(name, shape, dt=F32, stack=None):
            return (stack or ctx).enter_context(nc.sbuf_tensor(name, shape, dt))

        def sem(name):
            return ctx.enter_context(nc.semaphore(name))

        par = sb("par", [P, NPAR])
        rows = sb("rows", [P, NROW])
        con = sb("con", [P, NCONST])
        x_sb = sb("x_sb", [P, TT, D])
        xn = sb("xn", [P, TT, D])
        hT = sb("hT", [P, KT, T])
        st = sb("st", [P, 96])
        slot = [sb(f"slot{i}", [P, KT, FC]) for i in range(3)]

        def pcol(name, i=0, n=1):
            o = PAR[name][0] + i
            return par[:, o:o + n]

        def row(name):
            o, n = ROW[name]
            return rows[:, o:o + n]

        def cst(name, i=0, n=None):
            o, m = C0[name]
            n = m if n is None else n
            return con[:, o + i * n:o + i * n + n]

        ident = cst("ident")
        psum = [ctx.enter_context(nc.psum_tensor(f"ps{i}", [P, 512], F32)) for i in range(8)]

        gla = ExitStack()
        qkT = sb("qkT", [P, 4, T], stack=gla)
        Vg = sb("Vg", [P, TT, W], stack=gla)
        glT = sb("glT", [32, T], stack=gla)
        gw2 = sb("gw2", [32, DIRS, T], stack=gla)
        ogs = sb("ogs", [P, TT, W], stack=gla)
        gz = sb("gz", [P, DIRS, 2 * T], stack=gla)
        ge = sb("ge", [P, DIRS, 2 * T], stack=gla)
        gc = sb("gc", [P, 2, T], stack=gla)
        gce = sb("gce", [P, 2, T], stack=gla)
        gP = sb("gP", [P, 3, 2 * T], stack=gla)
        gPc = sb("gPc", [P, 2 * NCH], stack=gla)
        gR = sb("gR", [P, 2, T], stack=gla)
        gK = sb("gK", [P, 2, T], stack=gla)
        gKh = sb("gKh", [P, 2, T], stack=gla)
        gKt = sb("gKt", [P, TT, 2 * P], stack=gla)
        gQ = sb("gQ", [P, TT, 4, P], stack=gla)
        gH = sb("gH", [P, NCH, 2, P], stack=gla)
        gS = sb("gS", [P, NCH, 2, P], stack=gla)
        Yg = sb("Yg", [P, TT, W], stack=gla)
        Yq = sb("Yq", [P, TT, W], stack=gla)
        gla.close()

        rw = ExitStack()
        pT = sb("pT", [P, 15, T], stack=rw)
        kk = sb("kk", [P, 4, T], stack=rw)
        w2 = sb("w2", [P, W], stack=rw)
        a2 = sb("a2", [P, W], stack=rw)
        g2 = sb("g2", [P, W], stack=rw)
        omka = sb("omka", [P, 4], stack=rw)
        mus = sb("mus", [P, 2, 15], stack=rw)
        Vt = hT[:, 0:4, :].rearrange("p a b -> p (a b)").rearrange("p (t w) -> p t w", t=TT)
        kds = hT[:, 4:8, :]
        Yr = xn[:, :, 0:W]
        bon = sb("bon", [P, TT, NH], stack=rw)
        sca = sb("sca", [P, 3, 4 * T], stack=rw)
        Pc = sb("Pc", [P, 4 * NCH], stack=rw)
        AR = sb("AR", [P, 4, TT, 2, P], stack=rw)
        BK = sb("BK", [P, 2, 4, T], stack=rw)
        BKh = sb("BKh", [P, 2, 4, T], stack=rw)
        BKt = sb("BKt", [P, 2, W], stack=rw)
        AM = sb("AM", [P, NH, P], stack=rw)
        LN = sb("LN", [P, NH, 2, P], stack=rw)
        MQ = sb("MQ", [P, NH, 2, P], stack=rw)
        L1 = sb("L1", [P, NH, P], stack=rw)
        X = sca[:, 0, :].rearrange("p (h c) -> p h c", h=NH)
        XT = sca[:, 1, :].rearrange("p (h c) -> p h c", h=NH)
        WM = sca[:, 2, :].rearrange("p (h c) -> p h c", h=NH)
        TAM = L1
        Rf = sb("Rf", [P, TT, 4, P], stack=rw)
        GT = sb("GT", [P, NCH, 4, HD], stack=rw)
        Hc = sb("Hc", [P, NCH, 4, HD], stack=rw)
        S = sb("S", [P, NCH, 4, HD], stack=rw)
        rw.close()

        slot += [sb(f"slot{i}", [P, KT, FC]) for i in range(3, 6)]
        att = ExitStack()
        sqkT = sb("sqkT", [P, 8, T], stack=att)
        sV = sb("sV", [P, TT, W], stack=att)
        lat = sb("lat", [P, TT, 416], stack=att)
        latT = sb("latT", [P, 3, T], stack=att)
        wq_up = sb("wq_up", [P, 2, NH * MQK], stack=att)
        wkv_up = sb("wkv_up", [P, NH * P], stack=att)
        qh = xn[:, :, 0:NH * MQK].rearrange("p t (h c) -> p t h c", h=NH)
        kh = sb("kh", [P, TT, NH, MQK], stack=att)
        mV = sb("mV", [P, TT, NH, HD], stack=att)
        qhT = sb("qhT", [MQK, NH, T], stack=att)
        khT = sb("khT", [MQK, NH, T], stack=att)
        rp = sb("rp", [P, 3, NH * MR // 2], stack=att)
        sqr = sb("sqr", [P, NH * MQK], stack=att)
        stt = sb("stt", [P, 8, NH], stack=att)
        za = wq_up[:, :, :].rearrange("p a b -> p (a b)")[:, 0:9 * P].rearrange("p (a b) -> p a b", a=3)
        lf = wkv_up[:, 0:3 * P]
        wT = wkv_up[:, 3 * P:6 * P]
        mz = xn[:, 0, 0:3 * P]
        mp = xn[:, 0, 4 * P:7 * P]
        pTt = xn[:, 1, 0:6 * P].rearrange("p (a b) -> p a b", a=2)
        att.close()

        ssm = ExitStack()
        sb("dense_part", [P, 10, T], stack=ssm)
        uT = sb("uT", [P, 4, T], stack=ssm)
        bT = sb("bT", [P, 4, 2, P], stack=ssm)
        cT = sb("cT", [P, 16, 2, 32], stack=ssm)
        par16 = sb("par16", [P, 24, 16], stack=ssm)
        pi16 = sb("pi16", [P, 16], mybir.dt.int32, stack=ssm)
        rot = sb("rot", [P, 2, 16, T], stack=ssm)
        yT = hT[:, 0:4, :]
        rtm = xn[:, :, :].rearrange("p s (j t) -> p s j t", j=8)
        vst = xn[:, :, :].rearrange("p s (m c t) -> p s m c t", m=2, c=2)
        hst = hT[:, 4:8, :].rearrange("p (m c) b -> p m c b", m=2)
        gsig = xn[:, 1, 512:1024]
        gsig2 = hT[:, 4:6, :].rearrange("p a b -> p (a b)")
        ssm.close()

        ffn = ExitStack()
        sg = sb("sg", [P, 2, T], stack=ffn)
        hact = sb("hact", [P, 2, 4, T], stack=ffn)
        wr = sb("wr", [P, KT, 48], stack=ffn)
        lg = sb("lg", [P, TT, 36], stack=ffn)
        lm = sb("lm", [P, TT, 32], stack=ffn)
        top = sb("top", [P, TT, 8], stack=ffn)
        wexp = sb("wexp", [P, TT, N_E1], stack=ffn)
        msk = sb("msk", [P, TT, N_E1], stack=ffn)
        rank = sb("rank", [P, TT, N_E1], stack=ffn)
        cnt = sb("cnt", [P, 2], stack=ffn)
        over = sb("over", [P, 1], mybir.dt.int32, stack=ffn)
        sel = sb("sel", [P, 2, TT, CAP], stack=ffn)
        selT = sb("selT", [CAP, T], stack=ffn)
        xgT = sb("xgT", [P, 2, KT, CAP], stack=ffn)
        sgx = sb("sgx", [CAP, FC], stack=ffn)
        hsb = sb("hsb", [CAP, FC], stack=ffn)
        hTs = sb("hTs", [P, 4, CAP], stack=ffn)
        yacc = sb("yacc", [CAP, D], stack=ffn)
        ffn.close()

        misc_in = sem("misc_in")
        x_in = sem("x_in")
        lora_in = sem("lora_in")
        up_in = sem("up_in")
        ssm_in = sem("ssm_in")
        router_in = sem("router_in")
        slot_in = [sem(f"slot_in{i}") for i in range(6)]
        v_filled, v_emptied = sem("v_filled"), sem("v_emptied")
        s_filled, s_emptied = sem("s_filled"), sem("s_emptied")
        dve_own, act_own = sem("dve_own"), sem("act_own")
        meansq = sem("meansq")
        rooted = sem("rooted")
        normed = sem("normed")
        gl_arg = sem("gl_arg")
        gl_val = sem("gl_val")
        gl_ops = sem("gl_ops")
        shifted = sem("shifted")
        lora_act = sem("lora_act")
        kk_sq = sem("kk_sq")
        cum = sem("cum")
        cum_exp = sem("cum_exp")
        rw_ops = sem("rw_ops")
        inv_start = sem("inv_start")
        mixed = sem("mixed")
        w_read = sem("w_read")
        lat_ready = sem("lat_ready")
        heads_ready = sem("heads_ready")
        z_ready = sem("z_ready")
        z_soft = sem("z_soft")
        fails = sem("fails")
        w_arg = sem("w_arg")
        w_exp = sem("w_exp")
        w_ready = sem("w_ready")
        maxed = sem("maxed")
        p_exp = sem("p_exp")
        p_ready = sem("p_ready")
        logit_max = sem("logit_max")
        logit_exp = sem("logit_exp")
        silu_done = sem("silu_done")
        ranked = sem("ranked")
        route_known = sem("route_known")
        gu_read = sem("gu_read")
        down_read = sem("down_read")
        s5_arg = sem("s5_arg")
        s5_val = sem("s5_val")
        s5_mat = sem("s5_mat")
        s5_h = sem("s5_h")
        y_sum = sem("y_sum")
        y_gelu = sem("y_gelu")
        glu_sig = sem("glu_sig")
        out_ready = sem("out_ready")
        out_done = sem("out_done")

        inv_items = 4 + 4 + 2 + (NLEV - 1) * 2 + (NLEV - 2) * 2 + (NLEV - 1) * 2 + 4
        V = Ring(psum[0:4], v_filled, v_emptied, [
            ("ln1", 4), ("gl_z", 2)]
            + [(f"gl{d}_{n}", c) for d in range(DIRS) for n, c in (("q", 2), ("h", 2), ("y", 2))]
            + [("rw_p", 8), ("kk", 2)]
            + [(f"rw{d}_{n}", c) for d in range(DIRS) for n, c in (("t0", inv_items), ("t1", inv_items), ("s", 2), ("y", 2))]
            + [("bonus", 1), ("gate", 2), ("mixT", 4), ("wout", 4), ("ln2", 4), ("route1", 1), ("rank1", 1),
               ("att", 4), ("lat", 2), ("q_up", 4), ("kv_up", 4), ("heads", 3 * NH), ("wout2", 4),
               ("dffn", 4), ("ffn", 4 * NFC), ("ssm", 4), ("u", 2), ("s5", 24), ("glu", 4),
               ("moe", 4), ("route2", 1), ("rank2", 1)])
        S_ = Ring(psum[4:8], s_filled, s_emptied, [
            ("gl_qk", 2), ("gl_v", 2), ("gl_g", 1), ("gl_og", 2), ("gl0_kt", 1), ("gl1_kt", 1),
            ("vt", 2)]
            + [(f"rw{d}_{n}", c) for d in range(DIRS) for n, c in (("lora", 4), ("t0", 8), ("t1", 8))]
            + [("lat", 2), ("sqk", 4), ("sv", 2), ("headsT", 8)]
            + [("pair", 4 * HP)]
            + [("ffn", 4 * NFC), ("glu", 4)])

        class Experts:

            def __init__(self, name, count, nfc, used, last_s, twos=None):
                self.name, self.count, self.nfc, self.used, self.last_s = name, count, nfc, used, last_s
                self.twos = twos
                self.pair = name == "twos"
                self.hid_filled, self.hid_emptied = sem(name + "_hid_filled"), sem(name + "_hid_emptied")
                self.out_filled, self.out_emptied = sem(name + "_out_filled"), sem(name + "_out_emptied")
                self.dense_silu = sem(name + "_dense_silu")
                self.x_filled, self.x_emptied = sem(name + "_x_filled"), sem(name + "_x_emptied")
                self.y_filled, self.y_emptied = sem(name + "_y_filled"), sem(name + "_y_emptied")
                self.z_filled, self.z_emptied = sem(name + "_z_filled"), sem(name + "_z_emptied")
                self.silu, self.sel_ready = sem(name + "_silu"), sem(name + "_sel_ready")
                self.sel_weighted = sem(name + "_sel_weighted")
                full = self.items(False, False)
                self.len = len(full)
                self.first_len = len(self.items(True, False))
                self.back = {n: i - self.len for i, n in enumerate(full)}

            def items(self, first, last):
                if self.pair:
                    return ["gate0", "up0"] + ["ga", "gb"] * (not last) + ["hT0", "selT"]
                out = []
                for c in range(self.nfc):
                    out += [f"gate{c}"] + [f"hT{c}"] * (not (first and c == 0)) + [f"up{c}"]
                    if c == self.nfc - 1 and not last:
                        out += ["ga", "gb"]
                    if c == min(1, self.nfc - 1):
                        out += ["selT"]
                return out

            def walk(self, eng, expert):
                expert(0, 0, 2, True, False)
                base = 2 + self.first_len
                with eng.Fori(0, self.count // 2 - 1) as i:
                    expert(i, 1, base + 2 * self.len * i, False, False)
                    expert(i, 2, base + 2 * self.len * i + self.len, False, False)
                i = self.count // 2 - 1
                expert(i, 1, base + 2 * self.len * i, False, True)
                return base + 2 * self.len * i + self.len - 2

            def phase(self, k, first):
                return 2 if first else (2 + self.first_len + (self.len if k == 2 else 0)) % 4


        loads, uses = {}, [0] * 6

        def use(name, i):
            uses[i] += 1
            loads[name] = (i, uses[i])

        for n, i in (("g0", 0), ("g1", 1), ("g2", 2), ("g3", 0), ("r0", 1), ("r1", 2), ("r2", 0), ("r3", 1),
                     ("o0", 2), ("o1", 0)):
            use(n, i)
        moe1_use = list(uses)
        uses = [u + N_E1 // 2 for u in uses]
        for n, i in (("a3", 0), ("a0", 1), ("a1", 2), ("a2", 3), ("p0", 4), ("p1", 5)):
            use(n, i)
        for u in range(NFC):
            for j in range(3):
                use(f"f{u}_{j}", 3 * (u % 2) + j)
        for n, i in (("s0", 3), ("s1", 4), ("s2", 5)):
            use(n, i)
        moe2_use = list(uses)

        moe1_twos = Experts("twos", N_E1 // 2, 1, moe1_use, S_.at["rw1_t1"] + 7)
        moe1 = Experts("moe1", N_E1, 1, moe1_use, S_.at["rw1_t1"] + 7, moe1_twos)
        moe2 = Experts("moe2", N_E2, NFC, moe2_use, S_.at["glu"] + 3)

        def either(eng, x, dense, gathered):
            eng.wait_ge(route_known, 1 if x is moe1 else 2)
            flag = eng.value_load(over[0:1, 0:1], min_val=0, max_val=2)
            with eng.If(flag > 1):
                dense(x)
            with eng.Else():
                if x.twos is None:
                    gathered(x)
                else:
                    with eng.If(flag > 0):
                        gathered(x)
                    with eng.Else():
                        gathered(x.twos)

        def scores_item(kind, h):
            return V.at["heads"] + 3 * h + ("stick", "latent", "sums").index(kind)

        def pair_item(kind, hp):
            return S_.at["pair"] + 4 * hp + ("turned0", "turned1", "stick", "latent").index(kind)

        def s5_item(kind, i):
            return V.at["s5"] + (2 * i + max(i - 1, 0) if kind == "in" else (23 if i == 7 else 3 * i + 4))

        def arrived(eng, name):
            i, n = loads[name]
            eng.wait_ge(slot_in[i], 16 * n)
            return slot[i]

        win = a["w_in"][0].rearrange("(t p) n -> p t n", p=P)
        ROOTS = ["ln1", "gla", "kk", "gn", "ln2", "lnf", "att", "lat", "heads", "dffn", "ssm", "moe"]
        NORMS = ["ln1", "ln2", "att", "dffn", "ssm", "moe"]
        block = ctx.enter_context(nc.Block())

        @block.sync
        def _(sp):
            def load(name, src, ring=None, item=None):
                if isinstance(ring, Ring):
                    sp.wait_ge(ring.filled, item + 1)
                elif ring is not None:
                    sp.wait_ge(ring, item)
                i, n = loads[name]
                sp.dma_start(slot[i][:, 0:src.shape[1], 0:src.shape[2]], src).then_inc(slot_in[i], 16)

            sp.dma_start(x_sb[:], a["x"][0].rearrange("(t p) d -> p t d", p=P)).then_inc(x_in, 16)
            sp.dma_start(par[:], a["par"]).then_inc(misc_in, 16)
            sp.dma_start(con[:], a["con"]).then_inc(misc_in, 16)
            load("g0", win[:, :, GL_Q:GL_Q + 512])
            load("g1", win[:, :, GL_V:GL_V + 512])
            load("g2", win[:, :, GL_GATE:GL_GATE + 32])
            sp.dma_start(rows[:], a["rows"].partition_broadcast(P)).then_inc(misc_in, 16)
            sp.dma_start(gw2[:], a["gw2"]).then_inc(misc_in, 16)
            load("g3", win[:, :, GL_OG:GL_OG + 512], S_, S_.at["gl_qk"] + 1)
            load("r0", win[:, :, 0:512], S_, S_.at["gl_v"] + 1)
            load("r1", win[:, :, 512:1024], S_, S_.at["gl_g"])
            load("r2", win[:, :, 1024:1536], S_, S_.at["gl_og"] + 1)
            sp.wait_ge(mixed, 1)
            sp.dma_start(w2[:], a["w2"]).then_inc(lora_in, 16)
            sp.dma_start(a2[:], a["a2"]).then_inc(lora_in, 16)
            sp.dma_start(g2[:], a["rw_g2"][0]).then_inc(lora_in, 16)
            load("r3", win[:, :, 1536:RW_COLS], V, V.at["rw_p"] + 1)
            wo = a["w_out"][0].rearrange("(t p) n -> p t n", p=P)
            load("o0", wo[:, :, 0:512], V, V.at["rw_p"] + 3)
            load("o1", wo[:, :, 512:1024], V, V.at["rw_p"] + 5)

            def unit(parity, gate, up, down, vwait, swait):
                s = 3 * parity
                if vwait is not None:
                    sp.wait_ge(gu_read, vwait)
                sp.dma_start(slot[s][:], gate.rearrange("(t p) n -> p t n", p=P)).then_inc(slot_in[s], 16)
                sp.dma_start(slot[s + 1][:], up.rearrange("(t p) n -> p t n", p=P)).then_inc(slot_in[s + 1], 16)
                if swait is not None:
                    sp.wait_ge(down_read, swait)
                sp.dma_start(slot[s + 2][:].rearrange("p a b -> p (a b)").rearrange("p (t n) -> p t n", t=4),
                             down.rearrange("(t p) n -> p t n", p=P)).then_inc(slot_in[s + 2], 16)

            g1, u1, d1 = a["moe_w_gate"][0], a["moe_w_up"][0], a["moe_w_down"][0]
            sp.wait_ge(mixed, 2)
            sp.wait_ge(v_filled, V.at["wout"] + 4)
            sp.dma_start(wr[:, :, 0:36], a["wr1"].rearrange("(t p) n -> p t n", p=P)).then_inc(router_in, 16)

            def pair_of_units(experts_, free):
                for part in range(3):
                    if free is not None and part != 1:
                        sp.wait_ge(down_read if part else gu_read, free)
                    for m, e in enumerate(experts_):
                        w = (g1, u1, d1)[part][bass.ds(e, 1), :, :].rearrange("o k n -> (o k) n") \
                            if free is not None else (g1, u1, d1)[part][e]
                        o = slot[3 * m + part]
                        if part == 2:
                            sp.dma_start(o[:].rearrange("p a b -> p (a b)").rearrange("p (t n) -> p t n", t=4),
                                         w.rearrange("(t p) n -> p t n", p=P)).then_inc(slot_in[3 * m + part], 16)
                        else:
                            sp.dma_start(o[:], w.rearrange("(t p) n -> p t n", p=P)).then_inc(slot_in[3 * m + part], 16)

            pair_of_units((0, 1), None)
            with sp.Fori(1, N_E1 // 2) as i:
                pair_of_units((2 * i, 2 * i + 1), 2 * i)
            aw = a["att_w_in_2"][0].rearrange("(t p) n -> p t n", p=P)
            load("a3", aw[:, :, 1536:1952], gu_read, N_E1)
            load("a0", aw[:, :, 0:512])
            load("a1", aw[:, :, 512:1024], down_read, N_E1)
            load("a2", aw[:, :, 1024:1536])
            ow = a["att_w_out_2"][0].rearrange("(t p) n -> p t n", p=P)
            load("p0", ow[:, :, 0:512])
            load("p1", ow[:, :, 512:1024])
            sp.wait_ge(mixed, 3)
            sp.dma_start(wq_up[:], a["att_w_q_up_2"][0].rearrange("(t p) n -> p t n", p=P)).then_inc(up_in, 16)
            sp.dma_start(wkv_up[:], a["att_w_kv_up_2"][0]).then_inc(up_in, 16)
            fg, fu, fd = a["dffn_w_gate_2"][0], a["dffn_w_up_2"][0], a["dffn_w_down_2"][0]
            for u in range(NFC):
                c = slice(u * FC, u * FC + FC)
                if u == 0:
                    vw, sw = None, None
                    sp.wait_ge(s_filled, S_.at["sqk"] + 4)
                elif u == 1:
                    vw, sw = None, None
                    sp.wait_ge(v_filled, V.at["wout2"] + 4)
                    sp.dma_start(bT[:], a["bT"]).then_inc(ssm_in, 16)
                    sp.dma_start(cT[:], a["cT"]).then_inc(ssm_in, 16)
                else:
                    vw, sw = N_E1 + u - 1, N_E1 + u - 1
                unit(u % 2, fg[:, c], fu[:, c], fd[c, :], vw, sw)
            load("s0", a["ssm_w_in_2"][0].rearrange("(t p) n -> p t n", p=P), gu_read, N_E1 + NFC - 1)
            glu = a["ssm_w_glu_2"][0].rearrange("(t p) n -> p t n", p=P)
            for n, k in (("s1", 0), ("s2", 1)):
                i, _ = loads[n]
                sp.wait_ge(down_read, N_E1 + NFC - 1)
                sp.dma_start(slot[i][:].rearrange("p a b -> p (a b)").rearrange("p (t n) -> p t n", t=4),
                             glu[:, :, k * D:k * D + D]).then_inc(slot_in[i], 16)
            g2_, u2_, d2_ = a["moe_w_gate_2"][0], a["moe_w_up_2"][0], a["moe_w_down_2"][0]
            unit(0, g2_[0][:, 0:FC], u2_[0][:, 0:FC], d2_[0][0:FC, :], N_E1 + NFC, N_E1 + NFC)
            sp.wait_ge(v_emptied, V.at["glu"] + 4)
            sp.wait_ge(s_filled, S_.at["glu"] + 4)
            unit(1, g2_[0][:, FC:2 * FC], u2_[0][:, FC:2 * FC], d2_[0][FC:2 * FC, :], None, None)
            sp.dma_start(wr[:, :, 0:8], a["moe_router_2"][0].rearrange("(t p) n -> p t n", p=P)).then_inc(router_in, 16)
            with sp.Fori(1, N_E2 * NFC // 2) as i:
                for s in range(2):
                    n = 2 * i + s
                    e, c = n // NFC, (n % NFC) * FC
                    unit(s, g2_[bass.ds(e, 1), :, bass.ds(c, FC)].rearrange("o k n -> (o k) n"),
                         u2_[bass.ds(e, 1), :, bass.ds(c, FC)].rearrange("o k n -> (o k) n"),
                         d2_[bass.ds(e, 1), bass.ds(c, FC), :].rearrange("o k n -> (o k) n"),
                         N_E1 + NFC + n - 1, N_E1 + NFC + n - 1)
            sp.wait_ge(out_ready, 1)
            sp.dma_start(out[0].rearrange("(t p) d -> p t d", p=P), x_sb[:]).then_inc(out_done, 16)
            sp.wait_ge(out_done, 16)

        @block.tensor
        def _(pe):
            def mm(o, l, r, start=True, stop=True):
                return nc.tensor.matmul(o, l, r, start=start, stop=stop)

            def turn(n):
                for j in range(4):
                    b = V.claim(pe, n + j)
                    for k in range(2):
                        for t in range(TT):
                            c = (2 * j + k) * P
                            last = nc.tensor.transpose(b[:, k * T + t * P:k * T + t * P + P],
                                                       xn[:, t, c:c + P], ident)
                    last.then_inc(V.filled, 1)

            def project_T(o, w, c, width=P):
                for k in range(KT):
                    last = mm(o, w[:, k, c:c + width], hT[:, k, :], k == 0, k == KT - 1)
                return last

            def project(o, w, t, c, n):
                for k in range(KT):
                    last = mm(o, hT[:, k, t * P:t * P + P], w[:, k, c:c + n], k == 0, k == KT - 1)
                return last

            pe.wait_ge(misc_in, 64)
            pe.wait_ge(normed, 1)
            turn(V.at["ln1"])
            V.landed(pe, V.at["ln1"] + 3)
            w = arrived(pe, "g0")
            for j in range(2):
                b = S_.claim(pe, S_.at["gl_qk"] + j)
                for k in range(2):
                    last = project_T(b[:, k * T:k * T + T], w, (2 * j + k) * P)
                last.then_inc(S_.filled, 1)
            w = arrived(pe, "g1")
            for t in range(TT):
                project(S_.claim(pe, S_.at["gl_v"] + t)[:, :], w, t, 0, 512).then_inc(S_.filled, 1)
            w = arrived(pe, "g2")
            project_T(S_.claim(pe, S_.at["gl_g"])[0:32, 0:T], w, 0, 32).then_inc(S_.filled, 1)
            w = arrived(pe, "g3")
            for t in range(TT):
                project(S_.claim(pe, S_.at["gl_og"] + t)[:, :], w, t, 0, 512).then_inc(S_.filled, 1)
            S_.landed(pe, S_.at["gl_g"])
            for d in range(DIRS):
                b = V.claim(pe, V.at["gl_z"] + d)
                for k in range(2):
                    last = mm(b[:, k * T:k * T + T], gw2[:, d, k * P:k * P + P], glT[:, :])
                last.then_inc(V.filled, 1)

            for d in range(DIRS):
                order = list(range(NCH))[::1 - 2 * d]
                pe.wait_ge(gl_ops, 2 * d + 1)
                b = S_.claim(pe, S_.at[f"gl{d}_kt"])
                for t in range(TT):
                    for k in range(2):
                        last = nc.tensor.transpose(b[:, t * T + k * P:t * T + k * P + P],
                                                   gKh[:, k, t * P:t * P + P], ident)
                last.then_inc(S_.filled, 1)
                for e in range(2):
                    b = V.claim(pe, V.at[f"gl{d}_q"] + e)
                    o = 64 * e
                    for t in range(TT):
                        for k in range(2):
                            q = (2 * t + k) * P
                            last = mm(b[:, q:q + P], gK[o:o + 64, k, t * P:t * P + P],
                                      gR[o:o + 64, k, t * P:t * P + P])
                    last.then_inc(V.filled, 1)
                S_.landed(pe, S_.at[f"gl{d}_kt"])
                for c in range(2):
                    b = V.claim(pe, V.at[f"gl{d}_h"] + c)
                    for t in range(TT):
                        for h in range(4):
                            o = 64 * (h % 2)
                            last = mm(b[o:o + 64, t * 256 + (h // 2) * P:t * 256 + (h // 2) * P + P],
                                      gKt[64 * c:64 * c + 64, t, h * 64:h * 64 + 64],
                                      Vg[64 * c:64 * c + 64, t, h * P:h * P + P])
                    last.then_inc(V.filled, 1)
                pe.wait_ge(gl_ops, 2 * d + 2)
                for e in range(2):
                    b = V.claim(pe, V.at[f"gl{d}_y"] + e)
                    o = 64 * e
                    for t in range(TT):
                        for k in range(2):
                            h, q = 2 * k + e, (2 * t + k) * P
                            for c in range(2):
                                g = 2 * t + c
                                first = g == order[0]
                                last = mm(b[64 * c:64 * c + 64, q:q + P], gQ[:, t, h, 64 * c:64 * c + 64],
                                          Vg[:, t, h * P:h * P + P], True, first)
                                if not first:
                                    last = mm(b[64 * c:64 * c + 64, q:q + P], gR[o:o + 64, k, g * 64:g * 64 + 64],
                                              gS[o:o + 64, g, k, :], False, True)
                    last.then_inc(V.filled, 1)

            for j in range(8):
                w = arrived(pe, f"r{j // 2}")
                b = V.claim(pe, V.at["rw_p"] + j)
                for k in range(2):
                    c = 2 * j + k
                    if c < 15:
                        last = project_T(b[:, k * T:k * T + T], w, (c % 4) * P)
                last.then_inc(V.filled, 1)
            pe.wait_ge(shifted, 8)
            for t in range(TT):
                b = S_.claim(pe, S_.at["vt"] + t)
                for k in range(4):
                    last = nc.tensor.transpose(b[:, k * P:k * P + P], pT[:, 8 + k, t * P:t * P + P], ident)
                last.then_inc(S_.filled, 1)
            pe.wait_ge(kk_sq, 1)
            for j in range(2):
                b = V.claim(pe, V.at["kk"] + j)
                for k in range(2):
                    last = mm(b[:, k * T:k * T + T], cst("headones"), kds[:, 2 * j + k, :])
                last.then_inc(V.filled, 1)
            pe.wait_ge(lora_in, 48)
            pe.wait_ge(lora_act, 2)

            for d in range(DIRS):
                order = list(range(NCH))[::1 - 2 * d]
                lo = 64 * d
                for i, (wt, src) in enumerate(((w2, 12), (a2, 13))):
                    for j in range(2):
                        b = S_.claim(pe, S_.at[f"rw{d}_lora"] + 2 * i + j)
                        for k in range(2):
                            c = (2 * j + k) * P
                            last = mm(b[:, k * T:k * T + T], wt[lo:lo + 64, c:c + P], pT[lo:lo + 64, src, :])
                        last.then_inc(S_.filled, 1)
                pe.wait_ge(rw_ops, d + 1)
                for t in range(TT):
                    v, s = V.at[f"rw{d}_t{t}"], S_.at[f"rw{d}_t{t}"]
                    tk = slice(t * P, t * P + P)
                    for j in range(3):
                        b = S_.claim(pe, s + j)
                        for k in range(4):
                            src = AR[:, k, t, 0, :] if j == 0 else BKh[:, j - 1, k, tk]
                            last = nc.tensor.transpose(b[:, k * P:k * P + P], src, ident)
                        last.then_inc(S_.filled, 1)
                    for i in range(2):
                        for j in range(4):
                            b = V.claim(pe, v + 4 * i + j)
                            o = 64 * (j // 2)
                            for k in range(2):
                                hp = 2 * (j % 2) + k
                                last = mm(b[:, k * 256:k * 256 + 256], BK[o:o + 64, i, hp, tk],
                                          AR[o:o + 64, hp, t, :, :].rearrange("p a b -> p (a b)"))
                            last.then_inc(V.filled, 1)
                    for e in range(2):
                        b = V.claim(pe, v + 8 + e)
                        o = 64 * e
                        for k in range(4):
                            last = mm(b[:, k * P:k * P + P], AR[o:o + 64, k, t, 0, :], BK[o:o + 64, 0, k, tk])
                        last.then_inc(V.filled, 1)
                    n = v + 10
                    pe.wait_ge(inv_start, 2 * d + t + 1)
                    prev = [None, None]
                    for l in range(2, NLEV + 1):
                        wm_at = n
                        for g in range(2):
                            if prev[g] is not None:
                                V.landed(pe, prev[g])
                            b = V.claim(pe, n)
                            n += 1
                            for q in range(4):
                                h = 4 * g + q
                                last = mm(b[:, q * P:q * P + P], LN[:, h, 0, :], X[:, h, :])
                            last.then_inc(V.filled, 1)
                        for g in range(2):
                            V.landed(pe, wm_at + g)
                            if l < NLEV:
                                b = V.claim(pe, n)
                                n += 1
                                for q in range(4):
                                    h = 4 * g + q
                                    last = mm(b[:, q * P:q * P + P], XT[:, h, :], WM[:, h, :])
                                last.then_inc(V.filled, 1)
                            b = V.claim(pe, n)
                            for q in range(4):
                                h = 4 * g + q
                                last = mm(b[:, q * P:q * P + P], WM[:, h, :], XT[:, h, :])
                            last.then_inc(V.filled, 1)
                            prev[g] = n
                            n += 1
                    if d == 0 and t == 0:
                        S_.landed(pe, S_.at["vt"] + 1)
                    V.landed(pe, v + 9)
                    b = S_.claim(pe, s + 3)
                    for h in range(NH):
                        last = mm(b[:, h * 64:h * 64 + 64], MQ[:, h, 0, :], Vt[:, t, h * 64:h * 64 + 64])
                    last.then_inc(S_.filled, 1)
                    S_.landed(pe, s + 3)
                    for g in range(2):
                        V.landed(pe, prev[g])
                        b = S_.claim(pe, s + 4 + g)
                        for q in range(4):
                            h = 4 * g + q
                            last = mm(b[:, q * P:q * P + P], XT[:, h, :], AM[:, h, :])
                        last.then_inc(S_.filled, 1)
                    S_.landed(pe, s + 5)
                    b = V.claim(pe, n)
                    for h in range(NH):
                        o = 64 * (h % 2)
                        last = mm(b[o:o + 64, (h // 2) * P:(h // 2) * P + P], TAM[:, h, 0:64], LN[:, h, 1, :])
                    last.then_inc(V.filled, 1)
                    for c in range(2):
                        b = V.claim(pe, n + 1 + c)
                        r = slice(64 * c, 64 * c + 64)
                        for h in range(NH):
                            o = 64 * (h % 2)
                            q = (h // 2) * 64
                            last = mm(b[o:o + 64, q:q + 64], TAM[r, h, 0:64], BKt[r, 0, h * 64:h * 64 + 64])
                        last.then_inc(V.filled, 1)
                    for c in range(2):
                        b = S_.claim(pe, s + 6 + c)
                        r = slice(64 * c, 64 * c + 64)
                        for h in range(NH):
                            o = 64 * (h % 2)
                            q = (h // 2) * 64
                            mm(b[o:o + 64, q:q + 64], BKt[r, 1, h * 64:h * 64 + 64],
                               Vt[r, t, h * 64:h * 64 + 64], True, False)
                            last = mm(b[o:o + 64, q:q + 64], BKt[r, 0, h * 64:h * 64 + 64],
                                      TAM[r, h, 64:128], False, True)
                        last.then_inc(S_.filled, 1)
                    n += 1
                    b = V.claim(pe, n + 2)
                    for h in range(NH):
                        c = slice(h * 64, h * 64 + 64)
                        mm(b[:, c], MQ[:, h, 1, :], Vt[:, t, c], True, False)
                        last = mm(b[:, c], LN[:, h, 1, :], TAM[:, h, 64:128], False, True)
                    last.then_inc(V.filled, 1)
                    V.landed(pe, n + 2)
                S_.landed(pe, S_.at[f"rw{d}_t1"] + 7)
                for i in range(2):
                    c0 = order[i + 1]
                    src = Hc[:, order[0]] if i == 0 else S[:, c0]
                    if i:
                        V.landed(pe, V.at[f"rw{d}_s"] + i - 1)
                    b = V.claim(pe, V.at[f"rw{d}_s"] + i)
                    for h in range(NH):
                        o = 64 * (h % 2)
                        last = mm(b[o:o + 64, (h // 2) * 64:(h // 2) * 64 + 64], GT[o:o + 64, c0, h // 2, :],
                                  src[o:o + 64, h // 2, :])
                    last.then_inc(V.filled, 1)
                V.landed(pe, V.at[f"rw{d}_s"] + 1)
                for e in range(2):
                    b = V.claim(pe, V.at[f"rw{d}_y"] + e)
                    o = 64 * e
                    for g in order[1:]:
                        t, c = g // 2, g % 2
                        src = Hc[:, order[0]] if g == order[1] else S[:, g]
                        for k in range(4):
                            last = mm(b[64 * c:64 * c + 64, t * 256 + k * 64:t * 256 + k * 64 + 64],
                                      Rf[o:o + 64, t, k, 64 * c:64 * c + 64], src[o:o + 64, k, :])
                    last.then_inc(V.filled, 1)
            pe.wait_ge(kk_sq, 2)
            b = V.claim(pe, V.at["bonus"])
            for t in range(TT):
                for k in range(4):
                    last = mm(b[:, t * NH + 2 * k:t * NH + 2 * k + 2], kds[:, k, t * P:t * P + P],
                              cst("headones")[:, 0:128:64])
            last.then_inc(V.filled, 1)
            for t in range(TT):
                b = V.claim(pe, V.at["gate"] + t)
                mm(b[:, :], pT[:, 14, t * P:t * P + P], g2[:, :]).then_inc(V.filled, 1)

            pe.wait_ge(mixed, 2)
            turn(V.at["mixT"])
            V.landed(pe, V.at["mixT"] + 3)

            def out_proj(names, n):
                for c, name in enumerate(names):
                    w = arrived(pe, name)
                    for t in range(TT):
                        project(V.claim(pe, n + 2 * c + t)[:, :], w, t, 0, 512).then_inc(V.filled, 1)

            out_proj(("o0", "o1"), V.at["wout"])

            def expert(parity, loaded, hid, out_, vn, sn):
                vf, ve, vp = hid
                sf, se, sp_ = out_
                gate, up, down = slot[3 * parity:3 * parity + 3]
                down = down[:].rearrange("p a b -> p (a b)").rearrange("p (t n) -> p t n", t=4)
                pe.wait_ge(slot_in[3 * parity], 16 * loaded[0])
                pe.wait_ge(slot_in[3 * parity + 1], 16 * loaded[1])
                for f in range(4):
                    pe.wait_ge(ve, vn + f - 3)
                    b = V.bank(vp + f)
                    project_T(b[:, 0:T], gate, f * P)
                    project_T(b[:, T:2 * T], up, f * P).then_inc(vf, 1)
                pe.wait_ge(slot_in[3 * parity + 2], 16 * loaded[2])
                pe.wait_ge(ve, vn + 4)
                for t in range(TT):
                    for c in range(2):
                        pe.wait_ge(se, sn + 2 * t + c - 3)
                        b = S_.bank(sp_ + 2 * t + c)
                        for f in range(4):
                            last = mm(b[:, :], hact[:, parity, f, t * P:t * P + P],
                                      down[:, f, c * 512:c * 512 + 512], f == 0, f == 3)
                        last.then_inc(sf, 1)

            def dense(x):
                with pe.Fori(0, x.count * x.nfc // 2) as i:
                    for s in range(2):
                        k = [x.used[3 * s + j] + i + 1 for j in range(3)]
                        expert(s, k, (x.hid_filled, x.hid_emptied, 0), (x.out_filled, x.out_emptied, 0),
                               8 * i + 4 * s + 4, 8 * i + 4 * s + 4)

            def gathered(x):
                columns = [(m, slice(m * HALF, m * HALF + HALF)) for m in range(2)] if x.pair else [(0, slice(0, CAP))]

                def hidden(bank, b, half, parity, arrived_):
                    js = (half, 3 + half) if x.pair else (3 * parity + half,)
                    for j, count in zip(js, arrived_):
                        pe.wait_ge(slot_in[j], 16 * count)
                    for q in range(KT):
                        for m, c_ in columns:
                            last = mm(psum[bank % 4][c_, :], xgT[:, b, q, c_], slot[js[m]][:, q, :], q == 0, q == KT - 1)
                    last.then_inc(x.x_filled, 1)

                def gather(n, b, bank):
                    for j in range(2):
                        if n is not None:
                            pe.wait_ge(x.x_emptied, n + j - 3)
                        o = psum[(bank + j) % 4]
                        for k in range(4):
                            c = (4 * j + k) * P
                            for t in range(TT):
                                last = mm(o[:, k * CAP:k * CAP + CAP], xn[:, t, c:c + P], sel[:, b, t, :],
                                          t == 0, t == 1)
                        last.then_inc(x.x_filled, 1)

                def turn_hidden(n, bank, up_item):
                    pe.wait_ge(x.x_emptied, up_item + 1)
                    o = psum[bank % 4]
                    for f in range(4):
                        last = nc.tensor.transpose(o[:, f * CAP:f * CAP + CAP], hsb[:, f * P:f * P + P], ident)
                    last.then_inc(x.x_filled, 1)

                def down_proj(n, c, parity, arrived_, before):
                    js = (2, 5) if x.pair else (3 * parity + 2,)
                    w = [slot[j][:].rearrange("p a b -> p (a b)").rearrange("p (t n) -> p t n", t=4) for j in js]
                    for j, count in zip(js, arrived_):
                        pe.wait_ge(slot_in[j], 16 * count)
                    pe.wait_ge(x.x_emptied, n + 1)
                    if c == 0 and before is not None:
                        pe.wait_ge(x.y_emptied, 2 * before + 2)
                    for h in range(2):
                        for f in range(4):
                            for m, c_ in columns:
                                last = mm(psum[4 + h][c_, :], hTs[:, f, c_], w[m][:, f, h * 512:h * 512 + 512],
                                          c == 0 and f == 0, c == x.nfc - 1 and f == 3)
                        if c == x.nfc - 1:
                            last.then_inc(x.y_filled, 1)
                    if c < x.nfc - 1:
                        last.then_inc(down_read, 1)

                def scatter(e):
                    pe.wait_ge(x.y_emptied, 2 * e + 4)
                    for j in range(4):
                        pe.wait_ge(x.z_emptied, 4 * e + j + 1)
                        t, c = j // 2, j % 2
                        mm(psum[6 + j % 2][:, :], selT[:, t * P:t * P + P],
                           yacc[:, c * 512:c * 512 + 512]).then_inc(x.z_filled, 1)

                def loaded(i, k, c, j):
                    if x.pair:
                        return [x.used[3 * m + j] + 2 * i + k + 1 for m in range(2)]
                    u = k * x.nfc + c
                    return [x.used[3 * (u % 2) + j] + x.nfc * i + u // 2 + 1]

                def one(i, k, base, first, last):
                    at = {n: j for j, n in enumerate(x.items(first, last))}
                    ph = x.phase(k, first)
                    b = k % 2
                    e = 2 * i + k
                    for c in range(x.nfc):
                        par = (k * x.nfc + c) % 2
                        n = base + at[f"gate{c}"]
                        if c == 0:
                            pe.wait_ge(x.x_emptied, 2 if first else base + x.back["gb"] + 1)
                        if not (first and c == 0):
                            pe.wait_ge(x.x_emptied, n - 3)
                        hidden(ph + at[f"gate{c}"], b, 0, par, loaded(i, k, c, 0))
                        if f"hT{c}" in at:
                            n = base + at[f"hT{c}"]
                            pe.wait_ge(x.x_emptied, n - 3)
                            turn_hidden(n, ph + at[f"hT{c}"],
                                        base + (at[f"up{c - 1}"] if c else x.back[f"up{x.nfc - 1}"]))
                        n = base + at[f"up{c}"]
                        if not (first and c == 0):
                            pe.wait_ge(x.x_emptied, n - 3)
                        hidden(ph + at[f"up{c}"], b, 1, par, loaded(i, k, c, 1))
                        if f"hT{c}" in at:
                            ki, cc = (k, c - 1) if c else (k - 1, x.nfc - 1)
                            down_proj(base + at[f"hT{c}"], cc, 1 - par,
                                      loaded(i, ki, cc, 2), (e if c else e - 1) if not first else None)
                        if c == x.nfc - 1 and not last:
                            pe.wait_ge(x.sel_ready, e + 2)
                            gather(base + at["ga"], 1 - b, ph + at["ga"])
                        if c == min(1, x.nfc - 1):
                            if not first:
                                scatter(e - 1)
                            pe.wait_ge(x.x_emptied, base + at["selT"] - 3)
                            o = psum[(ph + at["selT"]) % 4]
                            for t in range(TT):
                                r = nc.tensor.transpose(o[:, t * P:t * P + P], sel[:, b, t, :], ident)
                            r.then_inc(x.x_filled, 1)

                def one_pair(i, k, base, first, last):
                    at = {n: j for j, n in enumerate(x.items(first, last))}
                    ph, b, e = x.phase(k, first), k % 2, 2 * i + k
                    pe.wait_ge(x.x_emptied, base)
                    hidden(ph + at["gate0"], b, 0, 0, loaded(i, k, 0, 0))
                    if not first:
                        scatter(e - 1)
                        pe.wait_ge(x.x_emptied, base + at["up0"] - 3)
                    hidden(ph + at["up0"], b, 1, 0, loaded(i, k, 0, 1))
                    if not last:
                        pe.wait_ge(x.sel_ready, e + 2)
                        gather(base + at["ga"], 1 - b, ph + at["ga"])
                    n = base + at["hT0"]
                    pe.wait_ge(x.x_emptied, n - 3)
                    turn_hidden(n, ph + at["hT0"], base + at["up0"])
                    down_proj(n, 0, 0, loaded(i, k, 0, 2), None if first else e)
                    pe.wait_ge(x.x_emptied, base + at["selT"] - 3)
                    pe.wait_ge(x.sel_weighted, e + 1)
                    o = psum[(ph + at["selT"]) % 4]
                    for t in range(TT):
                        r = nc.tensor.transpose(o[:, t * P:t * P + P], sel[:, b, t, :], ident)
                    r.then_inc(x.x_filled, 1)

                pe.wait_ge(x.sel_ready, 1)
                gather(None, 0, 0)
                if x.pair:
                    pe.wait_ge(x.x_emptied, x.walk(pe, one_pair))
                    scatter(x.count - 1)
                    return
                n = x.walk(pe, one)
                pe.wait_ge(x.x_emptied, n - 3)
                up_item = n - len(x.items(False, True)) + x.items(False, True).index(f"up{x.nfc - 1}")
                turn_hidden(n, x.phase(1, False) + len(x.items(False, True)), up_item)
                i = x.count // 2 - 1
                down_proj(n, x.nfc - 1, (x.nfc + x.nfc - 1) % 2, loaded(i, 1, x.nfc - 1, 2), x.count - 1)
                scatter(x.count - 1)

            def experts(x, rank_item):
                pe.wait_ge(ranked, 1 if x is moe1 else 2)
                b = V.claim(pe, rank_item)
                n = x.count
                mm(b[:, 0:n], cst("before"), msk[:, 0, 0:n])
                mm(b[:, n:2 * n], cst("before"), msk[:, 1, 0:n], True, False)
                mm(b[:, n:2 * n], cst("ones"), msk[:, 0, 0:n], False, True)
                mm(b[:, 2 * n:3 * n], cst("ones"), msk[:, 0, 0:n], True, False)
                mm(b[:, 2 * n:3 * n], cst("ones"), msk[:, 1, 0:n], False, True).then_inc(V.filled, 1)
                V.landed(pe, rank_item)
                S_.landed(pe, x.last_s)
                either(pe, x, dense, gathered)

            pe.wait_ge(normed, 2)
            turn(V.at["ln2"])
            V.landed(pe, V.at["ln2"] + 3)
            pe.wait_ge(router_in, 16)
            b = V.claim(pe, V.at["route1"])
            for t in range(TT):
                last = project(b[:, t * 36:t * 36 + 36], wr, t, 0, 36)
            last.then_inc(V.filled, 1)
            experts(moe1, V.at["rank1"])

            pe.wait_ge(normed, 3)
            turn(V.at["att"])
            V.landed(pe, V.at["att"] + 3)
            w = arrived(pe, "a3")
            for t in range(TT):
                project(S_.claim(pe, S_.at["lat"] + t)[:, 0:416], w, t, 0, 416).then_inc(S_.filled, 1)
            for i in range(2):
                w = arrived(pe, f"a{i}")
                for j in range(2):
                    b = S_.claim(pe, S_.at["sqk"] + 2 * i + j)
                    for k in range(2):
                        last = project_T(b[:, k * T:k * T + T], w, (2 * j + k) * P)
                    last.then_inc(S_.filled, 1)
            pe.wait_ge(lat_ready, 1)
            for j in range(2):
                b = V.claim(pe, V.at["lat"] + j)
                for k in range(2 - j):
                    for t in range(TT):
                        c = (2 * j + k) * P
                        last = nc.tensor.transpose(b[:, k * T + t * P:k * T + t * P + P], lat[:, t, c:c + P], ident)
                last.then_inc(V.filled, 1)
            V.landed(pe, V.at["lat"] + 1)
            pe.wait_ge(up_in, 32)
            for t in range(TT):
                for c in range(2):
                    b = V.claim(pe, V.at["q_up"] + 2 * t + c)
                    for k in range(2):
                        last = mm(b[:, 0:384], latT[:, k, t * P:t * P + P], wq_up[:, k, c * 384:c * 384 + 384],
                                  k == 0, k == 1)
                    last.then_inc(V.filled, 1)
            for t in range(TT):
                for c in range(2):
                    b = V.claim(pe, V.at["kv_up"] + 2 * t + c)
                    mm(b[:, :], latT[:, 2, t * P:t * P + P], wkv_up[:, c * 512:c * 512 + 512]).then_inc(V.filled, 1)
            w = arrived(pe, "a2")
            for t in range(TT):
                project(S_.claim(pe, S_.at["sv"] + t)[:, :], w, t, 0, 512).then_inc(S_.filled, 1)
            pe.wait_ge(heads_ready, 1)
            for i, src in enumerate((qh, kh)):
                for j in range(4):
                    b = S_.claim(pe, S_.at["headsT"] + 4 * i + j)
                    for k in range(2):
                        for t in range(TT):
                            last = nc.tensor.transpose(b[0:MQK, k * T + t * P:k * T + t * P + P],
                                                       src[:, t, 2 * j + k, :], ident)
                    last.then_inc(S_.filled, 1)
            def scores(h):
                o, hp = 64 * (h % 2), h // 2
                b = V.claim(pe, scores_item("stick", h))
                mm(b[:, 0:T], sqkT[o:o + 64, 4 + hp, 0:P], sqkT[o:o + 64, hp, :])
                mm(b[:, T:T + P], sqkT[o:o + 64, 4 + hp, P:T], sqkT[o:o + 64, hp, P:T]).then_inc(V.filled, 1)
                b = V.claim(pe, scores_item("latent", h))
                mm(b[:, 0:P], qhT[:, h, 0:P], khT[:, h, 0:P])
                mm(b[:, P:3 * P], qhT[:, h, P:T], khT[:, h, :]).then_inc(V.filled, 1)

            S_.landed(pe, S_.at["headsT"] + 7)
            scores(0)
            for h in range(NH):
                o, hp = 64 * (h % 2), h // 2
                pe.wait_ge(fails, h + 1)
                b = V.claim(pe, scores_item("sums", h))
                mm(b[:, 0:P], cst("after"), lf[:, 0:P])
                mm(b[:, P:T], cst("after"), lf[:, P:T], True, False)
                mm(b[:, P:T], cst("ones"), lf[:, T:T + P], False, True)
                mm(b[:, T:T + P], cst("after"), lf[:, T:T + P]).then_inc(V.filled, 1)
                if h + 1 < NH:
                    scores(h + 1)
                pe.wait_ge(p_ready, h + 1)
                b = S_.claim(pe, pair_item(f"turned{h % 2}", hp))
                for k in range(3):
                    last = nc.tensor.transpose(b[:, k * P:k * P + P], mp[:, k * P:k * P + P], ident)
                last.then_inc(S_.filled, 1)
                if h % 2 == 0:
                    pair = S_.claim(pe, pair_item("stick", hp))
                pe.wait_ge(w_ready, h + 1)
                mm(pair[o:o + 64, 0:T], sV[:, 0, h * 64:h * 64 + 64], wT[:, 0:T], True, False)
                last = mm(pair[o:o + 64, P:T], sV[:, 1, h * 64:h * 64 + 64], wT[:, T:T + P], False, True)
                if h % 2 == 0:
                    last.then_inc(w_read, 1)
                    continue
                last.then_inc(S_.filled, 1)
                S_.landed(pe, pair_item("turned1", hp))
                b = S_.claim(pe, pair_item("latent", hp))
                for k in range(2):
                    o = 64 * k
                    src = pTt[:, k, :]
                    mm(b[o:o + 64, 0:T], mV[:, 0, h - 1 + k, :], src[:, 0:T], True, False)
                    last = mm(b[o:o + 64, P:T], mV[:, 1, h - 1 + k, :], src[:, T:T + P], False, True)
                last.then_inc(S_.filled, 1)
            S_.landed(pe, pair_item("latent", HP - 1))
            out_proj(("p0", "p1"), V.at["wout2"])

            pe.wait_ge(normed, 4)
            turn(V.at["dffn"])
            V.landed(pe, V.at["dffn"] + 3)
            for u in range(NFC):
                k = [loads[f"f{u}_{j}"][1] for j in range(3)]
                expert(u % 2, k, (V.filled, V.emptied, V.at["ffn"]), (S_.filled, S_.emptied, S_.at["ffn"]),
                       V.at["ffn"] + 4 * u, S_.at["ffn"] + 4 * u)

            pe.wait_ge(normed, 5)
            turn(V.at["ssm"])
            V.landed(pe, V.at["ssm"] + 3)
            w = arrived(pe, "s0")
            for j in range(2):
                b = V.claim(pe, V.at["u"] + j)
                for k in range(2):
                    last = project_T(b[:, k * T:k * T + T], w, (2 * j + k) * P)
                last.then_inc(V.filled, 1)
            V.landed(pe, V.at["u"] + 1)
            pe.wait_ge(ssm_in, 32)
            def s5_in(i):
                for m in range(2):
                    j = 2 * i + m
                    o = 32 * (j % 4)
                    b = V.claim(pe, s5_item("in", i) + m)
                    for k in range(2):
                        last = mm(b[:, k * T:k * T + T], bT[o:o + 32, j // 4, k, :], uT[o:o + 32, j // 4, :])
                    last.then_inc(V.filled, 1)

            s5_in(0)
            s5_in(1)
            pe.wait_ge(s5_mat, 1)
            for i in range(8):
                pe.wait_ge(s5_h, i + 1)
                b = V.claim(pe, s5_item("out", i))
                for m in range(2):
                    j = 2 * i + m
                    o = 32 * (j % 4)
                    mm(b[o:o + 32, 0:T], cT[:, j, 0, :], hst[:, m, 0, :], True, False)
                    last = mm(b[o:o + 32, 0:T], cT[:, j, 1, :], hst[:, m, 1, :], False, True)
                last.then_inc(V.filled, 1)
                if i < 6:
                    s5_in(i + 2)
            pe.wait_ge(y_gelu, 1)
            for n, name in enumerate(("s2", "s1")):
                arrived(pe, name)
            gl = [slot[loads[n][0]][:].rearrange("p a b -> p (a b)").rearrange("p (t n) -> p t n", t=4)
                  for n in ("s1", "s2")]
            for t in range(TT):
                for c in range(2):
                    for r, ring in ((1, S_), (0, V)):
                        b = ring.claim(pe, ring.at["glu"] + 2 * t + c)
                        for k in range(4):
                            last = mm(b[:, :], yT[:, k, t * P:t * P + P], gl[r][:, k, c * 512:c * 512 + 512],
                                      k == 0, k == 3)
                        last.then_inc(ring.filled, 1)

            pe.wait_ge(normed, 6)
            turn(V.at["moe"])
            V.landed(pe, V.at["moe"] + 3)
            pe.wait_ge(router_in, 32)
            b = V.claim(pe, V.at["route2"])
            for t in range(TT):
                last = project(b[:, t * 8:t * 8 + 8], wr, t, 0, 8)
            last.then_inc(V.filled, 1)
            experts(moe2, V.at["rank2"])

        @block.scalar
        def _(act):
            own = Own(act, act_own)

            def f(o, i, func, bias=0.0, scale=1.0, **k):
                return nc.scalar.activation(o, i, func, bias=bias, scale=scale, **k)

            def root(name, o, i):
                act.wait_ge(meansq, ROOTS.index(name) + 1)
                f(o, i, ACT.Sqrt).then_inc(rooted, 1)

            def empty(n, *moves):
                b = S_.take(act, n)
                for o, pick, scale in moves:
                    last = f(o, pick(b), ACT.Copy, scale=scale)
                last.then_inc(S_.emptied, 1)

            whole = lambda b: b[:, :]

            root("ln1", st[:, 4:6], st[:, 2:4])
            for j in range(2):
                empty(S_.at["gl_qk"] + j, (qkT[:, 2 * j:2 * j + 2, :].rearrange("p a b -> p (a b)"), whole,
                                           0.125 if j == 0 else 1.0))
            for t in range(TT):
                empty(S_.at["gl_v"] + t, (Vg[:, t, :], whole, 1.0))
            empty(S_.at["gl_g"], (glT[:, :], lambda b: b[0:32, 0:T], 1.0))
            for t in range(TT):
                b = S_.take(act, S_.at["gl_og"] + t)
                f(ogs[:, t, :], b[:, :], ACT.Silu).then_inc(S_.emptied, 1)
            for d in range(DIRS):
                V.landed(act, V.at["gl_z"] + d)
                own(f(ge[:, d, :], gz[:, d, :], ACT.Abs))
                own.settle()
                own(f(ge[:, d, :], ge[:, d, :], ACT.Exp, scale=-1.0))
                own.settle()
                f(ge[:, d, :], ge[:, d, :], ACT.Ln, bias=1.0).then_inc(gl_val, 1)
            for d in range(DIRS):
                end = 0 if d else CH - 1
                cend = gc[:, :, :].rearrange("p k (c s) -> p (k c) s", s=CH)[:, :, end]
                flat = gc[:, :, :].rearrange("p a b -> p (a b)")
                act.wait_ge(gl_arg, d + 1)
                f(gP[:, 0, :], flat, ACT.Exp, scale=1 / 16)
                f(gP[:, 1, :], flat, ACT.Exp, scale=-1 / 16)
                f(gP[:, 2, :], gce[:, :, :].rearrange("p a b -> p (a b)"), ACT.Exp, scale=1 / 16)
                f(gPc[:, :], cend, ACT.Exp, scale=1 / 16).then_inc(gl_val, 1)
                b = S_.take(act, S_.at[f"gl{d}_kt"])
                f(gKt[:, :, :].rearrange("p a b -> p (a b)"), b[:, :], ACT.Copy).then_inc(S_.emptied, 1)
            root("gla", st[:, 24:32], st[:, 16:24])

            act.wait_ge(shifted, 8)
            f(pT[:, 12, :], pT[:, 12, :], ACT.Tanh).then_inc(lora_act, 1)
            f(pT[:, 14, :], pT[:, 14, :], ACT.Sigmoid).then_inc(lora_act, 1)
            for t in range(TT):
                empty(S_.at["vt"] + t, (Vt[:, t, :], whole, 1.0))
            root("kk", sca[:, 2, :], sca[:, 2, :])
            for d in range(DIRS):
                for i, name in enumerate(("w0", "a0")):
                    for j in range(2):
                        b = S_.take(act, S_.at[f"rw{d}_lora"] + 2 * i + j)
                        for k in range(2):
                            c = 2 * j + k
                            last = f(sca[:, i, c * T:c * T + T], b[:, k * T:k * T + T], ACT.Sigmoid,
                                     bias=pcol(name, 4 * d + c))
                        last.then_inc(S_.emptied, 1)
                act.wait_ge(cum, d + 1)
                end = 0 if d else CH - 1
                c4 = sca[:, 2, :].rearrange("p (k t c) -> p k t c", k=4, t=TT)
                f(AR[:, :, :, 0, :], BK[:, 1, :, :].rearrange("p k (t c) -> p k t c", t=TT), ACT.Exp, scale=-EXPM)
                f(AR[:, :, :, 1, :], c4, ACT.Exp, scale=-EXPM)
                f(BK[:, 0, :, :].rearrange("p a b -> p (a b)"), sca[:, 2, :], ACT.Exp, scale=EXPM)
                f(BKh[:, 0, :, :], BKh[:, 1, :, :], ACT.Exp, scale=-EXPM)
                f(Pc[:, :], sca[:, 2, :].rearrange("p (k s) -> p k s", s=CH)[:, :, end], ACT.Exp,
                  scale=-EXPM).then_inc(cum_exp, 1)
                for t in range(TT):
                    s = S_.at[f"rw{d}_t{t}"]
                    by_head = lambda b: b[:, :].rearrange("p (h c) -> p h c", h=NH)
                    empty(s, (AM[:, :, 0:64], by_head, 1.0))
                    empty(s + 1, (BKt[:, 0, :], whole, 1.0))
                    empty(s + 2, (BKt[:, 1, :], whole, 1.0))
                    empty(s + 3, (AM[:, :, 64:128], by_head, 1.0))
                    for g in range(2):
                        empty(s + 4 + g, (TAM[:, 4 * g:4 * g + 4, :].rearrange("p a b -> p (a b)"), whole, -1.0))
                    for c in range(2):
                        empty(s + 6 + c, (Hc[:, 2 * t + c].rearrange("p a b -> p (a b)"), lambda b: b[:, 0:256], 1.0))
            root("gn", st[:, 64:80], st[:, 48:64])

            def gates(phase, n, credit, filled, emptied, done):
                for h in range(4):
                    act.wait_ge(filled, n + h + 1)
                    act.wait_ge(emptied, n + h - 1 + credit)
                    b = V.bank(phase + h)
                    f(sg[:, h % 2, :], b[:, 0:T], ACT.Silu).then_inc(done, 1)

            def dense(x):
                with act.Fori(0, x.count * x.nfc) as i:
                    gates(0, 4 * i, 4, x.hid_filled, x.hid_emptied, x.dense_silu)

            def gathered(x):
                def one(i, k, base, first, last):
                    at = {n: j for j, n in enumerate(x.items(first, last))}
                    ph = x.phase(k, first)
                    for c in range(x.nfc):
                        act.wait_ge(x.x_filled, base + at[f"gate{c}"] + 1)
                        if not (first and c == 0):
                            up = at[f"up{c - 1}"] if c else x.back[f"up{x.nfc - 1}"]
                            act.wait_ge(x.x_emptied, base + up + 1)
                        f(sgx[:, :], psum[(ph + at[f"gate{c}"]) % 4][:, :], ACT.Silu).then_inc(x.silu, 1)
                x.walk(act, one)

            root("ln2", st[:, 4:6], st[:, 2:4])
            act.wait_ge(logit_max, 1)
            for t in range(TT):
                f(lg[:, t, 0:4], lg[:, t, 0:4], ACT.Exp, bias=st[:, 10 + t:11 + t], accum_out=st[:, 12 + t:13 + t])
                f(wexp[:, t, :], lm[:, t, :], ACT.Exp, bias=st[:, 14 + t:15 + t])
                f(st[:, 18 + t:19 + t], top[:, t, 1:2], ACT.Exp, bias=st[:, 14 + t:15 + t]).then_inc(logit_exp, 1)
            either(act, moe1, dense, gathered)
            root("lnf", st[:, 4:6], st[:, 2:4])

            root("att", st[:, 4:6], st[:, 2:4])
            for t in range(TT):
                empty(S_.at["lat"] + t, (lat[:, t, :], lambda b: b[:, 0:416], 1.0))
            root("lat", st[:, 20:24], st[:, 16:20])
            for j in range(4):
                empty(S_.at["sqk"] + j, (sqkT[:, 2 * j:2 * j + 2, :].rearrange("p a b -> p (a b)"), whole,
                                         0.125 if j < 2 else 1.0))
            for t in range(TT):
                empty(S_.at["sv"] + t, (sV[:, t, :], whole, 1.0))
            root("heads", stt[:, 4:8, :], stt[:, 0:4, :])
            for i, o in enumerate((qhT, khT)):
                for j in range(4):
                    empty(S_.at["headsT"] + 4 * i + j, (o[:, 2 * j:2 * j + 2, :].rearrange("p a b -> p (a b)"),
                                                        lambda b: b[0:MQK, :], 1.0))
            def soft(h):
                act.wait_ge(z_ready, h + 1)
                own(f(za[:, 1, :], za[:, 0, :], ACT.Abs))
                own.settle()
                own(f(za[:, 1, :], za[:, 1, :], ACT.Exp, scale=-1.0))
                own.settle()
                f(za[:, 1, :], za[:, 1, :], ACT.Ln, bias=1.0).then_inc(z_soft, 1)

            def probabilities(h):
                act.wait_ge(maxed, h + 1)
                for q, c in enumerate((slice(0, P), slice(P, 3 * P))):
                    last = f(mp[:, c], mz[:, c], ACT.Exp, bias=st[:, 24 + q:25 + q], scale=MQK ** -0.5,
                             accum_out=st[:, 26 + q:27 + q])
                last.then_inc(p_exp, 1)

            soft(0)
            probabilities(0)
            for h in range(NH):
                hp = h // 2
                act.wait_ge(w_arg, h + 1)
                f(wT, za[:, 2, :], ACT.Exp).then_inc(w_exp, 1)
                if h + 1 < NH:
                    soft(h + 1)
                empty(pair_item(f"turned{h % 2}", hp), (pTt[:, h % 2, :], lambda b: b[:, 0:3 * P], 1.0))
                if h + 1 < NH:
                    probabilities(h + 1)
                if h % 2:
                    empty(pair_item("stick", hp), (hT[:, hp, :], lambda b: b[:, 0:T], 1.0))
                    empty(pair_item("latent", hp), (hT[:, 4 + hp, :], lambda b: b[:, 0:T], 1.0))

            root("dffn", st[:, 4:6], st[:, 2:4])
            p16 = lambda i: par16[:, i, :]
            f(p16(0), pcol("ldt", 0, 16), ACT.Exp).then_inc(s5_val, 1)
            for u in range(NFC):
                gates(V.at["ffn"], V.at["ffn"] + 4 * u, 0, V.filled, V.emptied, silu_done)
                if u == 1:
                    act.wait_ge(s5_arg, 1)
                    f(p16(3), p16(2), ACT.Exp)
                    f(p16(5), p16(4), ACT.Sin)
                    f(p16(7), p16(6), ACT.Sin).then_inc(s5_val, 1)
            root("ssm", st[:, 4:6], st[:, 2:4])
            act.wait_ge(y_sum, 1)
            f(yT[:, :, :], yT[:, :, :], ACT.Gelu_apprx_tanh).then_inc(y_gelu, 1)
            for t in range(TT):
                for c in range(2):
                    n = 2 * t + c
                    b = S_.take(act, S_.at["glu"] + n)
                    if n:
                        V.landed(act, V.at["glu"] + n - 1)
                    f(gsig, b[:, :], ACT.Sigmoid).then_inc(S_.emptied, 1)
            root("moe", st[:, 4:6], st[:, 2:4])
            act.wait_ge(logit_max, 2)
            for t in range(TT):
                f(wexp[:, t, 0:8], lm[:, t, 0:8], ACT.Exp, bias=st[:, 14 + t:15 + t])
                f(st[:, 18 + t:19 + t], top[:, t, 1:2], ACT.Exp, bias=st[:, 14 + t:15 + t]).then_inc(logit_exp, 1)
            either(act, moe2, dense, gathered)

        @block.vector
        def _(dve):
            own = Own(dve, dve_own)
            vec = nc.vector

            def tt(o, x, y, op):
                return vec.tensor_tensor(o, x, y, op)

            def ts(o, x, s1, op0, s2=None, op1=None):
                return vec.tensor_scalar(o, x, s1, s2, op0, op1) if op1 is not None else \
                    vec.tensor_scalar(o, x, s1, None, op0)

            def stt_(o, x, s, y, op0, op1):
                return vec.scalar_tensor_tensor(out=o, in0=x, scalar=s, in1=y, op0=op0, op1=op1)

            def do(ins):
                own(ins)
                own.settle()

            def signal(ins, s, value):
                ins.then_inc(s, 1)
                dve.wait_ge(s, value)

            def flat(x):
                return x.rearrange("p a b -> p (a b)")

            def spread(col, n):
                return col.unsqueeze(2).to_broadcast([col.shape[0], col.shape[1], n])

            def tiled(x, n):
                return x.unsqueeze(1).to_broadcast([x.shape[0], n, x.shape[1]])

            def rooted_(name):
                dve.wait_ge(rooted, ROOTS.index(name) + 1)

            def mean_square(name, i, o, n, eps):
                signal(ts(o, i, 1.0 / n, ALU.mult, eps, ALU.add), meansq, ROOTS.index(name) + 1)

            def norm(name, dst=None):
                own.settle()
                for t in range(TT):
                    own(vec.tensor_tensor_reduce(out=xn[:, t, :], in0=x_sb[:, t, :], in1=x_sb[:, t, :], scale=1.0,
                                                 scalar=0.0, op0=ALU.mult, op1=ALU.add, accum_out=st[:, t:t + 1]))
                own.settle()
                mean_square(name, st[:, 0:2], st[:, 2:4], D, EPS)
                rooted_(name)
                do(vec.reciprocal(st[:, 6:8], st[:, 4:6]))
                for t in range(TT):
                    ins = ts((dst or xn)[:, t, :], x_sb[:, t, :], st[:, 6 + t:7 + t], ALU.mult)
                    if t == 0 or dst is not None:
                        own(ins)
                if dst is None:
                    ins.then_inc(normed, 1)
                own.settle()

            def turned(n, gain=None):
                for j in range(4):
                    b = V.take(dve, n + j)
                    for k in range(2):
                        c = 2 * j + k
                        if gain:
                            last = ts(hT[:, c, :], b[:, k * T:k * T + T], pcol(gain, c), ALU.mult)
                        else:
                            last = vec.tensor_copy(hT[:, c, :], b[:, k * T:k * T + T])
                    last.then_inc(V.emptied, 1)

            def add_out(n):
                for c in range(2):
                    for t in range(TT):
                        b = V.take(dve, n + 2 * c + t)
                        o = x_sb[:, t, c * 512:c * 512 + 512]
                        tt(o, b[:, :], o, ALU.add).then_inc(V.emptied, 1)
                V.landed(dve, n + 3)

            dve.wait_ge(x_in, 16)
            norm("ln1")
            dve.wait_ge(misc_in, 64)
            turned(V.at["ln1"], "ln1")

            for d in range(DIRS):
                b = V.take(dve, V.at["gl_z"] + d)
                for k in range(2):
                    last = ts(gz[:, d, k * T:k * T + T], b[:, k * T:k * T + T], pcol("gb", 2 * d + k), ALU.add)
                last.then_inc(V.emptied, 1)
            for d in range(DIRS):
                V.landed(dve, V.at["gl_z"] + d)
                dve.wait_ge(gl_val, d + 1)
                do(stt_(gz[:, d, :], gz[:, d, :], 0.0, ge[:, d, :], ALU.min, ALU.subtract))
            for d in range(DIRS):
                order = list(range(NCH))[::1 - 2 * d]
                way = slice(None, None, -1) if d else slice(None)
                end = 0 if d else CH - 1
                for k in range(2):
                    own(vec.tensor_tensor_scan(gc[:, k, way], cst("reset", d, T)[:, way],
                                               gz[:, d, k * T:k * T + T][:, way], 0.0, ALU.mult, ALU.add))
                own.settle()
                by_chunk = gc[:, :, :].rearrange("p k (c s) -> p (k c) s", s=CH)
                tt(gce[:, :, :].rearrange("p k (c s) -> p (k c) s", s=CH), spread(by_chunk[:, :, end], CH), by_chunk,
                   ALU.subtract).then_inc(gl_arg, 1)
                S_.landed(dve, S_.at["gl_qk"] + 1)
                dve.wait_ge(gl_val, DIRS + d + 1)
                own(tt(flat(gR[:, :, :]), gP[:, 0, :], flat(qkT[:, 0:2, :]), ALU.mult))
                own(tt(flat(gK[:, :, :]), gP[:, 1, :], flat(qkT[:, 2:4, :]), ALU.mult))
                own.settle()
                tt(flat(gKh[:, :, :]), gP[:, 2, :], flat(qkT[:, 2:4, :]), ALU.mult).then_inc(gl_ops, 1)
                for e in range(2):
                    b = V.take(dve, V.at[f"gl{d}_q"] + e)
                    for t in range(TT):
                        last = tt(gQ[:, t, e:4:2, :], b[:, t * 256:t * 256 + 256].rearrange("p (h c) -> p h c", h=2),
                                  tiled(cst("mask2", 2 * d + 1, P), 2), ALU.mult)
                    last.then_inc(V.emptied, 1)
                for c in range(2):
                    b = V.take(dve, V.at[f"gl{d}_h"] + c)
                    vec.tensor_copy(gH[:, c:4:2].rearrange("p a b c -> p a (b c)"),
                                    b[:, :].rearrange("p (a b) -> p a b", a=2)).then_inc(V.emptied, 1)
                V.landed(dve, V.at[f"gl{d}_h"] + 1)
                do(vec.tensor_copy(gS[:, order[1]], gH[:, order[0]]))
                for i in (1, 2):
                    for k in range(2):
                        c = order[i]
                        ins = stt_(gS[:, order[i + 1], k, :], gS[:, c, k, :], gPc[:, k * NCH + c:k * NCH + c + 1],
                                   gH[:, c, k, :], ALU.mult, ALU.add)
                        if (i, k) == (2, 1):
                            ins.then_inc(gl_ops, 1)
                        else:
                            own(ins)
                    if i == 1:
                        own.settle()
                own.settle()
                for e in range(2):
                    b = V.take(dve, V.at[f"gl{d}_y"] + e)
                    o = Yg[:, :, :].rearrange("p t (k e c) -> p t k e c", k=2, e=2)[:, :, :, e, :]
                    x = b[:, :].rearrange("p (t k c) -> p t k c", t=TT, k=2)
                    if d:
                        tt(o, x, o, ALU.add).then_inc(V.emptied, 1)
                    else:
                        vec.tensor_copy(o, x).then_inc(V.emptied, 1)
                V.landed(dve, V.at[f"gl{d}_y"] + 1)
            do(tt(Yq[:, :, :], Yg[:, :, :], Yg[:, :, :], ALU.mult))
            do(vec.tensor_reduce(st[:, 8:16], Yq[:, :, :].rearrange("p t (h c) -> p (t h) c", h=4), AXX, ALU.add))
            mean_square("gla", st[:, 8:16], st[:, 16:24], P, EPS)
            rooted_("gla")
            do(vec.reciprocal(st[:, 32:40], st[:, 24:32]))
            do(tt(Yg[:, :, :].rearrange("p t (h c) -> p (t h) c", h=4),
                  Yg[:, :, :].rearrange("p t (h c) -> p (t h) c", h=4), spread(st[:, 32:40], P), ALU.mult))
            do(tt(Yg[:, :, :], Yg[:, :, :], tiled(row("gnorm"), TT), ALU.mult))
            S_.landed(dve, S_.at["gl_og"] + 1)
            signal(tt(xn[:, :, W:D], Yg[:, :, :], ogs[:, :, :], ALU.mult), mixed, 1)

            raw = sca[:, 0, 0:2 * (T + 2)].rearrange("p (a b) -> p a b", a=2)
            both = sca[:, 1, 0:2 * T].rearrange("p (a b) -> p a b", a=2)
            do(vec.memset(raw[:, :, :], 0.0))
            own(ts(mus[:, 0, :], pcol("mu", 0, 15), -1.0, ALU.mult, 1.0, ALU.add))
            do(ts(mus[:, 1, :], pcol("mu", 0, 15), 0.5, ALU.mult))
            do(ts(omka[:, :], pcol("k_a", 0, 4), -1.0, ALU.mult, 1.0, ALU.add))
            for j in range(8):
                m = 2 if j < 7 else 1
                b = V.take(dve, V.at["rw_p"] + j)
                vec.tensor_copy(raw[:, 0:m, 1:T + 1],
                                b[:, 0:m * T].rearrange("p (a b) -> p a b", a=m)).then_inc(V.emptied, 1)
                V.landed(dve, V.at["rw_p"] + j)
                own(tt(both[:, 0:m, :], raw[:, 0:m, 0:T], raw[:, 0:m, 2:T + 2], ALU.add))
                for k in range(m):
                    c = 2 * j + k
                    own(ts(pT[:, c, :], raw[:, k, 1:T + 1], mus[:, 0, c:c + 1], ALU.mult))
                own.settle()
                for k in range(m):
                    c = 2 * j + k
                    ins = stt_(pT[:, c, :], both[:, k, :], mus[:, 1, c:c + 1], pT[:, c, :], ALU.mult, ALU.add)
                    if k < m - 1:
                        own(ins)
                signal(ins, shifted, j + 1)
                own.settle()
            for k in range(4):
                own(ts(kk[:, k, :], pT[:, 4 + k, :], pcol("k_k", k), ALU.mult))
            own.settle()
            tt(kds, kk[:, :, :], kk[:, :, :], ALU.mult).then_inc(kk_sq, 1)
            for j in range(2):
                b = V.take(dve, V.at["kk"] + j)
                ts(sca[:, 2, j * 512:j * 512 + 512], b[:, :], 1e-24, ALU.max).then_inc(V.emptied, 1)
                V.landed(dve, V.at["kk"] + j)
            signal(vec.memset(st[:, 93:94], 0.0), meansq, ROOTS.index("kk") + 1)
            rooted_("kk")
            do(vec.reciprocal(sca[:, 2, :], sca[:, 2, :]))
            do(tt(flat(kk[:, :, :]), flat(kk[:, :, :]), sca[:, 2, :], ALU.mult))

            for d in range(DIRS):
                order = list(range(NCH))[::1 - 2 * d]
                way = slice(None, None, -1) if d else slice(None)
                end = 0 if d else CH - 1
                S_.landed(dve, S_.at[f"rw{d}_lora"] + 3)
                for k in range(4):
                    c = slice(k * T, k * T + T)
                    own(vec.tensor_tensor_scan(sca[:, 2, c][:, way], cst("reset", d, T)[:, way],
                                               sca[:, 0, c][:, way], 0.0, ALU.mult, ALU.add))
                own.settle()
                own(tt(flat(BK[:, 1]), sca[:, 2, :], sca[:, 0, :], ALU.subtract))
                own.settle()
                by_chunk = sca[:, 2, :].rearrange("p (k s) -> p k s", s=CH)
                signal(tt(flat(BKh[:, 1]).rearrange("p (k s) -> p k s", s=CH), spread(by_chunk[:, :, end], CH),
                          by_chunk, ALU.subtract), cum, d + 1)
                for k in range(4):
                    c = slice(k * T, k * T + T)
                    own(ts(sca[:, 0, c], sca[:, 1, c], pcol("k_a", k), ALU.mult, omka[:, k:k + 1], ALU.add))
                own.settle()
                own(tt(sca[:, 0, :], sca[:, 0, :], flat(pT[:, 4:8, :]), ALU.mult))
                do(tt(sca[:, 1, :], sca[:, 1, :], flat(kk[:, :, :]), ALU.mult))
                if d:
                    do(tt(flat(kds), flat(kds), sca[:, 0, :], ALU.add))
                else:
                    do(vec.tensor_copy(flat(kds), sca[:, 0, :]))
                dve.wait_ge(cum_exp, d + 1)
                kk4 = kk[:, :, :].rearrange("p k (t c) -> p k t c", t=TT)
                r4 = pT[:, 0:4, :].rearrange("p k (t c) -> p k t c", t=TT)
                own(tt(AR[:, :, :, 0, :], AR[:, :, :, 0, :], kk4, ALU.mult))
                own(tt(AR[:, :, :, 1, :], AR[:, :, :, 1, :], r4, ALU.mult))
                own(tt(flat(BK[:, 1]), flat(BK[:, 0]), sca[:, 0, :], ALU.mult))
                own(tt(flat(BKh[:, 1]), flat(BKh[:, 0]), sca[:, 0, :], ALU.mult))
                own.settle()
                own(tt(flat(BK[:, 0]), flat(BK[:, 0]), sca[:, 1, :], ALU.mult))
                signal(tt(flat(BKh[:, 0]), flat(BKh[:, 0]), sca[:, 1, :], ALU.mult), rw_ops, d + 1)
                own.settle()
                lev, levt = (("levb", "levf") if d else ("levf", "levb"))
                for t in range(TT):
                    v = V.at[f"rw{d}_t{t}"]
                    for i, dst in enumerate((LN, MQ)):
                        for j in range(4):
                            b = V.take(dve, v + 4 * i + j)
                            h = 4 * (j % 2) + j // 2
                            tt(dst[:, h:h + 3:2].rearrange("p h a b -> p h (a b)"),
                               b[:, :].rearrange("p (h c) -> p h c", h=2),
                               tiled(cst("mask2", d, 2 * P), 2), ALU.mult).then_inc(V.emptied, 1)
                    for g in range(2):
                        b = V.take(dve, v + 8 + g)
                        tt(L1[:, g:NH:2, :], b[:, :].rearrange("p (h c) -> p h c", h=4),
                           tiled(cst("mask2", 2 * (1 - d), P), 4), ALU.mult).then_inc(V.emptied, 1)
                    V.landed(dve, v + 9)
                    own(tt(X, L1[:, :, :], tiled(cst(lev, 0, P), NH), ALU.mult))
                    own(tt(XT, LN[:, :, 0, :], tiled(cst(levt, 0, P), NH), ALU.mult))
                    own.settle()
                    own(tt(X, tiled(ident, NH), X, ALU.subtract))
                    own.settle()
                    signal(tt(XT, tiled(ident, NH), XT, ALU.subtract), inv_start, 2 * d + t + 1)
                    n = v + 10
                    for l in range(2, NLEV + 1):
                        for g in range(2):
                            b = V.take(dve, n)
                            tt(WM[:, 4 * g:4 * g + 4, :], b[:, :].rearrange("p (h c) -> p h c", h=4),
                               tiled(cst(lev, l - 1, P), 4), ALU.mult).then_inc(V.emptied, 1)
                            n += 1
                        for g in range(2):
                            for dst in ((X, XT) if l < NLEV else (XT,)):
                                b = V.take(dve, n)
                                o = dst[:, 4 * g:4 * g + 4, :]
                                V.landed(dve, n - 1)
                                tt(o, o, b[:, :].rearrange("p (h c) -> p h c", h=4),
                                   ALU.subtract).then_inc(V.emptied, 1)
                                n += 1
                    b = V.take(dve, n)
                    tt(Rf[:, t], b[:, :].rearrange("p (k c) -> p k c", k=4), AR[:, :, t, 1, :],
                       ALU.add).then_inc(V.emptied, 1)
                    for c in range(2):
                        b = V.take(dve, n + 1 + c)
                        for k in range(4):
                            g = 2 * t + c
                            last = stt_(GT[:, g, k, :], cst("eye2"), Pc[:, k * NCH + g:k * NCH + g + 1],
                                        b[:, k * 64:k * 64 + 64], ALU.mult, ALU.add)
                        last.then_inc(V.emptied, 1)
                    n += 1
                    b = V.take(dve, n + 2)
                    if d:
                        tt(Yr[:, t, :], b[:, :], Yr[:, t, :], ALU.add).then_inc(V.emptied, 1)
                    else:
                        vec.tensor_copy(Yr[:, t, :], b[:, :]).then_inc(V.emptied, 1)
                    V.landed(dve, n + 2)
                S_.landed(dve, S_.at[f"rw{d}_t1"] + 7)
                for i in range(2):
                    b = V.take(dve, V.at[f"rw{d}_s"] + i)
                    tt(S[:, order[i + 2]].rearrange("p a b -> p (a b)"), b[:, 0:256],
                       Hc[:, order[i + 1]].rearrange("p a b -> p (a b)"), ALU.add).then_inc(V.emptied, 1)
                for e in range(2):
                    b = V.take(dve, V.at[f"rw{d}_y"] + e)
                    for t in range(TT):
                        lo, hi = 0, P
                        if order[0] // 2 == t:
                            lo, hi = (0, 64) if order[0] % 2 else (64, P)
                        o = Yr[lo:hi, t, :].rearrange("p (k e c) -> p k e c", k=4, e=2)[:, :, e, :]
                        last = tt(o, b[lo:hi, t * 256:t * 256 + 256].rearrange("p (k c) -> p k c", k=4), o, ALU.add)
                    last.then_inc(V.emptied, 1)
                V.landed(dve, V.at[f"rw{d}_y"] + 1)
            for k in range(4):
                own(stt_(kds[:, k, :], pT[:, k, :], pcol("r_k", k), kds[:, k, :], ALU.mult, ALU.mult))
            own.settle()
            signal(vec.memset(st[:, 92:93], 0.0), kk_sq, 2)
            scr = BK[:, 0].rearrange("p a b -> p (a b)")
            heads = lambda x: x.rearrange("p t (h c) -> p t h c", h=NH)
            scr_h = scr.rearrange("p (t h c) -> p t h c", t=TT, h=NH)
            sp4 = lambda c: c.rearrange("p (t h) -> p t h", t=TT).unsqueeze(3).to_broadcast([P, TT, NH, HD])
            yh = heads(Yr)
            do(vec.tensor_reduce(st[:, 48:64], yh, AXX, ALU.add))
            do(ts(st[:, 48:64], st[:, 48:64], 1.0 / HD, ALU.mult))
            for t in range(TT):
                own(tt(yh[:, t], yh[:, t], spread(st[:, 48 + 8 * t:56 + 8 * t], HD), ALU.subtract))
            own.settle()
            do(tt(scr.rearrange("p (t c) -> p t c", t=TT), Yr, Yr, ALU.mult))
            do(vec.tensor_reduce(st[:, 48:64], scr_h, AXX, ALU.add))
            mean_square("gn", st[:, 48:64], st[:, 48:64], HD, GN_EPS)
            b = V.take(dve, V.at["bonus"])
            vec.tensor_copy(bon[:, :, :].rearrange("p a b -> p (a b)"), b[:, 0:TT * NH]).then_inc(V.emptied, 1)
            V.landed(dve, V.at["bonus"])
            rooted_("gn")
            do(vec.reciprocal(st[:, 48:64], st[:, 64:80]))
            for t in range(TT):
                own(tt(yh[:, t], yh[:, t], spread(st[:, 48 + 8 * t:56 + 8 * t], HD), ALU.mult))
                own(tt(scr_h[:, t], heads(Vt)[:, t], spread(bon[:, t, :], HD), ALU.mult))
            own.settle()
            do(tt(Yr, Yr, tiled(row("ln_w"), TT), ALU.mult))
            do(tt(Yr, Yr, tiled(row("ln_b"), TT), ALU.add))
            do(tt(Yr, Yr, scr.rearrange("p (t c) -> p t c", t=TT), ALU.add))
            for t in range(TT):
                b = V.take(dve, V.at["gate"] + t)
                tt(Yr[:, t, :], b[:, :], Yr[:, t, :], ALU.mult).then_inc(V.emptied, 1)
            V.landed(dve, V.at["gate"] + 1)
            signal(vec.memset(st[:, 92:93], 0.0), mixed, 2)
            turned(V.at["mixT"])
            add_out(V.at["wout"])

            norm("ln2")
            turned(V.at["ln2"], "ln2")

            def top_two(n, t):
                do(ts(wexp[:, t, 0:n], wexp[:, t, 0:n], st[:, 20 + t:21 + t], ALU.mult))
                do(stt_(wexp[:, t, 0:n], lm[:, t, 0:n], top[:, t, 1:2], wexp[:, t, 0:n], ALU.is_ge, ALU.mult))

            b = V.take(dve, V.at["route1"])
            tt(lg[:, :, :], b[:, 0:72].rearrange("p (t c) -> p t c", t=TT), tiled(row("rb"), TT),
               ALU.add).then_inc(V.emptied, 1)
            V.landed(dve, V.at["route1"])
            for t in range(TT):
                do(vec.tensor_reduce(st[:, 8 + t:9 + t], lg[:, t, 0:4], AXX, ALU.max))
                do(ts(st[:, 80:84], lg[:, t, 0:4], st[:, 8 + t:9 + t], ALU.is_ge))
                do(ts(st[:, 80:84], st[:, 80:84], 1e30, ALU.mult, -1e30, ALU.add))
                do(tt(lm[:, t, :].rearrange("p (g e) -> p g e", g=4), lg[:, t, 4:36].rearrange("p (g e) -> p g e", g=4),
                      spread(st[:, 80:84], 8), ALU.add))
                do(vec.max(top[:, t, :], lm[:, t, :]))
                do(ts(st[:, 14 + t:15 + t], top[:, t, 0:1], -1.0, ALU.mult))
            signal(ts(st[:, 10:12], st[:, 8:10], -1.0, ALU.mult), logit_max, 1)
            dve.wait_ge(logit_exp, 2)
            do(ts(st[:, 18:20], st[:, 18:20], 1.0, ALU.add))
            do(tt(st[:, 18:20], st[:, 18:20], st[:, 12:14], ALU.mult))
            do(vec.reciprocal(st[:, 20:22], st[:, 18:20]))
            for t in range(TT):
                top_two(32, t)

            def unit(hid, out_, n, sn, credit, silus, parity, weight):
                vf, ve, vp, done = hid
                sf, se, sp_ = out_
                for f in range(4):
                    dve.wait_ge(vf, n + f + 1)
                    dve.wait_ge(done, silus + f + 1)
                    b = V.bank(vp + f)
                    tt(hact[:, parity, f, :], b[:, T:2 * T], sg[:, f % 2, :], ALU.mult).then_inc(ve, 1)
                dve.sem_inc(gu_read, 1)
                dve.wait_ge(se, sn + credit)
                for t in range(TT):
                    for c in range(2):
                        dve.wait_ge(sf, sn + 2 * t + c + 1)
                        b = S_.bank(sp_ + 2 * t + c)
                        o = x_sb[:, t, c * 512:c * 512 + 512]
                        stt_(o, b[:, :], weight(t), o, ALU.mult, ALU.add).then_inc(se, 1)
                dve.sem_inc(down_read, 1)

            def dense(x):
                dve.sem_inc(x.hid_emptied, 4)
                dve.sem_inc(x.out_emptied, 4)
                with dve.Fori(0, x.count * x.nfc // 2) as i:
                    for s in range(2):
                        u = 2 * i + s
                        e = u // x.nfc if x.nfc > 1 else u
                        unit((x.hid_filled, x.hid_emptied, 0, x.dense_silu), (x.out_filled, x.out_emptied, 0),
                             4 * u, 4 * u, 4, 4 * u, s, lambda t: wexp[:, t, bass.ds(e, 1)])
                dve.wait_ge(x.out_emptied, 4 + 4 * x.count * x.nfc)

            def gathered(x):
                gain = "moe" if x is moe2 else "ln2"
                each = 2 if x.pair else 1

                def choose(e, b):
                    for t in range(TT):
                        for m in range(each):
                            n_ = CAP // each
                            ins = ts(sel[:, b, t, m * n_:m * n_ + n_], cst("iota")[:, 0:n_],
                                     rank[:, t, bass.ds(each * e + m, 1)], ALU.is_equal)
                    ins.then_inc(x.sel_ready, 1)

                def weigh(e, b):
                    dve.wait_ge(x.sel_ready, e + 1)
                    for t in range(TT):
                        for m in range(2):
                            o = sel[:, b, t, m * HALF:m * HALF + HALF]
                            ins = ts(o, o, wexp[:, t, bass.ds(2 * e + m, 1)], ALU.mult)
                    ins.then_inc(x.sel_weighted, 1)

                def take(n):
                    dve.wait_ge(x.x_filled, n + 1)

                def places(n, bank, b):
                    for j in range(2):
                        take(n + j)
                        for k in range(4):
                            c = 4 * j + k
                            ins = ts(xgT[:, b, c, :], psum[(bank + j) % 4][:, k * CAP:k * CAP + CAP], pcol(gain, c),
                                     ALU.mult)
                        ins.then_inc(x.x_emptied, 1)

                def outputs(e):
                    for h in range(2):
                        dve.wait_ge(x.y_filled, 2 * e + h + 1)
                        vec.tensor_copy(yacc[:, h * 512:h * 512 + 512], psum[4 + h][:, :]).then_inc(x.y_emptied, 1)
                    dve.sem_inc(down_read, each)

                def add(e):
                    dve.wait_ge(x.z_emptied, 4 * e + 2)
                    for j in range(4):
                        t, c = j // 2, j % 2
                        dve.wait_ge(x.z_filled, 4 * e + j + 1)
                        o = x_sb[:, t, c * 512:c * 512 + 512]
                        if x.pair:
                            ins = tt(o, psum[6 + j % 2][:, :], o, ALU.add)
                        else:
                            ins = stt_(o, psum[6 + j % 2][:, :], wexp[:, t, bass.ds(e, 1)], o, ALU.mult, ALU.add)
                        ins.then_inc(x.z_emptied, 1)

                def one(i, k, base, first, last):
                    at = {n: j for j, n in enumerate(x.items(first, last))}
                    ph = x.phase(k, first)
                    b = k % 2
                    e = 2 * i + k
                    if not last:
                        choose(e + 1, 1 - b)
                    for c in range(x.nfc):
                        dve.wait_ge(x.silu, x.nfc * e + c + 1)
                        dve.sem_inc(x.x_emptied, 1)
                        if f"hT{c}" in at:
                            take(base + at[f"hT{c}"])
                            vec.tensor_copy(hTs[:, :, :].rearrange("p a b -> p (a b)"),
                                            psum[(ph + at[f"hT{c}"]) % 4][:, :]).then_inc(x.x_emptied, 1)
                        take(base + at[f"up{c}"])
                        tt(hsb[:, :], psum[(ph + at[f"up{c}"]) % 4][:, :], sgx[:, :], ALU.mult).then_inc(x.x_emptied, 1)
                        dve.sem_inc(gu_read, each)
                        if c == 0 and not first:
                            outputs(e - 1)
                        if c == x.nfc - 1 and not last:
                            places(base + at["ga"], ph + at["ga"], 1 - b)
                        if c == min(1, x.nfc - 1):
                            if not first:
                                add(e - 1)
                            take(base + at["selT"])
                            vec.tensor_copy(selT[:, :], psum[(ph + at["selT"]) % 4][:, 0:T]).then_inc(x.x_emptied, 1)

                def turn(n, bank):
                    take(n)
                    vec.tensor_copy(hTs[:, :, :].rearrange("p a b -> p (a b)"),
                                    psum[bank % 4][:, :]).then_inc(x.x_emptied, 1)

                def one_pair(i, k, base, first, last):
                    at = {n: j for j, n in enumerate(x.items(first, last))}
                    ph, b, e = x.phase(k, first), k % 2, 2 * i + k
                    weigh(e, b)
                    if not last:
                        choose(e + 1, 1 - b)
                    dve.wait_ge(x.silu, e + 1)
                    dve.sem_inc(x.x_emptied, 1)
                    if not first:
                        add(e - 1)
                    take(base + at["up0"])
                    tt(hsb[:, :], psum[(ph + at["up0"]) % 4][:, :], sgx[:, :], ALU.mult).then_inc(x.x_emptied, 1)
                    dve.sem_inc(gu_read, 2)
                    if not last:
                        places(base + at["ga"], ph + at["ga"], 1 - b)
                    turn(base + at["hT0"], ph + at["hT0"])
                    outputs(e)
                    take(base + at["selT"])
                    vec.tensor_copy(selT[:, :], psum[(ph + at["selT"]) % 4][:, 0:T]).then_inc(x.x_emptied, 1)

                dve.sem_inc(x.y_emptied, 2)
                dve.sem_inc(x.z_emptied, 2)
                choose(0, 0)
                places(0, 0, 0)
                if x.pair:
                    x.walk(dve, one_pair)
                    add(x.count - 1)
                    dve.wait_ge(x.z_emptied, 4 * x.count + 2)
                    return
                n = x.walk(dve, one)
                take(n)
                vec.tensor_copy(hTs[:, :, :].rearrange("p a b -> p (a b)"),
                                psum[(x.phase(1, False) + len(x.items(False, True))) % 4][:, :]).then_inc(x.x_emptied, 1)
                outputs(x.count - 1)
                add(x.count - 1)
                dve.wait_ge(x.z_emptied, 4 * x.count + 2)

            def ranks(k, x, item):
                n = x.count
                own.settle()
                for t in range(TT):
                    do(ts(msk[:, t, 0:n], lm[:, t, 0:n], top[:, t, 1:2], ALU.is_ge))
                signal(vec.memset(st[:, 92:93], 0.0), ranked, k)
                b = V.take(dve, item)
                own(vec.tensor_reduce(cnt[:, 0:1], b[:, 2 * n:3 * n], AXX, ALU.max))
                stt_(rank[:, :, 0:n], b[:, 0:2 * n].rearrange("p (t e) -> p t e", t=TT), 1.0, msk[:, :, 0:n],
                     ALU.add, ALU.mult).then_inc(V.emptied, 1)
                V.landed(dve, item)
                own.settle()
                do(ts(rank[:, :, 0:n], rank[:, :, 0:n], -1.0, ALU.add))
                do(ts(cnt[:, 1:2], cnt[:, 0:1], HALF + 0.5, ALU.is_ge))
                signal(stt_(over[:, :], cnt[:, 0:1], CAP + 0.5, cnt[:, 1:2], ALU.is_ge, ALU.add), route_known, k)

            ranks(1, moe1, V.at["rank1"])
            either(dve, moe1, dense, gathered)
            norm("lnf", x_sb)
            signal(tt(x_sb[:, :, :], x_sb[:, :, :], tiled(row("lnf"), TT), ALU.mult), mixed, 3)

            norm("att")
            turned(V.at["att"], "att")
            S_.landed(dve, S_.at["lat"] + 1)
            for t in range(TT):
                for i, (lo, n) in enumerate(((0, 256), (256, 128))):
                    own(vec.tensor_tensor_reduce(out=sqr[:, lo:lo + n], in0=lat[:, t, lo:lo + n],
                                                 in1=lat[:, t, lo:lo + n], scale=1.0 / n, scalar=0.0, op0=ALU.mult,
                                                 op1=ALU.add, accum_out=st[:, 8 + 2 * t + i:9 + 2 * t + i]))
                own.settle()
            mean_square("lat", st[:, 8:12], st[:, 16:20], 1, EPS)
            rooted_("lat")
            do(vec.reciprocal(st[:, 20:24], st[:, 20:24]))
            for t in range(TT):
                for i, (lo, n) in enumerate(((0, 256), (256, 128))):
                    x = lat[:, t, lo:lo + n]
                    do(ts(x, x, st[:, 20 + 2 * t + i:21 + 2 * t + i], ALU.mult))
            vec.memset(st[:, 92:93], 0.0).then_inc(lat_ready, 1)
            dve.wait_ge(lat_ready, 1)
            for k in range(3):
                j = V.at["lat"] + k // 2
                b = V.take(dve, j)
                ins = ts(latT[:, k, :], b[:, (k % 2) * T:(k % 2) * T + T],
                         pcol("qlat", k) if k < 2 else pcol("kvlat"), ALU.mult)
                if k:
                    ins.then_inc(V.emptied, 1)
            for t in range(TT):
                for c in range(2):
                    b = V.take(dve, V.at["q_up"] + 2 * t + c)
                    vec.tensor_copy(qh[:, t, 4 * c:4 * c + 4, :],
                                    b[:, 0:384].rearrange("p (h c) -> p h c", h=4)).then_inc(V.emptied, 1)
            for t in range(TT):
                own(vec.tensor_copy(kh[:, t, :, MN:MQK], tiled(lat[:, t, 384:416], NH)))
                for c in range(2):
                    b = V.take(dve, V.at["kv_up"] + 2 * t + c)
                    x = b[:, :].rearrange("p (h c) -> p h c", h=4)
                    vec.tensor_copy(kh[:, t, 4 * c:4 * c + 4, 0:MN], x[:, :, 0:MN])
                    vec.tensor_copy(mV[:, t, 4 * c:4 * c + 4, :], x[:, :, MN:P]).then_inc(V.emptied, 1)
            own.settle()
            V.landed(dve, V.at["kv_up"] + 3)
            sqh = sqr[:, :].rearrange("p (h c) -> p h c", h=NH)
            for i, x in enumerate((qh, kh)):
                for t in range(TT):
                    do(tt(sqh, x[:, t], x[:, t], ALU.mult))
                    do(vec.tensor_reduce(stt[:, 2 * i + t, :], sqh, AXX, ALU.add))
            mean_square("heads", stt[:, 0:4, :], stt[:, 0:4, :], MQK, EPS)
            rooted_("heads")
            do(vec.reciprocal(stt[:, 0:4, :], stt[:, 4:8, :]))
            rope = cst("rope").rearrange("p (t s c) -> p t s c", t=TT, s=2)
            hf = MR // 2
            rpv = [rp[:, i, :].rearrange("p (h c) -> p h c", h=NH) for i in range(3)]
            for i, x in enumerate((qh, kh)):
                for t in range(TT):
                    do(tt(x[:, t], x[:, t], spread(stt[:, 2 * i + t, :], MQK), ALU.mult))
                    do(tt(x[:, t], x[:, t], tiled(row("kn" if i else "qn"), NH), ALU.mult))
                    r1, r2 = x[:, t, :, MN:MN + hf], x[:, t, :, MN + hf:MQK]
                    co, si = tiled(rope[:, t, 0, :], NH), tiled(rope[:, t, 1, :], NH)
                    own(tt(rpv[0], r1, si, ALU.mult))
                    own(tt(rpv[1], r2, si, ALU.mult))
                    own.settle()
                    own(tt(r1, r1, co, ALU.mult))
                    own(tt(r2, r2, co, ALU.mult))
                    own.settle()
                    own(tt(r1, r1, rpv[1], ALU.subtract))
                    do(tt(r2, r2, rpv[0], ALU.add))
            signal(vec.memset(st[:, 92:93], 0.0), heads_ready, 1)
            def edge(x):
                return x.rearrange("p (a b) -> p a b", a=3)[:, 0::2, :]

            def stick_scores(h):
                b = V.take(dve, scores_item("stick", h))
                vec.tensor_copy(za[:, 0, :], b[:, 0:3 * P]).then_inc(V.emptied, 1)
                V.landed(dve, scores_item("stick", h))
                signal(vec.memset(st[:, 91:92], 0.0), z_ready, h + 1)

            def latent_max(h):
                b = V.take(dve, scores_item("latent", h))
                own(tt(edge(mz), edge(b[:, 0:3 * P]), tiled(cst("causal"), 2), ALU.add))
                own.settle()
                vec.tensor_copy(mz[:, P:2 * P], b[:, P:2 * P]).then_inc(V.emptied, 1)
                V.landed(dve, scores_item("latent", h))
                own(vec.tensor_reduce(st[:, 22:23], mz[:, 0:P], AXX, ALU.max))
                do(vec.tensor_reduce(st[:, 23:24], mz[:, P:3 * P], AXX, ALU.max))
                if h:
                    dve.wait_ge(S_.filled, pair_item(f"turned{(h - 1) % 2}", (h - 1) // 2) + 1)
                signal(ts(st[:, 24:26], st[:, 22:24], -(MQK ** -0.5), ALU.mult), maxed, h + 1)

            V.landed(dve, V.at["kv_up"] + 3)
            stick_scores(0)
            latent_max(0)
            for h in range(NH):
                dve.wait_ge(z_soft, h + 1)
                do(stt_(lf, za[:, 0, :], 0.0, za[:, 1, :], ALU.max, ALU.add))
                signal(tt(edge(lf), edge(lf), tiled(cst("before"), 2), ALU.mult), fails, h + 1)
                own(stt_(za[:, 2, :], za[:, 0, :], 0.0, za[:, 1, :], ALU.min, ALU.subtract))
                dve.wait_ge(p_exp, h + 1)
                do(vec.reciprocal(st[:, 28:30], st[:, 26:28]))
                own(ts(mp[:, 0:P], mp[:, 0:P], st[:, 28:29], ALU.mult))
                own.settle()
                signal(ts(mp[:, P:3 * P], mp[:, P:3 * P], st[:, 29:30], ALU.mult), p_ready, h + 1)
                b = V.take(dve, scores_item("sums", h))
                tt(za[:, 2, :], za[:, 2, :], b[:, 0:3 * P], ALU.subtract).then_inc(V.emptied, 1)
                V.landed(dve, scores_item("sums", h))
                if h % 2:
                    dve.wait_ge(w_read, h // 2 + 1)
                elif h:
                    dve.wait_ge(S_.filled, pair_item("stick", h // 2 - 1) + 1)
                signal(vec.memset(st[:, 91:92], 0.0), w_arg, h + 1)
                if h + 1 < NH:
                    stick_scores(h + 1)
                    latent_max(h + 1)
                dve.wait_ge(w_exp, h + 1)
                signal(tt(edge(wT), edge(wT), tiled(cst("before"), 2), ALU.mult), w_ready, h + 1)
            dve.wait_ge(S_.filled, pair_item("latent", HP - 1) + 1)
            add_out(V.at["wout2"])

            norm("dffn")
            turned(V.at["dffn"], "dffn")
            q = lambda i: par16[:, i, :]

            def s5_arguments():
                dve.wait_ge(s5_val, 1)
                do(ts(q(1), pcol("lre", 0, 16), -1e-4, ALU.min))
                do(tt(q(2), q(1), q(0), ALU.mult))
                do(tt(q(4), pcol("lim", 0, 16), q(0), ALU.mult))
                do(ts(q(6), q(4), float(np.pi / 2), ALU.add))
                magic = 12582912.0
                pi_hi = float(np.float32(6.28125))
                pi_lo = float(2 * np.pi - 6.28125)
                for i in (4, 6):
                    do(ts(q(8), q(i), float(1 / (2 * np.pi)), ALU.mult, magic, ALU.add))
                    do(ts(q(8), q(8), magic, ALU.subtract))
                    do(stt_(q(i), q(8), -pi_hi, q(i), ALU.mult, ALU.add))
                    do(stt_(q(i), q(8), -pi_lo, q(i), ALU.mult, ALU.add))
                    do(ts(q(i), q(i), 3.1415925, ALU.min, -3.1415925, ALU.max))
                signal(vec.memset(st[:, 92:93], 0.0), s5_arg, 1)

            def s5_coefficients():
                dve.wait_ge(s5_val, 2)
                im = pcol("lim", 0, 16)
                do(tt(q(9), q(3), q(7), ALU.mult))
                do(ts(q(9), q(9), -1.0, ALU.add))
                do(tt(q(10), q(3), q(5), ALU.mult))
                do(tt(q(11), q(1), q(1), ALU.mult))
                do(tt(q(8), im, im, ALU.mult))
                do(tt(q(11), q(11), q(8), ALU.add))
                do(vec.reciprocal(q(11), q(11)))
                do(tt(q(12), q(9), q(1), ALU.mult))
                do(tt(q(8), q(10), im, ALU.mult))
                do(tt(q(12), q(12), q(8), ALU.add))
                do(tt(q(12), q(12), q(11), ALU.mult))
                do(tt(q(13), q(10), q(1), ALU.mult))
                do(tt(q(8), q(9), im, ALU.mult))
                do(tt(q(13), q(13), q(8), ALU.subtract))
                do(tt(q(13), q(13), q(11), ALU.mult))
                dve.wait_ge(ssm_in, 32)
                cr, ci = spread(q(12), 32), spread(q(13), 32)
                t0 = xn[:, 0, 0:512].rearrange("p (a b) -> p a b", a=16)
                t1 = xn[:, 1, 0:512].rearrange("p (a b) -> p a b", a=16)
                own(tt(t0, cT[:, :, 0, :], ci, ALU.mult))
                own(tt(t1, cT[:, :, 1, :], ci, ALU.mult))
                own.settle()
                own(tt(cT[:, :, 0, :], cT[:, :, 0, :], cr, ALU.mult))
                own(tt(cT[:, :, 1, :], cT[:, :, 1, :], cr, ALU.mult))
                own.settle()
                own(tt(cT[:, :, 0, :], cT[:, :, 0, :], t1, ALU.subtract))
                do(tt(cT[:, :, 1, :], cT[:, :, 1, :], t0, ALU.add))
                do(ts(cT[:, :, 1, :], cT[:, :, 1, :], -1.0, ALU.mult))
                signal(vec.memset(st[:, 92:93], 0.0), s5_mat, 1)

            def s5_table(n, j0, jn):
                c, s = spread(q(14)[:, j0:j0 + jn], n), spread(q(15)[:, j0:j0 + jn], n)
                re, mi = rot[:, 0, j0:j0 + jn, 0:n], rot[:, 1, j0:j0 + jn, 0:n]
                ra, rb = rot[:, 0, j0:j0 + jn, n:2 * n], rot[:, 1, j0:j0 + jn, n:2 * n]
                ta, tb = rtm[:, 0, :, 0:n], rtm[:, 1, :, 0:n]
                own(tt(ta, mi, s, ALU.mult))
                own(tt(tb, mi, c, ALU.mult))
                own(tt(ra, re, c, ALU.mult))
                own(tt(rb, re, s, ALU.mult))
                own.settle()
                own(tt(ra, ra, ta, ALU.subtract))
                do(tt(rb, rb, tb, ALU.add))

            def s5_tables(lo, hi):
                if lo == 1:
                    own(vec.memset(rot[:, 0, :, 0:1], 1.0))
                    own(vec.memset(rot[:, 1, :, 0:1], 0.0))
                    own(vec.tensor_copy(q(14), q(7)))
                    do(vec.tensor_copy(q(15), q(5)))
                n = lo
                while n < hi:
                    for j0 in (0, 8):
                        s5_table(n, j0, 8)
                    do(tt(q(16), q(15), q(15), ALU.mult))
                    do(tt(q(15), q(15), q(14), ALU.mult))
                    do(ts(q(15), q(15), 2.0, ALU.mult))
                    do(tt(q(14), q(14), q(14), ALU.mult))
                    do(tt(q(14), q(14), q(16), ALU.subtract))
                    n *= 2

            beside = {0: s5_arguments, 2: s5_coefficients, 3: lambda: s5_tables(1, 32),
                      4: lambda: s5_tables(32, 128), 5: lambda: s5_tables(128, 256)}
            for u in range(NFC):
                unit((V.filled, V.emptied, V.at["ffn"], silu_done), (S_.filled, S_.emptied, S_.at["ffn"]),
                     V.at["ffn"] + 4 * u, S_.at["ffn"] + 4 * u, 0, 4 * u, u % 2, lambda t: 1.0)
                if u in beside:
                    beside[u]()
            dve.wait_ge(S_.emptied, S_.at["ffn"] + 4 * NFC)
            signal(vec.memset(st[:, 92:93], 0.0), mixed, 4)

            norm("ssm")
            turned(V.at["ssm"], "ssm")
            for j in range(2):
                b = V.take(dve, V.at["u"] + j)
                vec.tensor_copy(uT[:, 2 * j:2 * j + 2, :].rearrange("p a b -> p (a b)"), b[:, :]).then_inc(V.emptied, 1)
            V.landed(dve, V.at["u"] + 1)
            for i in range(9):
                if i < 8:
                    C_, S2 = vst[:, 0], vst[:, 1]
                    n = s5_item("in", i)
                    for m in range(2):
                        b = V.take(dve, n + m)[:, :].rearrange("p (c t) -> p c t", c=2)
                        own(tt(C_[:, m], b, tiled(rot[:, 0, 2 * i + m, :], 2), ALU.mult))
                        tt(S2[:, m], b, tiled(rot[:, 1, 2 * i + m, :], 2), ALU.mult).then_inc(V.emptied, 1)
                    own.settle()
                    V.landed(dve, n + 1)
                    own(tt(C_[:, :, 0, :], C_[:, :, 0, :], S2[:, :, 1, :], ALU.add))
                    own(tt(C_[:, :, 1, :], C_[:, :, 1, :], S2[:, :, 0, :], ALU.subtract))
                    own.settle()
                    for m in range(2):
                        dec = q(3)[:, 2 * i + m:2 * i + m + 1].to_broadcast([P, T])
                        for k in range(2):
                            own(vec.tensor_tensor_scan(S2[:, m, k, :], dec, C_[:, m, k, :], 0.0, ALU.mult, ALU.add))
                    own.settle()
                    if i:
                        dve.wait_ge(V.filled, s5_item("out", i - 1) + 1)
                    for m in range(2):
                        own(tt(hst[:, m], S2[:, m], tiled(rot[:, 0, 2 * i + m, :], 2), ALU.mult))
                        own(tt(C_[:, m], S2[:, m], tiled(rot[:, 1, 2 * i + m, :], 2), ALU.mult))
                    own.settle()
                    own(tt(hst[:, :, 0, :], hst[:, :, 0, :], C_[:, :, 1, :], ALU.subtract))
                    own(tt(hst[:, :, 1, :], hst[:, :, 1, :], C_[:, :, 0, :], ALU.add))
                    own.settle()
                    signal(vec.memset(st[:, 92:93], 0.0), s5_h, i + 1)
                if i:
                    n, o, j = s5_item("out", i - 1), 64 * ((i - 1) % 2), (i - 1) // 2
                    b = V.take(dve, n)
                    stt_(yT[o:o + 64, j, :], uT[o:o + 64, j, :], pcol("sd", j)[o:o + 64, :], b[o:o + 64, 0:T],
                         ALU.mult, ALU.add).then_inc(V.emptied, 1)
            V.landed(dve, s5_item("out", 7))
            signal(vec.memset(st[:, 92:93], 0.0), y_sum, 1)
            for t in range(TT):
                for c in range(2):
                    n = 2 * t + c
                    b = V.take(dve, V.at["glu"] + n)
                    S_.landed(dve, S_.at["glu"] + n)
                    o = x_sb[:, t, c * 512:c * 512 + 512]
                    do(tt(gsig2, b[:, :], gsig, ALU.mult))
                    tt(o, o, gsig2, ALU.add).then_inc(V.emptied, 1)
                    V.landed(dve, V.at["glu"] + n)

            norm("moe")
            turned(V.at["moe"], "moe")
            b = V.take(dve, V.at["route2"])
            vec.tensor_copy(lm[:, :, 0:8], b[:, 0:16].rearrange("p (t c) -> p t c", t=TT)).then_inc(V.emptied, 1)
            V.landed(dve, V.at["route2"])
            for t in range(TT):
                do(vec.max(top[:, t, :], lm[:, t, 0:8]))
                do(ts(st[:, 14 + t:15 + t], top[:, t, 0:1], -1.0, ALU.mult))
            signal(vec.memset(st[:, 92:93], 0.0), logit_max, 2)
            dve.wait_ge(logit_exp, 4)
            do(ts(st[:, 18:20], st[:, 18:20], 1.0, ALU.add))
            do(vec.reciprocal(st[:, 20:22], st[:, 18:20]))
            for t in range(TT):
                top_two(8, t)
            ranks(2, moe2, V.at["rank2"])
            either(dve, moe2, dense, gathered)
            vec.memset(st[:, 92:93], 0.0).then_inc(out_ready, 1)


_RAW = ["x", "w_in", "rw_g2", "w_out", "moe_w_gate", "moe_w_up", "moe_w_down", "att_w_in_2", "att_w_q_up_2",
        "att_w_kv_up_2", "att_w_out_2", "dffn_w_gate_2", "dffn_w_up_2", "dffn_w_down_2", "ssm_w_in_2",
        "ssm_w_glu_2", "moe_router_2", "moe_w_gate_2", "moe_w_up_2", "moe_w_down_2"]


def layout(x):
    col = lambda v: v.reshape(-1, P).T
    f = np.float32
    par = [x["ln1_w"], x["rw_mu"], x["rw_w0_f"], x["rw_w0_b"], x["rw_a0_f"], x["rw_a0_b"], x["rw_k_k"],
           x["rw_k_a"], x["rw_r_k"], x["gla_gb_f"], x["gla_gb_b"], x["ln2_w"], x["att_norm_2"],
           x["att_q_latent_norm_2"], x["att_kv_latent_norm_2"], x["dffn_norm_2"], x["ssm_norm_2"], x["moe_norm_2"],
           x["ssm_d_2"], x["ssm_a_re_2"], x["ssm_a_im_2"], np.broadcast_to(x["ssm_log_dt_2"][0][:, None], (32, 64))]
    rows = [x["rw_ln_w"], x["rw_ln_b"], x["gla_norm_w"], x["ln_f_w"], x["att_q_norm_2"], x["att_k_norm_2"],
            x["moe_b_coarse"], x["moe_b_fine"]]
    gw2 = np.zeros((32, 2, 256), f)
    gw2[0:16, 0] = x["gla_gw2_f"][0]
    gw2[16:32, 1] = x["gla_gw2_b"][0]
    bT = np.zeros((4, 2, 16, 4, 2, 2, 64), f)
    cT = np.zeros((2, 64, 16, 2, 2, 16), f)
    for r, (b, c) in enumerate((("ssm_b_re_2", "ssm_c_re_2"), ("ssm_b_im_2", "ssm_c_im_2"))):
        bb = x[b][0].reshape(4, 4, 2, 64, 16)
        cc = x[c][0].reshape(16, 2, 16, 64)
        for g in range(2):
            bT[:, g, :, :, r, g, :] = bb[:, :, g].transpose(1, 3, 0, 2)
            cT[g, :, :, r, g, :] = cc[:, g].transpose(2, 0, 1)
    return {
        "par": np.concatenate([col(v) for v in par], 1),
        "rows": np.concatenate([v.reshape(-1) for v in rows]),
        "con": np.concatenate(list(constants().values()), 1),
        "gw2": gw2,
        "w2": np.concatenate([x["rw_w2_f"][0], x["rw_w2_b"][0]], 0),
        "a2": np.concatenate([x["rw_a2_f"][0], x["rw_a2_b"][0]], 0),
        "wr1": np.concatenate([x["moe_w_coarse"][0], x["moe_w_fine"][0]], 1),
        "bT": bT.reshape(P, 4, 2, P),
        "cT": cT.reshape(P, 16, 2, 32),
    }


def kernel(**inputs):
    import concourse.bacc as _bacc
    from concourse.bass_utils import run_bass_kernel_spmd as _run

    x = {n: np.asarray(v) for n, v in inputs.items()}
    given = {n: x[n] for n in _RAW} | layout(x)
    nc = _bacc.Bacc("TRN2", target_bir_lowering=False, num_devices=1)
    arrays, aps = {}, {}
    for name, v in given.items():
        arrays[f"in_{name}"] = v = np.ascontiguousarray(v)
        aps[name] = nc.dram_tensor(f"in_{name}", v.shape, mybir.dt.from_np(v.dtype), kind="ExternalInput").ap()
    out = nc.dram_tensor("out", (1, T, D), F32, kind="ExternalOutput").ap()
    block_kernel(nc, aps, out)
    r = _run(nc, [arrays], core_ids=[0])
    return r.results[0]["out"]
```
